# Optimizing a Trainium2 kernel written in Bass

```python
import jax, jax.numpy as jnp
from jax import lax
import numpy as np

D_MODEL = 1024
BATCH = 1
SEQ = 256
DEPTH = 1
DEC_BATCH = 1
DEC_SEQ = 1024
PAST_LEN = 256

GRID_W = 64
N_Q_HEADS = 8
N_KV_HEADS = 2
Q_PER_KV = N_Q_HEADS // N_KV_HEADS
HEAD_DIM = 64
WINDOW = 128
BLOCK = 128
ROPE_BASE = 10000.0
GLA_HEADS = 4
GLA_DK = 64
GLA_DV = 128
GLA_LOW_RANK = 16
GLA_TAU = 16.0
GLA_CHUNK = 16
D_FF = 2816
N_MOD = 9
EPS = 1e-6
NEG = -1e30

ATT_Q = N_Q_HEADS * HEAD_DIM
ATT_KV = N_KV_HEADS * HEAD_DIM
GLA_QK = GLA_HEADS * GLA_DK
GLA_V = GLA_HEADS * GLA_DV
MIX_WIDTH = ATT_Q + GLA_V
SPLIT_SIZES = (ATT_Q, ATT_KV, ATT_KV, GLA_QK, GLA_QK, GLA_V, GLA_V, GLA_LOW_RANK, GLA_LOW_RANK)
IN_WIDTH = ATT_Q + 2 * ATT_KV + 2 * GLA_QK + 2 * GLA_V + 2 * GLA_LOW_RANK

kernel_name = 'hybrid_gla_swa_diffusion_step'

def rmsnorm(x, g):
    xf = x.astype(jnp.float32)
    y = xf * lax.rsqrt(jnp.mean(xf * xf, axis=-1, keepdims=True) + EPS)
    return (y * g.astype(jnp.float32)).astype(x.dtype)

def swiglu(h, w1, w3, w2):
    return (jax.nn.silu(h @ w1) * (h @ w3)) @ w2

def ada_modulation(cond, w_ada, b_ada):
    m = jax.nn.silu(cond) @ w_ada + b_ada
    return m.reshape(cond.shape[0], N_MOD, D_MODEL)

def split_proj(p):
    points, acc = [], 0
    for s in SPLIT_SIZES[:-1]:
        acc += s
        points.append(acc)
    return jnp.split(p, points, axis=-1)

def _rotate_half(x, ang):
    f = ang.shape[-1]
    cos = jnp.cos(ang)[:, None, :]
    sin = jnp.sin(ang)[:, None, :]
    x1, x2 = x[..., :f], x[..., f:]
    return jnp.concatenate([x1 * cos - x2 * sin, x1 * sin + x2 * cos], axis=-1)

def rope_2d(x):
    L = x.shape[1]
    rows = L // GRID_W
    row = jnp.repeat(jnp.arange(rows, dtype=jnp.float32), GRID_W)
    col = jnp.tile(jnp.arange(GRID_W, dtype=jnp.float32), rows)
    half = HEAD_DIM // 2
    inv_freq = ROPE_BASE ** (-jnp.arange(0, half, 2, dtype=jnp.float32) / half)
    xf = x.astype(jnp.float32)
    xr = _rotate_half(xf[..., :half], row[:, None] * inv_freq[None, :])
    xc = _rotate_half(xf[..., half:], col[:, None] * inv_freq[None, :])
    return jnp.concatenate([xr, xc], axis=-1).astype(x.dtype)

def sink_softmax(s, sink):
    sk = sink.astype(jnp.float32).reshape(N_KV_HEADS, Q_PER_KV)[None, :, :, None, None]
    m = jnp.maximum(jnp.max(s, axis=-1, keepdims=True), sk)
    p = jnp.exp(s - m)
    return p / (jnp.sum(p, axis=-1, keepdims=True) + jnp.exp(sk - m))

def context_attention(q, k, v, sink):
    B, L = q.shape[0], q.shape[1]
    nb = L // BLOCK
    scale = HEAD_DIM ** -0.5
    qb = q.reshape(B, nb, BLOCK, N_KV_HEADS, Q_PER_KV, HEAD_DIM).swapaxes(0, 1)

    def one_block(qi):
        s = jnp.einsum('bqgrd,bkgd->bgrqk', qi, k, preferred_element_type=jnp.float32) * scale
        p = sink_softmax(s, sink)
        return jnp.einsum('bgrqk,bkgd->bqgrd', p.astype(v.dtype), v)

    o = lax.map(one_block, qb)
    return o.swapaxes(0, 1).reshape(B, L, ATT_Q)

def latent_attention(q, k, v, k_ctx, v_ctx, sink):
    B, L = q.shape[0], q.shape[1]
    nb = L // BLOCK
    scale = HEAD_DIM ** -0.5
    pad = ((0, 0), (BLOCK, BLOCK), (0, 0), (0, 0))
    kp = jnp.pad(k, pad).reshape(B, nb + 2, BLOCK, N_KV_HEADS, HEAD_DIM)
    vp = jnp.pad(v, pad).reshape(B, nb + 2, BLOCK, N_KV_HEADS, HEAD_DIM)
    k_band = jnp.concatenate([kp[:, :-2], kp[:, 1:-1], kp[:, 2:]], axis=2).swapaxes(0, 1)
    v_band = jnp.concatenate([vp[:, :-2], vp[:, 1:-1], vp[:, 2:]], axis=2).swapaxes(0, 1)
    qb = q.reshape(B, nb, BLOCK, N_KV_HEADS, Q_PER_KV, HEAD_DIM).swapaxes(0, 1)
    r = jnp.arange(BLOCK)[:, None]
    j = jnp.arange(3 * BLOCK)[None, :]
    in_window = jnp.abs(j - BLOCK - r) <= WINDOW

    def one_block(args):
        i, qi, ki, vi = args
        kpos = (i - 1) * BLOCK + j
        valid = in_window & (kpos >= 0) & (kpos < L)
        s_loc = jnp.einsum('bqgrd,bkgd->bgrqk', qi, ki, preferred_element_type=jnp.float32) * scale
        s_loc = jnp.where(valid, s_loc, NEG)
        s_ctx = jnp.einsum('bqgrd,bkgd->bgrqk', qi, k_ctx, preferred_element_type=jnp.float32) * scale
        p = sink_softmax(jnp.concatenate([s_loc, s_ctx], axis=-1), sink)
        vals = jnp.concatenate([vi, v_ctx], axis=1)
        return jnp.einsum('bgrqk,bkgd->bqgrd', p.astype(vals.dtype), vals)

    o = lax.map(one_block, (jnp.arange(nb), qb, k_band, v_band))
    return o.swapaxes(0, 1).reshape(B, L, ATT_Q)

def gla_scan(q, k, v, log_a, s0):
    B, L, H, dk = q.shape
    dv = v.shape[-1]
    n, C = L // GLA_CHUNK, GLA_CHUNK

    def chunks(t):
        return t.reshape(B, n, C, H, t.shape[-1]).transpose(0, 1, 3, 2, 4)

    qc, kc, vc, ac = chunks(q), chunks(k), chunks(v), chunks(log_a)
    b = jnp.cumsum(ac, axis=3)
    tri = jnp.tril(jnp.ones((C, C), dtype=bool))[:, :, None]
    diff = b[:, :, :, :, None, :] - b[:, :, :, None, :, :]
    decay = jnp.exp(jnp.where(tri, diff, NEG))
    scores = jnp.einsum('bnhtd,bnhsd,bnhtsd->bnhts', qc, kc, decay)
    o_intra = jnp.einsum('bnhts,bnhsv->bnhtv', scores, vc)
    b_last = b[:, :, :, -1:, :]
    q_in = qc * jnp.exp(b)
    k_in = kc * jnp.exp(b_last - b)
    a_last = jnp.exp(b_last[:, :, :, 0, :])

    def step(S, xs):
        qi, ki, vi, ai = xs
        o = jnp.einsum('bhtd,bhdv->bhtv', qi, S)
        S = ai[..., None] * S + jnp.einsum('bhtd,bhtv->bhdv', ki, vi)
        return S, o

    xs = (q_in.swapaxes(0, 1), k_in.swapaxes(0, 1), vc.swapaxes(0, 1), a_last.swapaxes(0, 1))
    s_final, o_inter = lax.scan(step, s0, xs)
    o = o_intra + o_inter.swapaxes(0, 1)
    return o.transpose(0, 1, 3, 2, 4).reshape(B, L, H, dv), s_final

def gla_mixer(gq, gk, gv, gg, lr_f, lr_b, w_up, b_up, norm_w, s0_f, s0_b):
    B, L = gq.shape[0], gq.shape[1]
    f32 = jnp.float32
    q = gq.astype(f32).reshape(B, L, GLA_HEADS, GLA_DK) * (GLA_DK ** -0.5)
    k = gk.astype(f32).reshape(B, L, GLA_HEADS, GLA_DK)
    v = gv.astype(f32).reshape(B, L, GLA_HEADS, GLA_DV)

    def log_gate(lr, d):
        z = lr.astype(f32) @ w_up[d].astype(f32) + b_up[d].astype(f32)
        return (jax.nn.log_sigmoid(z) / GLA_TAU).reshape(B, L, GLA_HEADS, GLA_DK)

    def flip(t):
        return jnp.flip(t, axis=1)

    o_f, s_f = gla_scan(q, k, v, log_gate(lr_f, 0), s0_f)
    o_b, s_b = gla_scan(flip(q), flip(k), flip(v), flip(log_gate(lr_b, 1)), s0_b)
    o = o_f + flip(o_b)
    o = o * lax.rsqrt(jnp.mean(o * o, axis=-1, keepdims=True) + EPS) * norm_w.astype(f32)
    o = o * jax.nn.silu(gg.astype(f32).reshape(B, L, GLA_HEADS, GLA_DV))
    return o.reshape(B, L, GLA_V).astype(gq.dtype), s_f, s_b

def mixer_context(h, w):
    B, L = h.shape[0], h.shape[1]
    aq, ak, av, gq, gk, gv, gg, lf, lb = split_proj(h @ w['w_in'])
    k = ak.reshape(B, L, N_KV_HEADS, HEAD_DIM)
    v = av.reshape(B, L, N_KV_HEADS, HEAD_DIM)
    att = context_attention(aq.reshape(B, L, N_Q_HEADS, HEAD_DIM), k, v, w['attn_sink'])
    s0 = jnp.zeros((B, GLA_HEADS, GLA_DK, GLA_DV), jnp.float32)
    gla, s_f, s_b = gla_mixer(gq, gk, gv, gg, lf, lb, w['gla_w_up'], w['gla_b_up'], w['gla_norm'], s0, s0)
    out = jnp.concatenate([att, gla], axis=-1) @ w['w_out']
    return out, (k, v, s_f, s_b)

def mixer_latent(h, w, k_ctx, v_ctx, s0_f, s0_b):
    B, L = h.shape[0], h.shape[1]
    aq, ak, av, gq, gk, gv, gg, lf, lb = split_proj(h @ w['w_in'])
    q = rope_2d(aq.reshape(B, L, N_Q_HEADS, HEAD_DIM))
    k = rope_2d(ak.reshape(B, L, N_KV_HEADS, HEAD_DIM))
    v = av.reshape(B, L, N_KV_HEADS, HEAD_DIM)
    att = latent_attention(q, k, v, k_ctx, v_ctx, w['attn_sink'])
    gla, _, _ = gla_mixer(gq, gk, gv, gg, lf, lb, w['gla_w_up'], w['gla_b_up'], w['gla_norm'],
                          s0_f.astype(jnp.float32), s0_b.astype(jnp.float32))
    out = jnp.concatenate([att, gla], axis=-1) @ w['w_out']
    return out, ()

def trunk_layer(x, mod, w, mixer_fn):
    def modulated(x, i):
        return rmsnorm(x, w['norm_pre'][i]) * (1 + mod[:, 3 * i + 1, None]) + mod[:, 3 * i, None]

    def residual(x, out, i, weight):
        return x + weight * mod[:, 3 * i + 2, None] * rmsnorm(out, w['norm_post'][i])

    x = residual(x, swiglu(modulated(x, 0), w['ffn_w1'][0], w['ffn_w3'][0], w['ffn_w2'][0]), 0, 0.5)
    mix, ctx_tensors = mixer_fn(modulated(x, 1))
    x = residual(x, mix, 1, 1.0)
    x = residual(x, swiglu(modulated(x, 2), w['ffn_w1'][1], w['ffn_w3'][1], w['ffn_w2'][1]), 2, 0.5)
    return x, ctx_tensors

def setup_inputs(seed: int = 0) -> dict:
    key = jax.random.key(seed)
    ks = jax.random.split(key, 21)
    D = D_MODEL

    def nrm(k, shape, s):
        return jax.random.normal(k, shape, jnp.float32) * s

    return {
        'x_prompt': nrm(ks[0], (BATCH, SEQ, D), 1.0),
        'x_sample': nrm(ks[1], (DEC_BATCH, DEC_SEQ, D), 1.0),
        'cache_k': nrm(ks[2], (DEC_BATCH, DEPTH, PAST_LEN, N_KV_HEADS, HEAD_DIM), 1.0),
        'cache_v': nrm(ks[3], (DEC_BATCH, DEPTH, PAST_LEN, N_KV_HEADS, HEAD_DIM), 1.0),
        'state_gla_fwd': nrm(ks[4], (DEC_BATCH, DEPTH, GLA_HEADS, GLA_DK, GLA_DV), 0.5),
        'state_gla_bwd': nrm(ks[5], (DEC_BATCH, DEPTH, GLA_HEADS, GLA_DK, GLA_DV), 0.5),
        'c': nrm(ks[6], (DEC_BATCH, D), 1.0),
        'c_ctx': nrm(ks[7], (D,), 1.0),
        'w_ada': nrm(ks[8], (DEPTH, D, N_MOD * D), 0.5 * D ** -0.5),
        'b_ada': nrm(ks[9], (DEPTH, N_MOD * D), 0.02),
        'norm_pre': 1.0 + nrm(ks[10], (DEPTH, 3, D), 0.1),
        'norm_post': 1.0 + nrm(ks[11], (DEPTH, 3, D), 0.1),
        'ffn_w1': nrm(ks[12], (DEPTH, 2, D, D_FF), D ** -0.5),
        'ffn_w3': nrm(ks[13], (DEPTH, 2, D, D_FF), D ** -0.5),
        'ffn_w2': nrm(ks[14], (DEPTH, 2, D_FF, D), D_FF ** -0.5),
        'w_in': nrm(ks[15], (DEPTH, D, IN_WIDTH), D ** -0.5),
        'gla_w_up': nrm(ks[16], (DEPTH, 2, GLA_LOW_RANK, GLA_QK), GLA_LOW_RANK ** -0.5),
        'gla_b_up': nrm(ks[17], (DEPTH, 2, GLA_QK), 0.5),
        'gla_norm': 1.0 + nrm(ks[18], (DEPTH, GLA_DV), 0.1),
        'attn_sink': nrm(ks[19], (DEPTH, N_Q_HEADS), 0.5),
        'w_out': nrm(ks[20], (DEPTH, MIX_WIDTH, D), MIX_WIDTH ** -0.5),
    }

def reference(x_prompt, x_sample, cache_k, cache_v, state_gla_fwd, state_gla_bwd, c, c_ctx,
              w_ada, b_ada, norm_pre, norm_post, ffn_w1, ffn_w3, ffn_w2, w_in,
              gla_w_up, gla_b_up, gla_norm, attn_sink, w_out):
    y_prompt = x_prompt
    y_sample = x_sample
    ks_new, vs_new, sf_new, sb_new = [], [], [], []
    for l in range(DEPTH):
        w = {'w_in': w_in[l], 'w_out': w_out[l], 'gla_w_up': gla_w_up[l], 'gla_b_up': gla_b_up[l],
             'gla_norm': gla_norm[l], 'attn_sink': attn_sink[l], 'norm_pre': norm_pre[l],
             'norm_post': norm_post[l], 'ffn_w1': ffn_w1[l], 'ffn_w3': ffn_w3[l], 'ffn_w2': ffn_w2[l]}
        mod_ctx = ada_modulation(c_ctx[None, :], w_ada[l], b_ada[l])
        mod_lat = ada_modulation(c, w_ada[l], b_ada[l])
        y_prompt, (k_l, v_l, sf_l, sb_l) = trunk_layer(
            y_prompt, mod_ctx, w, lambda h: mixer_context(h, w))
        y_sample, _ = trunk_layer(
            y_sample, mod_lat, w,
            lambda h: mixer_latent(h, w, cache_k[:, l], cache_v[:, l], state_gla_fwd[:, l], state_gla_bwd[:, l]))
        ks_new.append(k_l)
        vs_new.append(v_l)
        sf_new.append(sf_l)
        sb_new.append(sb_l)
    new_cache_k = jnp.stack(ks_new, axis=1)
    new_cache_v = jnp.stack(vs_new, axis=1)
    new_state_gla_fwd = jnp.stack(sf_new, axis=1).astype(x_prompt.dtype)
    new_state_gla_bwd = jnp.stack(sb_new, axis=1).astype(x_prompt.dtype)
    return (y_prompt, y_sample, new_cache_k, new_cache_v, new_state_gla_fwd, new_state_gla_bwd)


_drawn_inputs = setup_inputs


def setup_inputs(seed=0):
    import zlib

    import numpy as np

    out = dict(_drawn_inputs(seed))
    spreads = {}
    factors = {'cache_k': 2.877, 'state_gla_fwd': 29.679, 'state_gla_bwd': 29.269, 'attn_sink': 22.551}
    for name, (base, spread) in spreads.items():
        noise = np.random.default_rng([zlib.crc32(name.encode()), seed]).standard_normal(out[name].shape)
        drawn = base * np.exp(spread * noise) if base else spread * noise
        out[name] = __import__('jax').numpy.asarray(drawn.astype(out[name].dtype))
    for name, factor in factors.items():
        out[name] = (out[name] * factor).astype(out[name].dtype)
    return out
```

```python
import numpy as np
import concourse.bass as bass
from concourse import mybir

F32 = mybir.dt.float32
F32R = mybir.dt.float32r
ALU = mybir.AluOpType
ACT = mybir.ActivationFunctionType
AX_X = mybir.AxisListType.X
ds = bass.ds

P = 128
D = 1024
KB = D // P
CTX, LAT = 256, 1024
TOK = CTX + LAT
TILES = TOK // P
CTX_TILES = CTX // P
FF = 2816
FFB = FF // P
GROUP = 2
FF_GROUPS = FFB // GROUP
N_MOD = 9
MODB = N_MOD * KB
SPANS = [(0, 256), (256, 512), (768, 512)]
NSP = len(SPANS)
CH = 256
NCH = TOK // CH
EPS = 1e-6
NEG = -1e30
GRID_W = 64
HD = 64
NQ, NKV = 8, 2
GLA_C = 32
CPT = P // GLA_C
GH, DK, DV = 4, 64, 128
IN_W = 2336
B_Q, B_K, B_V, B_GQ, B_GK, B_GV, B_GG, B_LR = 0, 4, 5, 6, 8, 10, 14, 18
PROJB = 19


def shape_constants():
    ident = np.eye(P, dtype=np.float32)
    ones = np.full((P, P), 1.0 / D, np.float32)
    t = np.arange(LAT)
    half = HD // 2
    inv = (10000.0 ** (-np.arange(0, half, 2, dtype=np.float32) / np.float32(half))).astype(np.float32)
    p = np.arange(P)
    in_col = (p % HD) >= half
    freq = inv[p % (half // 2)]
    pos = np.where(in_col[:, None], (t % GRID_W)[None], (t // GRID_W)[None]).astype(np.float32)
    ang = (pos * freq[:, None]).astype(np.float32)
    cos = np.cos(ang).astype(np.float32)
    sin = np.sin(ang).astype(np.float32) * np.where((p % half) < half // 2, -1, 1)[:, None]
    r = np.arange(P)[:, None]
    j = np.arange(3 * P)[None]
    win = np.where(np.abs(j - P - r) <= P, 0.0, NEG).astype(np.float32)
    masks = []
    for first, last in ((True, False), (False, False), (False, True)):
        m = np.zeros((P, 3 * P + CTX), np.float32)
        m[:, :3 * P] = win
        if first:
            m[:, :P] = NEG
        if last:
            m[:, 2 * P:3 * P] = NEG
        masks.append(m)
    s, q = np.arange(P)[:, None], np.arange(P)[None]
    same = (s // GLA_C) == (q // GLA_C)
    tau = 1.0 / 16.0
    gla = []
    for incl, rest in ((s <= q, s > q), (s >= q, s < q)):
        gla += [np.where(same & incl, tau, 0.0), np.where(same & rest, tau, 0.0), np.where(same & incl, 1.0, 0.0)]
    return {
        "const_ident": ident, "const_mean": ones,
        "const_rope": np.concatenate([cos, sin], 1).astype(np.float32),
        "const_mask": np.concatenate(masks, 1).astype(np.float32),
        "const_gla": np.concatenate(gla, 1).astype(np.float32),
    }


class Core:

    def __init__(self, nc, d, o):
        self.nc, self.d, self.o = nc, d, o
        self.live = []
        self.base = -(-nc.sbuf_base // 64) * 64
        self.end = nc.sbuf_usable_end
        self.at = self.base
        put = self.put
        self.ident = put("ident", [P, P])
        self.mean = put("mean", [P, P])
        self.mod = put("mod", [P, MODB, 2])
        self.vec = put("vec", [P, MODB + 48])
        self.pre = put("pre", [P, 3, KB, 2])
        self.gate = put("gate", [P, 3, KB, 2])
        self.eps = put("eps", [P, 1])
        self.hi_at = self.at
        self.h_hi = put("h_hi", [P, KB, TOK], F32R)
        self.h_lo = put("h_lo", [P, KB, TOK], F32R)
        self.rest = self.at
        self.x_t = nc.dram_tensor("x_t", [P, KB, TOK], F32, kind="Internal").ap()

    def put(self, name, shape, dt=F32):
        n = -(-int(np.prod(shape[1:])) * 4 // 32) * 32
        assert self.at + n <= self.end, (name, self.at + n - self.end)
        t = self.nc.alloc_sbuf_tensor_at(name, shape, dt, offset=self.at)
        self.at += n
        return t

    def sem(self, name):
        s = self.nc.alloc_semaphore(name)
        self.live.append(s)
        return s

    def recycle(self):
        self.nc.clear_and_free_semaphores(self.live)
        self.nc.all_engine_barrier()
        self.live = []


def f32(ap):
    return ap.bitcast(F32)


def product3(pe, out, w_hi, w_lo, x_hi, x_lo, first, last):
    pe.matmul(out, w_hi, x_hi, start=first, stop=False)
    pe.matmul(out, w_hi, x_lo, start=False, stop=False)
    return pe.matmul(out, w_lo, x_hi, start=False, stop=last)


def modulation_stage(nc, k):
    WB = 4
    RING = 3
    LOADS = MODB // WB
    ROUNDS = LOADS // RING
    k.at = k.hi_at
    rows = k.put("mod_rows", [MODB + 48, P])
    cond_rows = k.put("cond_rows", [2 * KB, P])
    cond = k.put("cond", [P, 2 * KB])
    w = [k.put(f"ada_w{s}", [P, KB, WB * P]) for s in range(RING)]
    k.at = k.rest
    rows_in, w_in = k.sem("rows_in"), [k.sem(f"ada_in{s}") for s in range(RING)]
    w_used = [k.sem(f"ada_used{s}") for s in range(RING)]
    turned, cond_ready, evac = k.sem("rows_turned"), k.sem("cond_ready"), [k.sem(f"ada_evac{s}") for s in range(RING)]
    vec_ready, coef = k.sem("vec_ready"), k.sem("mod_coef")
    d = k.d
    with (
        nc.psum_tensor("ps_rows", [P, 512], F32) as ps_rows,
        nc.psum_tensor("ps_m0", [P, 512], F32) as pm0,
        nc.psum_tensor("ps_m1", [P, 512], F32) as pm1,
        nc.psum_tensor("ps_m2", [P, 512], F32) as pm2,
        nc.Block() as block,
    ):
        pm = [pm0, pm1, pm2]

        @block.sync
        def _(sp):
            for dst, src in ((k.ident[:], d["const_ident"]), (k.mean[:], d["const_mean"]),
                             (rows[0:MODB, :], d["b_ada"].rearrange("a (b p) -> (a b) p", p=P)),
                             (rows[MODB:MODB + 24, :], d["norm_pre"].rearrange("a i (b p) -> (a i b) p", p=P)),
                             (rows[MODB + 24:MODB + 48, :], d["norm_post"].rearrange("a i (b p) -> (a i b) p", p=P)),
                             (cond_rows[0:KB, :], d["c_ctx"].rearrange("(b p) -> b p", p=P)),
                             (cond_rows[KB:2 * KB, :], d["c"].rearrange("a (b p) -> (a b) p", p=P))):
                sp.dma_start(dst, src).then_inc(rows_in, 16)
            w_ada = d["w_ada"].rearrange("a (k p) n -> (a p) k n", p=P)
            with sp.Fori(0, ROUNDS) as i:
                for s in range(RING):
                    sp.wait_ge(w_used[s], i + 1)
                    sp.dma_start(w[s][:], w_ada[:, :, ds(i * (RING * WB * P) + s * WB * P, WB * P)]).then_inc(w_in[s], 16)

        @block.tensor
        def _(pe):
            for s in range(RING):
                pe.sem_inc(w_used[s], 1)
            pe.wait_ge(rows_in, 16 * 7)
            pe.transpose(ps_rows[:, 0:MODB + 48], rows[:], k.ident[0:MODB + 48, 0:MODB + 48])
            pe.transpose(ps_rows[:, 256:256 + 2 * KB], cond_rows[:], k.ident[0:2 * KB, 0:2 * KB]).then_inc(turned, 1)
            pe.wait_ge(cond_ready, 1)
            with pe.Fori(0, ROUNDS) as i:
                for s in range(RING):
                    pe.wait_ge(w_in[s], i * 16 + 16)
                    pe.wait_ge(evac[s], i + 1)
                    for b in range(WB):
                        for kk in range(KB):
                            mm = pe.matmul(pm[s][:, 2 * b:2 * b + 2], w[s][:, kk, b * P:(b + 1) * P],
                                           cond[:, kk:2 * KB:KB], start=kk == 0, stop=kk == KB - 1)
                    mm.then_inc(w_used[s], 1)

        @block.scalar
        def _(act):
            act.wait_ge(turned, 1)
            act.activation(cond[:], ps_rows[:, 256:256 + 2 * KB], ACT.Silu).then_inc(cond_ready, 1)

        @block.vector
        def _(dve):
            for s in range(RING):
                dve.sem_inc(evac[s], 1)
            dve.memset(k.eps[:], EPS)
            dve.wait_ge(turned, 1)
            dve.wait_ge(cond_ready, 1)
            dve.tensor_copy(k.vec[:], ps_rows[:, 0:MODB + 48]).then_inc(vec_ready, 1)
            dve.wait_ge(vec_ready, 1)
            with dve.Fori(0, ROUNDS) as i:
                for s in range(RING):
                    dve.wait_ge(w_used[s], i + 2)
                    at = i * (RING * WB) + s * WB
                    dve.tensor_tensor(k.mod[:, ds(at, WB), :], pm[s][:, 0:2 * WB].rearrange("p (b c) -> p b c", c=2),
                                      k.vec[:, ds(at, WB)].unsqueeze(2).broadcast_to([P, WB, 2]),
                                      ALU.add).then_inc(evac[s], 1)
            for s in range(RING):
                dve.wait_ge(evac[s], ROUNDS + 1)
            for i in range(3):
                shift = MODB + KB * i
                dve.scalar_tensor_tensor(
                    out=k.pre[:, i], in0=k.mod[:, (3 * i + 1) * KB:(3 * i + 2) * KB, :], scalar=1.0,
                    in1=k.vec[:, shift:shift + KB].unsqueeze(2).broadcast_to([P, KB, 2]),
                    op0=ALU.add, op1=ALU.mult).then_inc(coef, 1)
                dve.scalar_tensor_tensor(
                    out=k.gate[:, i], in0=k.mod[:, (3 * i + 2) * KB:(3 * i + 3) * KB, :], scalar=1.0 if i == 1 else 0.5,
                    in1=k.vec[:, shift + 24:shift + 24 + KB].unsqueeze(2).broadcast_to([P, KB, 2]),
                    op0=ALU.mult, op1=ALU.mult).then_inc(coef, 1)
            dve.wait_ge(coef, 6)


def norm_stage(nc, k, i_post, i_pre, acc):
    n_ = f"n{0 if i_post is None else i_post + 1}_"
    first, final = i_post is None, i_pre is None
    put = lambda name, shape, dt=F32: k.put(n_ + name, shape, dt)
    sem = lambda name: k.sem(n_ + name)
    x = [put(f"x{s}", [P, KB, CH]) for s in range(2)]
    tmp = [put(f"tmp{s}", [P, KB, CH]) for s in range(2)]
    if first or final:
        nat = [put(f"nat{s}", [P, 2, D]) for s in range(2)]
    if not final:
        sq = put("sq", [P, KB, CH])
        v = [put(f"v{s}", [P, KB, CH]) for s in range(2)]
    sqo = put("sqo", [P, KB, CH])
    part = put("part", [P, 2, CH])
    std = put("std", [P, 2, CH])
    rstd = put("rstd", [P, 2, CH])
    x_in = [sem(f"x_in{s}") for s in range(2)]
    x_out = [sem(f"x_out{s}") for s in range(2)]
    (o_sq, o_part, o_mean, o_std, o_rstd, o_scaled, x_ready, p_sq, p_part, p_mean, p_std, p_rstd, p_scaled, p_v, p_hi,
     p_lo, turned, evac) = [sem(s) for s in (
         "o_sq", "o_part", "o_mean", "o_std", "o_rstd", "o_scaled", "x_ready", "p_sq", "p_part", "p_mean", "p_std",
         "p_rstd", "p_scaled", "p_v", "p_hi", "p_lo", "turned", "evac")]
    d, o = k.d, k.o
    x_rows = [d["x_prompt"][0].rearrange("(a p) f -> p a f", p=P)] + [
        d["x_sample"][0, CH * n:CH * (n + 1)].rearrange("(a p) f -> p a f", p=P) for n in range(NCH - 1)]
    y_rows = [o[0][0].rearrange("(a p) f -> p a f", p=P)] + [
        o[1][0, CH * n:CH * (n + 1)].rearrange("(a p) f -> p a f", p=P) for n in range(NCH - 1)]
    chunk = lambda n: slice(n * CH, (n + 1) * CH)
    cond = lambda n: 0 if n == 0 else 1
    with (
        nc.psum_tensor(n_ + "ps_o", [P, 512], F32) as ps_o,
        nc.psum_tensor(n_ + "ps_p", [P, 512], F32) as ps_p,
        nc.psum_tensor(n_ + "ps_x", [P, KB, CH], F32) as ps_x,
        nc.Block() as block,
    ):
        def store(sp, n):
            s = n % 2
            if final:
                sp.wait_ge(evac, n + 1)
                sp.dma_start(y_rows[n], nat[s][:]).then_inc(x_out[s], 16)
            else:
                sp.wait_ge(x_ready, n + 1)
                sp.dma_start(k.x_t[:, :, chunk(n)], x[s][:]).then_inc(x_out[s], 16)

        @block.sync
        def _(sp):
            for n in range(NCH):
                s = n % 2
                if first:
                    if n >= 2:
                        sp.wait_ge(turned, n - 1)
                    sp.dma_start(nat[s][:], x_rows[n]).then_inc(x_in[s], 16)
                else:
                    if n >= 2:
                        sp.wait_ge(x_out[s], 16 * (n // 2))
                        if not final:
                            sp.wait_ge(p_scaled, n - 1)
                    if final and n >= 2:
                        sp.wait_ge(turned, n - 1)
                    sp.dma_start(x[s][:], k.x_t[:, :, chunk(n)]).then_inc(x_in[s], 16)
                if n >= 1:
                    store(sp, n - 1)
            store(sp, NCH - 1)
            for s in range(2):
                sp.wait_ge(x_out[s], 16 * ((NCH + 1 - s) // 2))

        @block.tensor
        def _(pe):
            def turn_in(n):
                pe.wait_ge(x_in[n % 2], 16 * (n // 2 + 1))
                if n >= 1:
                    pe.wait_ge(x_ready, n)
                for a in range(2):
                    for b in range(KB):
                        mm = pe.transpose(ps_x[:, b, a * P:(a + 1) * P], nat[n % 2][:, a, b * P:(b + 1) * P], k.ident[:])
                mm.then_inc(turned, 1)

            def turn_out(n):
                pe.wait_ge(x_ready, n + 1)
                if n >= 1:
                    pe.wait_ge(evac, n)
                for a in range(2):
                    for b in range(KB):
                        mm = pe.transpose(ps_x[:].rearrange("p b t -> p (b t)")[:, a * D + b * P:a * D + (b + 1) * P],
                                          x[n % 2][:, b, a * P:(a + 1) * P], k.ident[:])
                mm.then_inc(turned, 1)

            def mean(n, ready, row, bank, std_ready, out_sem):
                pe.wait_ge(ready, n + 1)
                if n >= 1:
                    pe.wait_ge(std_ready, n)
                pe.matmul(bank[:, 0:CH], k.mean[:], part[:, row, :], start=True, stop=True).then_inc(out_sem, 1)

            for n in range(NCH):
                if first:
                    turn_in(n)
                else:
                    mean(n, o_part, 0, ps_o, o_std, o_mean)
                if not final:
                    mean(n, p_part, 1, ps_p, p_std, p_mean)
                else:
                    turn_out(n)

        @block.scalar
        def _(act):
            for n in range(NCH):
                s, c = n % 2, cond(n)
                if first:
                    act.wait_ge(turned, n + 1)
                    if n >= 2:
                        act.wait_ge(x_out[s], 16 * (n // 2))
                        act.wait_ge(p_scaled, n - 1)
                    act.activation(x[s][:], ps_x[:], ACT.Copy).then_inc(x_ready, 1)
                else:
                    if n >= 1:
                        act.wait_ge(o_part, n)
                    act.activation(sqo[:], acc[:, :, chunk(n)], ACT.Square).then_inc(o_sq, 1)
                    act.wait_ge(o_mean, n + 1)
                    if n >= 1:
                        act.wait_ge(o_rstd, n)
                    act.activation(std[:, 0, :], ps_o[:, 0:CH], ACT.Sqrt, bias=k.eps[:]).then_inc(o_std, 1)
                if not final:
                    act.wait_ge(x_ready, n + 1)
                    if n >= 1:
                        act.wait_ge(p_part, n)
                    act.activation(sq[:], x[s][:], ACT.Square).then_inc(p_sq, 1)
                    act.wait_ge(p_mean, n + 1)
                    if n >= 1:
                        act.wait_ge(p_rstd, n)
                    act.activation(std[:, 1, :], ps_p[:, 0:CH], ACT.Sqrt, bias=k.eps[:]).then_inc(p_std, 1)
                    act.wait_ge(p_scaled, n + 1)
                    if n >= 2:
                        act.wait_ge(p_lo, n - 1)
                    for b in range(KB):
                        act.activation(v[s][:, b], tmp[s][:, b], ACT.Identity, bias=k.mod[:, 3 * i_pre * KB + b, c:c + 1],
                                       scale=k.pre[:, i_pre, b, c:c + 1]).then_inc(p_v, 1)
                else:
                    act.wait_ge(turned, n + 1)
                    if n >= 2:
                        act.wait_ge(x_out[s], 16 * (n // 2))
                    act.activation(nat[s][:].rearrange("p a f -> p (a f)"), ps_x[:].rearrange("p b t -> p (b t)"),
                                   ACT.Copy).then_inc(evac, 1)

        @block.gpsimd
        def _(pool):
            if not final:
                for n in range(NCH):
                    pool.wait_ge(p_v, KB * (n + 1))
                    pool.tensor_copy(k.h_hi[:, :, chunk(n)], v[n % 2][:]).then_inc(p_hi, 1)

        @block.vector
        def _(dve):
            def rms(n, ready, src, row, part_sem, std_sem, rstd_sem, scaled, src2, mean_sem):
                dve.wait_ge(ready, n + 1)
                if n >= 1:
                    dve.wait_ge(mean_sem, n)
                dve.tensor_reduce(part[:, row, :], src[:].rearrange("p b t -> p t b"), AX_X, ALU.add).then_inc(part_sem, 1)
                dve.wait_ge(std_sem, n + 1)
                dve.reciprocal(rstd[:, row, :], std[:, row, :]).then_inc(rstd_sem, 1)
                dve.wait_ge(rstd_sem, n + 1)
                dve.tensor_tensor(tmp[n % 2][:], src2, rstd[:, row:row + 1, :].broadcast_to([P, KB, CH]),
                                  ALU.mult).then_inc(scaled, 1)

            def lo(n):
                dve.wait_ge(p_hi, n + 1)
                dve.tensor_tensor(k.h_lo[:, :, chunk(n)], v[n % 2][:], f32(k.h_hi[:, :, chunk(n)]),
                                  ALU.subtract).then_inc(p_lo, 1)

            for n in range(NCH):
                s, c = n % 2, cond(n)
                if not final and n >= 2:
                    dve.wait_ge(p_v, KB * (n - 1))
                if not first:
                    rms(n, o_sq, sqo, 0, o_part, o_std, o_rstd, o_scaled, acc[:, :, chunk(n)], o_mean)
                    dve.wait_ge(x_in[s], 16 * (n // 2 + 1))
                    dve.wait_ge(o_scaled, n + 1)
                    for b in range(KB):
                        ins = dve.scalar_tensor_tensor(out=x[s][:, b], in0=tmp[s][:, b], scalar=k.gate[:, i_post, b, c:c + 1],
                                                       in1=x[s][:, b], op0=ALU.mult, op1=ALU.add)
                    ins.then_inc(x_ready, 1)
                if not final:
                    if not first:
                        dve.wait_ge(x_ready, n + 1)
                    rms(n, p_sq, sq, 1, p_part, p_std, p_rstd, p_scaled, x[s][:], p_mean)
                    if n >= 1:
                        lo(n - 1)
            if not final:
                lo(NCH - 1)
                dve.wait_ge(p_lo, NCH)


def gemm_stage(nc, k, name, w_halves, tail_cols, blocks, out_buf):
    put = lambda n, shape, dt=F32: k.put(f"{name}_{n}", shape, dt)
    sem = lambda n: k.sem(f"{name}_{n}")
    raw = [put(f"raw{b}", [P, KB, P]) for b in range(2)]
    hi = [put(f"hi{b}", [P, KB, P], F32R) for b in range(2)]
    lo = [put(f"lo{b}", [P, KB, P], F32R) for b in range(2)]
    landed = [sem(f"landed{b}") for b in range(2)]
    rounded = [sem(f"rounded{b}") for b in range(2)]
    split = [sem(f"split{b}") for b in range(2)]
    ready = sem("ready")
    evac = [sem(f"evac{t}") for t in range(2 * NSP)]
    rounds = blocks // 2
    tail = tail_cols is not None
    with (
        nc.psum_tensor(name + "_ps", [P, 2 * NSP, 512], F32) as ps,
        nc.Block() as block,
    ):
        @block.sync
        def _(sp):
            for rng, halves in w_halves:
                def load(i, first):
                    for b in range(2):
                        if not first:
                            sp.wait_ge(split[b], i)
                        for part, src in halves(i, b):
                            sp.dma_start(part(raw[b]), src).then_inc(landed[b], 16)
                lo_, hi_ = rng
                if lo_ == 0:
                    load(0, True)
                    lo_ = 1
                if hi_ - lo_ == 1:
                    load(lo_, False)
                elif hi_ > lo_:
                    with sp.Fori(lo_, hi_) as i:
                        load(i, False)
            if tail:
                sp.wait_ge(split[0], rounds)
                for part, src in tail_cols:
                    sp.dma_start(part(raw[0]), src).then_inc(landed[0], 16)

        @block.tensor
        def _(pe):
            def one(i, b):
                pe.wait_ge(split[b], i + 1)
                for t, (at, n) in enumerate(SPANS):
                    pe.wait_ge(evac[NSP * b + t], i + 1)
                    for kk in range(KB):
                        mm = product3(pe, ps[:, NSP * b + t, 0:n], hi[b][:, kk], lo[b][:, kk],
                                      k.h_hi[:, kk, at:at + n], k.h_lo[:, kk, at:at + n], kk == 0, kk == KB - 1)
                    mm.then_inc(ready, 1)
            with pe.Fori(0, rounds) as i:
                for b in range(2):
                    one(i, b)
            if tail:
                one(rounds, 0)

        def split_hi(act, i, b):
            act.wait_ge(landed[b], i * 32 + 32)
            act.activation(hi[b][:], raw[b][:], ACT.Copy).then_inc(rounded[b], 1)

        def split_lo(dve, i, b):
            dve.wait_ge(rounded[b], i + 1)
            dve.tensor_tensor(lo[b][:], raw[b][:], f32(hi[b][:]), ALU.subtract).then_inc(split[b], 1)

        def free_banks(eng, spans):
            for b in range(2):
                for t in spans:
                    eng.sem_inc(evac[NSP * b + t], 1)

        def out_of(eng, i, b, spans, op, with_next):
            for t in spans:
                at, n = SPANS[t]
                eng.wait_ge(ready, i * (2 * NSP) + NSP * b + t + 1)
                dst = out_buf[:, ds(2 * i + b, 1), at:at + n]
                op(dst, ps[:, NSP * b + t:NSP * b + t + 1, 0:n]).then_inc(evac[NSP * b + t], 1)
            if with_next:
                eng.wait_ge(ready, i * (2 * NSP) + NSP * (b + 1))

        @block.scalar
        def _(act):
            copy = lambda dst, src: act.activation(dst, src, ACT.Copy)
            free_banks(act, (0, 1))
            for b in range(2):
                split_hi(act, 0, b)
            if rounds > 1:
                with act.Fori(0, rounds - 1) as i:
                    for b in range(2):
                        out_of(act, i, b, (0, 1), copy, True)
                        split_hi(act, i + 1, b)
            out_of(act, rounds - 1, 0, (0, 1), copy, tail)
            if tail:
                split_hi(act, rounds, 0)
            out_of(act, rounds - 1, 1, (0, 1), copy, False)
            if tail:
                out_of(act, rounds, 0, (0, 1), copy, False)

        @block.vector
        def _(dve):
            free_banks(dve, (2,))
            for b in range(2):
                split_lo(dve, 0, b)
            if rounds > 1:
                with dve.Fori(0, rounds - 1) as i:
                    for b in range(2):
                        out_of(dve, i, b, (2,), dve.tensor_copy, True)
                        split_lo(dve, i + 1, b)
            out_of(dve, rounds - 1, 0, (2,), dve.tensor_copy, tail)
            if tail:
                split_lo(dve, rounds, 0)
            out_of(dve, rounds - 1, 1, (2,), dve.tensor_copy, False)
            if tail:
                out_of(dve, rounds, 0, (2,), dve.tensor_copy, False)


def ffn_stage(nc, k, which, acc):
    f = f"f{which}_"
    put = lambda n, shape, dt=F32: k.put(f + n, shape, dt)
    sem = lambda n: k.sem(f + n)
    raw = [put(f"raw{s}", [P, KB, P]) for s in range(2)]
    hi = [put(f"w_hi{j}", [P, KB, P], F32R) for j in range(6)]
    lo = [put(f"w_lo{j}", [P, KB, P], F32R) for j in range(6)]
    hid_hi = put("hid_hi", [P, GROUP, TOK], F32R)
    hid_lo = put("hid_lo", [P, GROUP, TOK], F32R)
    act_t = [put(f"act{s}", [P, 512]) for s in range(2)]
    landed = [sem(f"landed{s}") for s in range(2)]
    rounded, split = [sem(f"rounded{s}") for s in range(2)], [sem(f"split{s}") for s in range(2)]
    up_ready = [sem(f"up_ready{b}") for b in range(GROUP)]
    silu_done, prod_done = [sem(f"silu{s}") for s in range(2)], [sem(f"prod{s}") for s in range(2)]
    hid_r, hid_ready = [sem(f"hid_r{s}") for s in range(2)], [sem(f"hid_ready{t}") for t in range(NSP)]
    down_ready, down_evac = sem("down_ready"), [sem(f"down_evac{s}") for s in range(4)]
    zeroed = sem("zeroed")
    w1 = k.d["ffn_w1"][0, which].rearrange("(k p) n -> p k n", p=P)
    w3 = k.d["ffn_w3"][0, which].rearrange("(k p) n -> p k n", p=P)
    w2 = k.d["ffn_w2"][0, which]
    LAST = FF_GROUPS - 1
    with (
        nc.psum_tensor(f + "ps_g", [P, 2, 512], F32) as ps_g,
        nc.psum_tensor(f + "ps_u", [P, 2, 512], F32) as ps_u,
        nc.psum_tensor(f + "ps_d", [P, 4, 512], F32) as ps_d,
        nc.Block() as block,
    ):
        @block.sync
        def _(sp):
            def load(i, first):
                for j in range(6):
                    s, n = j % 2, j // 2
                    if not (first and n == 0):
                        sp.wait_ge(split[s], i * 3 + n)
                    if j < 4:
                        src = (w1, w3)[j % 2][:, :, ds(i * (GROUP * P) + (j // 2) * P, P)]
                        sp.dma_start(raw[s][:], src).then_inc(landed[s], 16)
                    else:
                        src = w2[ds(i * (GROUP * P) + (j - 4) * P, P), :]
                        sp.dma_start(raw[s][:].rearrange("p k n -> p (k n)"), src).then_inc(landed[s], 16)
            load(0, True)
            with sp.Fori(1, FF_GROUPS) as i:
                load(i, False)

        @block.tensor
        def _(pe):
            pe.wait_ge(zeroed, 1)
            with pe.Fori(0, FF_GROUPS) as i:
                for b in range(GROUP):
                    for t, (at, n) in enumerate(SPANS):
                        s = (NSP * b + t) % 2
                        pe.wait_ge(prod_done[s], i * 3 + (NSP * b + t) // 2 + 1)
                        for ps, j in ((ps_g, 2 * b), (ps_u, 2 * b + 1)):
                            pe.wait_ge(split[j % 2], i * 3 + j // 2 + 1)
                            for kk in range(KB):
                                mm = product3(pe, ps[:, s, 0:n], hi[j][:, kk], lo[j][:, kk],
                                              k.h_hi[:, kk, at:at + n], k.h_lo[:, kk, at:at + n], kk == 0, kk == KB - 1)
                        mm.then_inc(up_ready[b], 1)
                for j in (4, 5):
                    pe.wait_ge(split[j % 2], i * 3 + 3)
                for t, (at, n) in enumerate(SPANS):
                    pe.wait_ge(hid_ready[t], i * GROUP + GROUP + 1)
                    for m in range(KB):
                        s = m % 4
                        pe.wait_ge(down_evac[s], i * (2 * NSP) + 2 * t + m // 4 + 1)
                        for b in range(GROUP):
                            mm = product3(pe, ps_d[:, s, 0:n], hi[4 + b][:, m], lo[4 + b][:, m],
                                          hid_hi[:, b, at:at + n], hid_lo[:, b, at:at + n], b == 0, b == GROUP - 1)
                        mm.then_inc(down_ready, 1)

        def free_of(eng, i, j):
            if j < 4:
                eng.wait_ge(up_ready[j // 2], i * NSP + NSP)
            else:
                eng.wait_ge(down_ready, i * (NSP * KB) + NSP * KB)

        def split_hi(act, i, j):
            act.wait_ge(landed[j % 2], i * 48 + 16 * (j // 2) + 16)
            act.activation(hi[j][:], raw[j % 2][:], ACT.Copy).then_inc(rounded[j % 2], 1)

        def split_lo(dve, i, j):
            dve.wait_ge(rounded[j % 2], i * 3 + j // 2 + 1)
            dve.tensor_tensor(lo[j][:], raw[j % 2][:], f32(hi[j][:]), ALU.subtract).then_inc(split[j % 2], 1)

        @block.scalar
        def _(act):
            for j in range(6):
                split_hi(act, 0, j)

            def group(i, more):
                for b in range(GROUP):
                    for t, (at, n) in enumerate(SPANS):
                        q = NSP * b + t
                        s = q % 2
                        act.wait_ge(up_ready[b], i * NSP + t + 1)
                        pb, pt = divmod((q - 2) % 6, NSP)
                        act.wait_ge(hid_ready[pt], i * GROUP + (pb + 2 if q >= 2 else 1))
                        act.activation(act_t[s][:, 0:n], ps_g[:, s, 0:n], ACT.Silu).then_inc(silu_done[s], 1)
                        act.wait_ge(prod_done[s], i * 3 + q // 2 + 2)
                        act.activation(hid_hi[:, b, at:at + n], act_t[s][:, 0:n], ACT.Copy).then_inc(hid_r[s], 1)
                    if more:
                        for j in (2 * b, 2 * b + 1):
                            free_of(act, i, j)
                            split_hi(act, i + 1, j)
                if more:
                    for j in (4, 5):
                        free_of(act, i, j)
                        split_hi(act, i + 1, j)
            with act.Fori(0, LAST) as i:
                group(i, True)
            group(LAST, False)

        @block.gpsimd
        def _(pool):
            pool.memset(acc[:], 0.0).then_inc(zeroed, 1)

        @block.vector
        def _(dve):
            for free in prod_done + hid_ready + down_evac:
                dve.sem_inc(free, 1)
            for j in range(6):
                split_lo(dve, 0, j)

            def group(i, more):
                for b in range(GROUP):
                    for t, (at, n) in enumerate(SPANS):
                        q = NSP * b + t
                        s = q % 2
                        dve.wait_ge(silu_done[s], i * 3 + q // 2 + 1)
                        dve.tensor_tensor(act_t[s][:, 0:n], ps_u[:, s, 0:n], act_t[s][:, 0:n],
                                          ALU.mult).then_inc(prod_done[s], 1)
                        dve.wait_ge(hid_r[s], i * 3 + q // 2 + 1)
                        dve.wait_ge(prod_done[s], i * 3 + q // 2 + 2)
                        dve.tensor_tensor(hid_lo[:, b, at:at + n], act_t[s][:, 0:n], f32(hid_hi[:, b, at:at + n]),
                                          ALU.subtract).then_inc(hid_ready[t], 1)
                    if more:
                        for j in (2 * b, 2 * b + 1):
                            split_lo(dve, i + 1, j)
                for t, (at, n) in enumerate(SPANS):
                    for m in range(KB):
                        dve.wait_ge(down_ready, i * (NSP * KB) + KB * t + m + 1)
                        dve.tensor_tensor(acc[:, m, at:at + n], ps_d[:, m % 4, 0:n], acc[:, m, at:at + n],
                                          ALU.add).then_inc(down_evac[m % 4], 1)
                if more:
                    for j in (4, 5):
                        split_lo(dve, i + 1, j)
            dve.wait_ge(zeroed, 1)
            with dve.Fori(0, LAST) as i:
                group(i, True)
            group(LAST, False)
            for s in range(4):
                dve.wait_ge(down_evac[s], FF_GROUPS * 2 * NSP + 1)


def turn_stage(nc, k, proj, b):
    sem = lambda n: k.sem("t_" + n)
    tabs_in, turned, evac = sem("tabs_in"), sem("turned"), [sem(f"evac{s}") for s in range(4)]
    shuffled, rotated, stored, pads = sem("shuffled"), sem("rotated"), sem("stored"), sem("pads")
    tile = lambda t: slice(t * P, (t + 1) * P)
    groups = [([b.kc_rows[:, a, :] for a in range(2)], b.kc_t[:].rearrange("p (a t) -> p a t", a=2)),
              ([proj[:, B_K, tile(t)] for t in range(2)], b.k_new[:])]
    for t in range(TILES):
        groups.append(([proj[:, B_V, tile(t)]], proj[:, B_V:B_V + 1, tile(t)]))
        groups.append(([proj[:, B_GK + p, tile(t)] for p in range(2)],
                       b.gk_rows[:, t, :].rearrange("p (a f) -> p a f", a=2)))
        groups.append(([proj[:, B_GV + h, tile(t)] for h in range(GH)], proj[:, B_GV:B_GV + GH, tile(t)]))
    n_on = [sum(1 for g in range(len(groups)) if g % 4 == s) for s in range(4)]
    LOADS = 9
    with nc.psum_tensor("t_ps", [P, 4, 512], F32) as ps, nc.Block() as block:
        @block.sync
        def _(sp):
            d = k.d
            for dst, src in ((b.rope[:], d["const_rope"]), (b.mask[:], d["const_mask"]), (b.gla_c[:], d["const_gla"]),
                             (b.kc_rows[:], d["cache_k"][0, 0].rearrange("(a p) g e -> p a (g e)", p=P)),
                             (b.vc[:], d["cache_v"][0, 0].rearrange("(a p) g e -> p a (g e)", p=P)),
                             (b.sink[:], d["attn_sink"][0].partition_broadcast(P)),
                             (b.b_up[:], d["gla_b_up"][0].rearrange("a n -> (a n)").partition_broadcast(P))):
                sp.dma_start(dst, src).then_inc(tabs_in, 16)
            sp.wait_ge(pads, 1)
            for a in range(2):
                sp.dma_start(b.w_up[96 + 16 * a:112 + 16 * a, 256 * a:256 * a + 256], d["gla_w_up"][0, a]).then_inc(tabs_in, 16)
            for g in (1, 2, 5):
                sp.wait_ge(evac[g % 4], g // 4 + 1)
            sp.dma_start(k.o[2][0, 0].rearrange("(a p) g e -> p a (g e)", p=P), b.k_new[:]).then_inc(stored, 16)
            sp.dma_start(k.o[3][0, 0].rearrange("(a p) g e -> p a (g e)", p=P),
                         proj[:, B_V, 0:CTX].rearrange("p (a f) -> p a f", a=2)).then_inc(stored, 16)
            sp.wait_ge(stored, 32)
            sp.wait_ge(tabs_in, 16 * LOADS)

        @block.gpsimd
        def _(pool):
            pool.memset(b.w_up[96:P, :], 0.0).then_inc(pads, 1)
            pool.wait_ge(pads, 1)
            pool.memset(b.kin[:], 0.0)

        @block.tensor
        def _(pe):
            pe.wait_ge(tabs_in, 16 * LOADS)
            for g, (srcs, _) in enumerate(groups):
                if g >= 4:
                    pe.wait_ge(evac[g % 4], g // 4)
                for a, src in enumerate(srcs):
                    mm = pe.transpose(ps[:, g % 4, a * P:(a + 1) * P], src, k.ident[:])
                mm.then_inc(turned, 1)

        def read_out(eng, g, op):
            srcs, dst = groups[g]
            eng.wait_ge(turned, g + 1)
            op(dst, ps[:, g % 4, 0:len(srcs) * P].rearrange("p (a f) -> p a f", f=P)).then_inc(evac[g % 4], 1)

        @block.scalar
        def _(act):
            for g in range(len(groups)):
                if g % 4 != 3:
                    read_out(act, g, lambda dst, src: act.activation(dst, src, ACT.Copy))

        @block.vector
        def _(dve):
            dve.wait_ge(tabs_in, 16 * LOADS)
            swap = [(i + 16) % 32 for i in range(32)]
            for q in range(5):
                x = proj[:, q, CTX:TOK]
                dve.stream_shuffle(b.rot[:], x, swap).then_inc(shuffled, 1)
                dve.wait_ge(shuffled, q + 1)
                dve.tensor_tensor(b.rot[:], b.rot[:], b.rope[:, LAT:2 * LAT], ALU.mult).then_inc(rotated, 1)
                dve.tensor_tensor(x, x, b.rope[:, 0:LAT], ALU.mult).then_inc(rotated, 1)
                dve.wait_ge(rotated, 3 * q + 2)
                dve.tensor_tensor(x, x, b.rot[:], ALU.add).then_inc(rotated, 1)
                dve.wait_ge(rotated, 3 * q + 3)
                for g in range(3 + 8 * q, min(3 + 8 * q + 8, len(groups)), 4):
                    read_out(dve, g, dve.tensor_copy)


def attention_stage(nc, k, proj, b):
    sem = lambda n: k.sem("a_" + n)
    (scored, masked, neg_max, exped, sink_exped, turned, pt_done, weighted, den_done, inv_done, scaled, out_turned,
     out_done) = [sem(n) for n in ("scored", "masked", "neg_max", "exped", "sink_exped", "turned", "pt_done", "weighted",
                                   "den_done", "inv_done", "scaled", "out_turned", "out_done")]
    flat = proj[:].rearrange("p b t -> p (b t)")
    units = [(t, q, g) for t in range(TILES) for q in range(4) for g in range(NKV)]
    U, PER = len(units), NQ
    keys = lambda t: CTX if t < CTX_TILES else 3 * P + CTX
    col = lambda u: (u // PER) * NQ + units[u][1] + 4 * units[u][2]
    with (
        nc.psum_tensor("a_s0", [P, 1024], F32) as s0, nc.psum_tensor("a_s1", [P, 1024], F32) as s1,
        nc.psum_tensor("a_t", [P, 1024], F32) as ps_t, nc.psum_tensor("a_v", [P, 512], F32) as ps_v,
        nc.psum_tensor("a_o", [P, 512], F32) as ps_o, nc.Block() as block,
    ):
        ps_s = [s0, s1]

        def score_cols(t):
            return (512, 768) if t < CTX_TILES else (P, 768)

        @block.tensor
        def _(pe):
            def scores(u):
                t, q, g = units[u]
                rows = slice(HD * g, HD * g + HD)
                if u >= 2:
                    pe.wait_ge(masked, u - 1)
                lhs = proj[rows, q, t * P:(t + 1) * P]
                if t < CTX_TILES:
                    mm = pe.matmul(ps_s[u % 2][:, 512:768], lhs, proj[rows, B_K, 0:CTX], start=True, stop=True)
                else:
                    at = B_K * TOK + (t - 1) * P
                    pe.matmul(ps_s[u % 2][:, P:512], lhs, flat[rows, at:at + 3 * P], start=True, stop=True)
                    mm = pe.matmul(ps_s[u % 2][:, 512:768], lhs, b.kc_t[rows, :], start=True, stop=True)
                mm.then_inc(scored, 1)

            def turn(u):
                pe.wait_ge(exped, u + 1)
                if u >= 1:
                    pe.wait_ge(pt_done, u)
                for a in range(keys(units[u][0]) // P):
                    mm = pe.transpose(ps_t[:, a * P:(a + 1) * P], b.prob[u % 2][:, a * P:(a + 1) * P], k.ident[:])
                mm.then_inc(turned, 1)

            def weigh(u):
                t, q, g = units[u]
                pe.wait_ge(pt_done, u + 1)
                if u % PER == 0 and u:
                    pe.wait_ge(scaled, u // PER)
                cols = slice((q + 4 * g) * HD, (q + 4 * g + 1) * HD)
                n = keys(t) // P
                for a in range(n):
                    if t < CTX_TILES:
                        v = proj[:, B_V, a * P + g * HD:a * P + (g + 1) * HD]
                    elif a < 3:
                        at = B_V * TOK + (t - 1 + a) * P + g * HD
                        v = flat[:, at:at + HD]
                    else:
                        v = b.vc[:, a - 3, g * HD:(g + 1) * HD]
                    mm = pe.matmul(ps_v[:, cols], b.prob_t[u % 2][:, a * P:(a + 1) * P], v, start=a == 0, stop=a == n - 1)
                mm.then_inc(weighted, 1)

            def turn_out(t):
                pe.wait_ge(scaled, t + 1)
                if t:
                    pe.wait_ge(out_done, t)
                for a in range(4):
                    mm = pe.transpose(ps_o[:, a * P:(a + 1) * P], b.att[t % 2][:, a * P:(a + 1) * P], k.ident[:])
                mm.then_inc(out_turned, 1)

            for u in range(U + 4):
                if u < U:
                    scores(u)
                if 1 <= u <= U:
                    turn(u - 1)
                if 2 <= u <= U + 1:
                    weigh(u - 2)
                if u >= 4 and (u - 4) % PER == PER - 1:
                    turn_out((u - 4) // PER)

        @block.scalar
        def _(act):
            def exps(u):
                t, q, g = units[u]
                c = col(u)
                act.wait_ge(neg_max, u + 1)
                if u >= 2:
                    act.wait_ge(turned, u - 1)
                act.activation(b.prob[u % 2][:, 0:keys(t)], b.score[u % 2][:, 0:keys(t)], ACT.Exp, bias=b.negm[:, c:c + 1],
                               accum_out=b.rsum[:, c:c + 1]).then_inc(exped, 1)
                act.activation(b.esink[:, c:c + 1], b.sink[:, q + 4 * g:q + 4 * g + 1], ACT.Exp,
                               bias=b.negm[:, c:c + 1]).then_inc(sink_exped, 1)

            def copy_t(u):
                act.wait_ge(turned, u + 1)
                if u >= 2:
                    act.wait_ge(weighted, u - 1)
                act.activation(b.prob_t[u % 2][:, 0:keys(units[u][0])], ps_t[:, 0:keys(units[u][0])], ACT.Copy).then_inc(pt_done, 1)

            for u in range(U + 4):
                if u < U:
                    exps(u)
                if 1 <= u <= U:
                    copy_t(u - 1)
                if u >= 4 and (u - 4) % PER == PER - 1:
                    t = (u - 4) // PER
                    act.wait_ge(out_turned, t + 1)
                    act.activation(proj[:, 0:4, t * P:(t + 1) * P], ps_o[:].rearrange("p (a f) -> p a f", a=4),
                                   ACT.Copy).then_inc(out_done, 1)

        @block.vector
        def _(dve):
            def mask(u):
                t, q, g = units[u]
                c = col(u)
                lo, hi = score_cols(t)
                kind = 0 if t == CTX_TILES else 2 if t == TILES - 1 else 1
                at = kind * (3 * P + CTX) + (3 * P if t < CTX_TILES else 0)
                dve.wait_ge(scored, u + 1)
                if u >= 2:
                    dve.wait_ge(exped, u - 1)
                dve.tensor_tensor_reduce(b.score[u % 2][:, 0:keys(t)], ps_s[u % 2][:, lo:hi], b.mask[:, at:at + keys(t)],
                                         HD ** -0.5, -3.0e38, ALU.add, ALU.max, b.rmax[:, c:c + 1]).then_inc(masked, 1)
                dve.wait_ge(masked, u + 1)
                dve.tensor_scalar(b.negm[:, c:c + 1], b.rmax[:, c:c + 1], b.sink[:, q + 4 * g:q + 4 * g + 1], -1.0,
                                  ALU.max, ALU.mult).then_inc(neg_max, 1)

            def finish(t):
                cols = slice(t * NQ, (t + 1) * NQ)
                dve.wait_ge(sink_exped, (t + 1) * PER)
                dve.tensor_tensor(b.den[:, cols], b.rsum[:, cols], b.esink[:, cols], ALU.add).then_inc(den_done, 1)
                dve.wait_ge(den_done, t + 1)
                dve.reciprocal(b.inv[:, cols], b.den[:, cols]).then_inc(inv_done, 1)
                dve.wait_ge(inv_done, t + 1)
                dve.wait_ge(weighted, (t + 1) * PER)
                if t >= 2:
                    dve.wait_ge(out_turned, t - 1)
                dve.tensor_tensor(b.att[t % 2][:].rearrange("p (h e) -> p h e", h=NQ), ps_v[:].rearrange("p (h e) -> p h e", h=NQ),
                                  b.inv[:, cols].unsqueeze(2).broadcast_to([P, NQ, HD]), ALU.mult).then_inc(scaled, 1)

            for u in range(U + 3):
                if u < U:
                    mask(u)
                if u >= 2 and (u - 2) % PER == PER - 1:
                    finish((u - 2) // PER)


def gla_stage(nc, k, proj, b):
    sem = lambda n: k.sem("g_" + n)
    (z_ready, z_sum, abs_r, exp_r, ln_ready, la_ready, b_ready, half_done, rel_done, ex_ready, mul_done, s_ready,
     kv_ready, at_ready, st_ready, o_ready, o_used, st_in) = [sem(n) for n in (
         "z_ready", "z_sum", "abs_r", "exp_r", "ln_ready", "la_ready", "b_ready", "half_done", "rel_done", "ex_ready",
         "mul_done", "s_ready", "kv_ready", "at_ready", "st_ready", "o_ready", "o_used", "st_in")]
    st_out = [sem("st_out0"), sem("st_out1")]
    inited = sem("inited")
    order = [(0, t) for t in range(TILES)] + [(1, t) for t in (1, 0)] + [(1, t) for t in range(TILES - 1, CTX_TILES - 1, -1)]
    U = len(order)
    starts = {0: None, CTX_TILES: 0, TILES: None, TILES + CTX_TILES: 1}
    ends = {CTX_TILES - 1: 0, TILES + CTX_TILES - 1: 1}
    tile = lambda t: slice(t * P, (t + 1) * P)
    steps = 2 * CPT
    last_col = lambda dr: GLA_C - 1 if dr == 0 else 0
    chunks = lambda dr: range(CPT) if dr == 0 else range(CPT - 1, -1, -1)
    with (
        nc.psum_tensor("g_z", [P, 512], F32) as ps_z, nc.psum_tensor("g_b", [P, 512], F32) as ps_b,
        nc.psum_tensor("g_s", [P, 2, 512], F32) as ps_s, nc.psum_tensor("g_o", [P, 2, 512], F32) as ps_o,
        nc.psum_tensor("g_kv", [P, CPT, 2, P], F32) as ps_kv, nc.Block() as block,
    ):
        decay = ps_b[:, 0:2 * P].rearrange("p (a t) -> p a t", a=2)

        @block.sync
        def _(sp):
            for dr, name in ((0, "state_gla_fwd"), (1, "state_gla_bwd")):
                for a in range(2):
                    sp.dma_start(b.s_in[dr][a * DK:(a + 1) * DK], k.d[name][0, 0, a::2].rearrange("q e v -> e q v")).then_inc(st_in, 16)
            for n, dr in ends.items():
                sp.wait_ge(st_ready, steps * (n + 1))
                for a in range(2):
                    sp.dma_start(k.o[4 + dr][0, 0, a::2].rearrange("q e v -> e q v"),
                                 b.state[(n + 1) % 2][a * DK:(a + 1) * DK, 0]).then_inc(st_out[dr], 16)
                sp.wait_ge(st_out[dr], 32)

        @block.tensor
        def _(pe):
            def gates(n):
                dr, t = order[n]
                if n >= 1:
                    pe.wait_ge(ex_ready, 4 * n)
                pe.matmul(ps_z[:, 0:256], proj[96:P, B_LR, tile(t)], b.w_up[96:P, dr * 256:dr * 256 + 256],
                          start=True, stop=True).then_inc(z_ready, 1)

            def sums(n):
                dr, t = order[n]
                pe.wait_ge(la_ready, n + 1)
                for a in range(2):
                    pe.matmul(decay[:, a], b.la[:, a * P:(a + 1) * P], b.gla_c[:, 3 * dr * P:(3 * dr + 1) * P],
                              start=True, stop=True)
                pe.matmul(ps_z[:, 256:512], b.gla_c[:, (3 * dr + 1) * P:(3 * dr + 2) * P], b.la[:],
                          start=True, stop=True).then_inc(b_ready, 1)

            def scores(n):
                pe.wait_ge(mul_done, 7 * n + 7)
                if n >= 1:
                    pe.wait_ge(at_ready, 2 * n)
                for h in range(GH):
                    rows = slice(DK * (h % 2), DK * (h % 2) + DK)
                    mm = pe.matmul(ps_s[:, h % 2, (h // 2) * P:(h // 2 + 1) * P], b.kp[rows, h // 2], b.qp[rows, h // 2],
                                   start=True, stop=True)
                mm.then_inc(s_ready, 1)

            def outer(n):
                dr, t = order[n]
                if n >= 1:
                    pe.wait_ge(st_ready, steps * n)
                for c in chunks(dr):
                    for h in range(GH):
                        mm = pe.matmul(ps_kv[DK * (h % 2):DK * (h % 2) + DK, c, h // 2, :], b.kin[:, c, h * DK:(h + 1) * DK],
                                       proj[:, B_GV + h, tile(t)], start=True, stop=True)
                mm.then_inc(kv_ready, 1)

            def outputs(n):
                dr, t = order[n]
                pe.wait_ge(at_ready, 2 * n + 2)
                if n >= 1:
                    pe.wait_ge(o_used, n)
                pe.wait_ge(st_ready, steps * (n + 1))
                for h in range(GH):
                    rows = slice(DK * (h % 2), DK * (h % 2) + DK)
                    cols = slice((h // 2) * P, (h // 2 + 1) * P)
                    pe.matmul(ps_o[:, h % 2, cols], b.at[:, h % 2, h // 2], proj[:, B_GV + h, tile(t)], start=True, stop=False)
                    for i, c in enumerate(chunks(dr)):
                        cc = slice(c * GLA_C, (c + 1) * GLA_C)
                        mm = pe.matmul(ps_o[cc, h % 2, cols], b.qin[rows, h // 2, cc], b.state[n % 2][rows, i, h // 2],
                                       start=False, stop=True)
                mm.then_inc(o_ready, 1)

            gates(0)
            for n in range(U):
                sums(n)
                if n + 1 < U:
                    pass
                scores(n)
                outer(n)
                if n + 1 < U:
                    gates(n + 1)
                outputs(n)

        @block.scalar
        def _(act):
            for n in range(U):
                act.wait_ge(z_sum, n + 1)
                act.activation(b.za[:], b.z[:], ACT.Abs).then_inc(abs_r, 1)
                act.wait_ge(abs_r, n + 1)
                act.activation(b.ze[:], b.za[:], ACT.Exp, scale=-1.0).then_inc(exp_r, 1)
                act.wait_ge(exp_r, n + 1)
                act.activation(b.zl[:], b.ze[:], ACT.Ln, bias=1.0).then_inc(ln_ready, 1)
                act.wait_ge(rel_done, n + 1)
                if n >= 1:
                    act.wait_ge(st_ready, steps * n)
                act.activation(b.eb[:], decay, ACT.Exp).then_inc(ex_ready, 1)
                act.activation(b.ep[:], b.rel[:], ACT.Exp).then_inc(ex_ready, 1)
                act.activation(b.en[:], b.rel[:], ACT.Exp, scale=-1.0).then_inc(ex_ready, 1)
                act.activation(b.er[:], ps_z[:, 256:512], ACT.Exp).then_inc(ex_ready, 1)

        @block.gpsimd
        def _(pool):
            pool.memset(b.zero[:], 0.0).then_inc(inited, 1)

        @block.vector
        def _(dve):
            dve.wait_ge(st_in, 64)
            dve.wait_ge(inited, 1)

            def log_gates(n):
                dr, t = order[n]
                dve.wait_ge(z_ready, n + 1)
                if n >= 1:
                    dve.wait_ge(abs_r, n)
                dve.tensor_tensor(b.z[:], ps_z[:, 0:256], b.b_up[:, dr * 256:dr * 256 + 256], ALU.add).then_inc(z_sum, 1)
                dve.wait_ge(ln_ready, n + 1)
                if n >= 1:
                    dve.wait_ge(b_ready, n)
                dve.scalar_tensor_tensor(out=b.la[:], in0=b.z[:], scalar=0.0, in1=b.zl[:], op0=ALU.min,
                                         op1=ALU.subtract).then_inc(la_ready, 1)

            def unit(n):
                dr, t = order[n]
                dve.wait_ge(b_ready, n + 1)
                lc = last_col(dr)
                chunked = decay.rearrange("p a (c t) -> p a c t", t=GLA_C)
                dve.tensor_scalar(b.half[:], chunked[:, :, :, lc], 0.5, None, ALU.mult).then_inc(half_done, 1)
                dve.wait_ge(half_done, n + 1)
                if n >= 1:
                    dve.wait_ge(ex_ready, 4 * n)
                dve.tensor_tensor(b.rel[:].rearrange("p a (c t) -> p a c t", t=GLA_C), chunked,
                                  b.half[:].unsqueeze(3).broadcast_to([P, 2, CPT, GLA_C]), ALU.subtract).then_inc(rel_done, 1)
                dve.wait_ge(ex_ready, 4 * n + 4)
                if n >= 1:
                    dve.wait_ge(o_ready, n)
                q, kk = proj[:, B_GQ:B_GQ + 2, tile(t)], proj[:, B_GK:B_GK + 2, tile(t)]
                sc = DK ** -0.5
                dve.scalar_tensor_tensor(out=b.qp[:], in0=q, scalar=sc, in1=b.ep[:], op0=ALU.mult, op1=ALU.mult).then_inc(mul_done, 1)
                dve.tensor_tensor(b.kp[:], kk, b.en[:], ALU.mult).then_inc(mul_done, 1)
                for c in range(CPT):
                    rows = slice(c * GLA_C, (c + 1) * GLA_C)
                    dve.tensor_tensor(b.kin[rows, c], b.gk_rows[rows, t], b.er[rows], ALU.mult).then_inc(mul_done, 1)
                dve.scalar_tensor_tensor(out=b.qin[:], in0=q, scalar=sc, in1=b.eb[:], op0=ALU.mult, op1=ALU.mult).then_inc(mul_done, 1)
                dve.wait_ge(s_ready, n + 1)
                m = b.gla_c[:, (3 * dr + 2) * P:(3 * dr + 3) * P]
                for par in range(2):
                    dve.tensor_tensor(b.at[:, par], ps_s[:, par, 0:2 * P].rearrange("p (a t) -> p a t", a=2),
                                      m.unsqueeze(1).broadcast_to([P, 2, P]), ALU.mult).then_inc(at_ready, 1)
                if n in starts:
                    src = b.zero[:] if starts[n] is None else b.s_in[starts[n]][:]
                    if n in (CTX_TILES, TILES + CTX_TILES):
                        dve.wait_ge(st_out[0 if n == CTX_TILES else 1], 32)
                    dve.tensor_copy(b.state[n % 2][:, 0], src).then_inc(inited, 1)
                    dve.wait_ge(inited, 2 + sorted(starts).index(n))
                dve.wait_ge(kv_ready, n + 1)
                for i, c in enumerate(chunks(dr)):
                    if i or n:
                        dve.wait_ge(st_ready, steps * n + 2 * i)
                    for a in range(2):
                        dst = b.state[n % 2][:, i + 1, a] if i + 1 < CPT else b.state[(n + 1) % 2][:, 0, a]
                        dve.scalar_tensor_tensor(out=dst, in0=b.state[n % 2][:, i, a],
                                                 scalar=b.eb[:, a, c * GLA_C + lc:c * GLA_C + lc + 1], in1=ps_kv[:, c, a],
                                                 op0=ALU.mult, op1=ALU.add).then_inc(st_ready, 1)

            def collect(n):
                dr, t = order[n]
                dve.wait_ge(o_ready, n + 1)
                dst = b.o_rows[:, t].rearrange("p (a q v) -> p q a v", q=2, v=DV)
                src = ps_o[:, :, 0:2 * P].rearrange("p q (a v) -> p q a v", a=2)
                if dr == 0:
                    dve.tensor_copy(dst, src).then_inc(o_used, 1)
                else:
                    dve.tensor_tensor(dst, src, dst, ALU.add).then_inc(o_used, 1)

            log_gates(0)
            for n in range(U):
                unit(n)
                if n + 1 < U:
                    log_gates(n + 1)
                collect(n)


def gla_out_stage(nc, k, proj, b):
    sem = lambda n: k.sem("e_" + n)
    sq_done, var_done, std_done, inv_done, normed, turned, evac, silu_done, w_in = [sem(n) for n in (
        "sq_done", "var_done", "std_done", "inv_done", "normed", "turned", "evac", "silu_done", "w_in")]
    tile = lambda t: slice(t * P, (t + 1) * P)
    with nc.psum_tensor("e_ps", [P, 2, 512], F32) as ps, nc.Block() as block:
        @block.sync
        def _(sp):
            with nc.allow_non_contiguous_dma(reason="one column of 128 values"):
                sp.dma_start(b.nw[:], k.d["gla_norm"].rearrange("a v -> v a")).then_inc(w_in, 16)

        @block.scalar
        def _(act):
            for t in range(TILES):
                for h in range(GH):
                    n = t * GH + h
                    if n >= 4:
                        act.wait_ge(sq_done, n - 3)
                    act.activation(b.junk[:, n % 4], b.o_rows[:, t, h * DV:(h + 1) * DV], ACT.Square,
                                   accum_out=b.var[:, t * GH + h:t * GH + h + 1]).then_inc(sq_done, 1)
            act.wait_ge(sq_done, TILES * GH)
            act.activation(b.std[:], b.var[:], ACT.Sqrt, bias=k.eps[:], scale=1.0 / DV).then_inc(std_done, 1)
            for h in range(GH):
                act.activation(proj[:, B_GG + h], proj[:, B_GG + h], ACT.Silu).then_inc(silu_done, 1)

        @block.vector
        def _(dve):
            dve.wait_ge(std_done, 1)
            dve.reciprocal(b.istd[:], b.std[:]).then_inc(inv_done, 1)
            dve.wait_ge(inv_done, 1)
            for t in range(TILES):
                o = b.o_rows[:, t].rearrange("p (h v) -> p h v", h=GH)
                dve.tensor_tensor(o, o, b.istd[:, t * GH:(t + 1) * GH].unsqueeze(2).broadcast_to([P, GH, DV]),
                                  ALU.mult).then_inc(normed, 1)
            dve.wait_ge(silu_done, GH)
            dve.wait_ge(w_in, 16)
            for t in range(TILES):
                dve.wait_ge(turned, t + 1)
                g = proj[:, B_GG:B_GG + GH, tile(t)]
                dve.scalar_tensor_tensor(out=g, in0=ps[:, t % 2].rearrange("p (h t) -> p h t", h=GH), scalar=b.nw[:, 0:1],
                                         in1=g, op0=ALU.mult, op1=ALU.mult).then_inc(evac, 1)

        @block.tensor
        def _(pe):
            for t in range(TILES):
                pe.wait_ge(normed, t + 1)
                if t >= 2:
                    pe.wait_ge(evac, t - 1)
                for h in range(GH):
                    mm = pe.transpose(ps[:, t % 2, h * P:(h + 1) * P], b.o_rows[:, t, h * DV:(h + 1) * DV], k.ident[:])
                mm.then_inc(turned, 1)


def mix_split_stage(nc, k, proj):
    rounded, split = k.sem("m_rounded"), k.sem("m_split")
    src = [0, 1, 2, 3] + [B_GG + h for h in range(GH)]
    with nc.Block() as block:
        @block.scalar
        def _(act):
            for j, q in enumerate(src):
                act.activation(k.h_hi[:, j], proj[:, q], ACT.Copy).then_inc(rounded, 1)

        @block.vector
        def _(dve):
            for j, q in enumerate(src):
                dve.wait_ge(rounded, j + 1)
                dve.tensor_tensor(k.h_lo[:, j], proj[:, q], f32(k.h_hi[:, j]), ALU.subtract).then_inc(split, 1)
            dve.wait_ge(split, len(src))


class MixerBuffers:

    def __init__(self, k):
        k.at = k.hi_at
        put = lambda name, shape: k.put("x_" + name, shape)
        self.kc_rows, self.vc, self.k_new = put("kc_rows", [P, 2, P]), put("vc", [P, 2, P]), put("k_new", [P, 2, P])
        self.kc_t = put("kc_t", [P, CTX])
        self.sink, self.b_up, self.w_up = put("sink", [P, NQ]), put("b_up", [P, 512]), put("w_up", [P, 512])
        self.gk_rows = put("gk_rows", [P, TILES, 2 * P])
        self.gla_c = put("gla_c", [P, 6 * P])
        self.kin = put("kin", [P, CPT, GH * DK])
        shared = k.at
        self.mask = put("mask", [P, 3 * (3 * P + CTX)])
        self.rope, self.rot = put("rope", [P, 2 * LAT]), put("rot", [P, LAT])
        self.score = [put(f"score{s}", [P, 3 * P + CTX]) for s in range(2)]
        self.prob = [put(f"prob{s}", [P, 3 * P + CTX]) for s in range(2)]
        self.prob_t = [put(f"prob_t{s}", [P, 3 * P + CTX]) for s in range(2)]
        self.att = [put(f"att{s}", [P, 512]) for s in range(2)]
        self.rmax, self.negm, self.rsum, self.esink, self.den, self.inv = [
            put(n, [P, TILES * NQ]) for n in ("rmax", "negm", "rsum", "esink", "den", "inv")]
        assert k.at <= k.rest
        k.at = shared
        self.o_rows = put("o_rows", [P, TILES, GH * DV])
        self.z, self.za, self.ze, self.zl, self.la, self.er = [put(n, [P, 256]) for n in ("z", "za", "ze", "zl", "la", "er")]
        self.eb, self.ep, self.en, self.rel, self.qp, self.kp, self.qin = [
            put(n, [P, 2, P]) for n in ("eb", "ep", "en", "rel", "qp", "kp", "qin")]
        self.half = put("half", [P, 2, CPT])
        self.at = put("at", [P, 2, 2, P])
        self.state = [put(f"state{s}", [P, CPT, 2, DV]) for s in range(2)]
        self.s_in = [put(f"s_in{s}", [P, 2, DV]) for s in range(2)]
        self.zero = put("zero", [P, 2, DV])
        self.junk, self.nw = put("junk", [P, 4, DV]), put("nw", [P, 1])
        self.var, self.std, self.istd = [put(n, [P, TILES * GH]) for n in ("var", "std", "istd")]
        assert k.at <= k.rest


def mixer(nc, k):
    k.at = k.rest
    proj = k.put("proj", [P, PROJB, TOK])
    w_in = k.d["w_in"][0].rearrange("(k p) n -> p k n", p=P)

    def heads(i, b):
        return [(lambda r, q=q: r[:, :, q * HD:(q + 1) * HD], w_in[:, :, 64 * (2 * i + b) + 256 * q:64 * (2 * i + b) + 256 * q + 64])
                for q in range(2)]

    def plain(i, b):
        return k_halves(w_in, i * (2 * P) + b * P)

    gemm_stage(nc, k, "wi", [((0, 2), heads), ((2, 9), plain)], k_halves(w_in, IN_W - P), 18, proj)
    b = MixerBuffers(k)
    turn_stage(nc, k, proj, b)
    attention_stage(nc, k, proj, b)
    gla_stage(nc, k, proj, b)
    gla_out_stage(nc, k, proj, b)
    mix_split_stage(nc, k, proj)


def k_halves(w, col):
    h = KB // 2
    return [(lambda r, q=q: r[:, q * h:(q + 1) * h, :], w[:, q * h:(q + 1) * h, ds(col, P)]) for q in range(2)]


def layer(nc, d, o):
    k = Core(nc, d, o)
    ACC = 4 * KB * TOK

    def accumulator(n):
        k.at = k.rest
        return k.put(f"acc{n}", [P, KB, TOK])

    modulation_stage(nc, k)
    k.at = k.rest
    norm_stage(nc, k, None, 0, None)
    acc = accumulator(0)
    ffn_stage(nc, k, 0, acc)
    k.at = k.rest + ACC
    norm_stage(nc, k, 0, 1, acc)
    mixer(nc, k)
    k.recycle()
    acc = accumulator(1)
    w_out = d["w_out"][0].rearrange("(k p) n -> p k n", p=P)
    gemm_stage(nc, k, "wo", [((0, KB // 2), lambda i, b: k_halves(w_out, i * (2 * P) + b * P))], None, KB, acc)
    k.at = k.rest + ACC
    norm_stage(nc, k, 1, 2, acc)
    acc = accumulator(2)
    ffn_stage(nc, k, 1, acc)
    k.at = k.rest + ACC
    norm_stage(nc, k, 2, None, acc)


_INS = ["x_prompt", "x_sample", "cache_k", "cache_v", "state_gla_fwd", "state_gla_bwd", "c", "c_ctx", "w_ada", "b_ada",
        "norm_pre", "norm_post", "ffn_w1", "ffn_w3", "ffn_w2", "w_in", "gla_w_up", "gla_b_up", "gla_norm", "attn_sink",
        "w_out"]
_OUTS = [(1, CTX, D), (1, LAT, D), (1, 1, CTX, NKV, HD), (1, 1, CTX, NKV, HD), (1, 1, GH, DK, DV), (1, 1, GH, DK, DV)]


def kernel(**inputs):
    import concourse.bacc as bacc
    from concourse.bass_utils import run_bass_kernel_spmd

    nc = bacc.Bacc("TRN2", target_bir_lowering=False, num_devices=1)
    arrays = {name: np.ascontiguousarray(inputs[name]) for name in _INS}
    arrays.update(shape_constants())
    d = {name: nc.dram_tensor(f"in_{name}", a.shape, mybir.dt.from_np(a.dtype), kind="ExternalInput").ap()
         for name, a in arrays.items()}
    o = [nc.dram_tensor(f"out_{i}", shape, F32, kind="ExternalOutput").ap() for i, shape in enumerate(_OUTS)]
    layer(nc, d, o)
    r = run_bass_kernel_spmd(nc, [{f"in_{name}": a for name, a in arrays.items()}], core_ids=[0])
    return tuple(r.results[0][f"out_{i}"] for i in range(len(_OUTS)))
```

```python
import numpy as np
import concourse.bass as bass
from concourse import mybir

F32 = mybir.dt.float32
F32R = mybir.dt.float32r
ALU = mybir.AluOpType
ACT = mybir.ActivationFunctionType
AX_X = mybir.AxisListType.X
ds = bass.ds

P = 128
D = 1024
KB = D // P
CTX, LAT = 256, 1024
TOK = CTX + LAT
TILES = TOK // P
CTX_TILES = CTX // P
FF = 2816
FFB = FF // P
GROUP = 2
FF_GROUPS = FFB // GROUP
N_MOD = 9
MODB = N_MOD * KB
SPANS = [(0, 256), (256, 512), (768, 512)]
NSP = len(SPANS)
CH = 256
NCH = TOK // CH
EPS = 1e-6
NEG = -1e30
GRID_W = 64
HD = 64
NQ, NKV = 8, 2
GLA_C = 32
CPT = P // GLA_C
GH, DK, DV = 4, 64, 128
IN_W = 2336
B_Q, B_K, B_V, B_GQ, B_GK, B_GV, B_GG, B_LR = 0, 4, 5, 6, 8, 10, 14, 18
PROJB = 19


def shape_constants():
    ident = np.eye(P, dtype=np.float32)
    ones = np.full((P, P), 1.0 / D, np.float32)
    t = np.arange(LAT)
    half = HD // 2
    inv = (10000.0 ** (-np.arange(0, half, 2, dtype=np.float32) / np.float32(half))).astype(np.float32)
    p = np.arange(P)
    in_col = (p % HD) >= half
    freq = inv[p % (half // 2)]
    pos = np.where(in_col[:, None], (t % GRID_W)[None], (t // GRID_W)[None]).astype(np.float32)
    ang = (pos * freq[:, None]).astype(np.float32)
    cos = np.cos(ang).astype(np.float32)
    sin = np.sin(ang).astype(np.float32) * np.where((p % half) < half // 2, -1, 1)[:, None]
    r = np.arange(P)[:, None]
    j = np.arange(3 * P)[None]
    win = np.where(np.abs(j - P - r) <= P, 0.0, NEG).astype(np.float32)
    masks = []
    for first, last in ((True, False), (False, False), (False, True)):
        m = np.zeros((P, 3 * P + CTX), np.float32)
        m[:, :3 * P] = win
        if first:
            m[:, :P] = NEG
        if last:
            m[:, 2 * P:3 * P] = NEG
        masks.append(m)
    s, q = np.arange(P)[:, None], np.arange(P)[None]
    same = (s // GLA_C) == (q // GLA_C)
    tau = 1.0 / 16.0
    gla = []
    for incl, rest in ((s <= q, s > q), (s >= q, s < q)):
        gla += [np.where(same & incl, tau, 0.0), np.where(same & rest, tau, 0.0), np.where(same & incl, 1.0, 0.0)]
    return {
        "const_ident": ident, "const_sel": (np.arange(P)[:, None] % 32 == np.arange(2)[None]).astype(np.float32), "const_mean": ones,
        "const_rope": np.concatenate([cos, sin], 1).astype(np.float32),
        "const_mask": np.concatenate(masks, 1).astype(np.float32),
        "const_gla": np.concatenate(gla, 1).astype(np.float32),
    }


class Core:

    def __init__(self, nc, d, o):
        self.nc, self.d, self.o = nc, d, o
        self.live = []
        self.base = -(-nc.sbuf_base // 64) * 64
        self.end = nc.sbuf_usable_end
        self.at = self.base
        put = self.put
        self.ident = put("ident", [P, P])
        self.mean = put("mean", [P, P])
        self.mod = put("mod", [P, MODB, 2])
        self.vec = put("vec", [P, MODB + 48])
        self.pre = put("pre", [P, 3, KB, 2])
        self.gate = put("gate", [P, 3, KB, 2])
        self.eps = put("eps", [P, 1])
        self.hi_at = self.at
        self.h_hi = put("h_hi", [P, KB, TOK], F32R)
        self.h_lo = put("h_lo", [P, KB, TOK], F32R)
        self.rest = self.at
        self.x_t = nc.dram_tensor("x_t", [P, KB, TOK], F32, kind="Internal").ap()

    def put(self, name, shape, dt=F32):
        n = -(-int(np.prod(shape[1:])) * 4 // 32) * 32
        assert self.at + n <= self.end, (name, self.at + n - self.end)
        t = self.nc.alloc_sbuf_tensor_at(name, shape, dt, offset=self.at)
        self.at += n
        return t

    def sem(self, name):
        s = self.nc.alloc_semaphore(name)
        self.live.append(s)
        return s

    def recycle(self):
        self.nc.clear_and_free_semaphores(self.live)
        self.nc.all_engine_barrier()
        self.live = []


def f32(ap):
    return ap.bitcast(F32)


def product3(pe, out, w_hi, w_lo, x_hi, x_lo, first, last):
    pe.matmul(out, w_hi, x_hi, start=first, stop=False)
    pe.matmul(out, w_hi, x_lo, start=False, stop=False)
    return pe.matmul(out, w_lo, x_hi, start=False, stop=last)


def modulation_stage(nc, k):
    WB = 4
    RING = 3
    LOADS = MODB // WB
    ROUNDS = LOADS // RING
    COLT = 4
    k.at = k.hi_at
    rows = k.put("mod_rows", [MODB + 48, P])
    cond_rows = k.put("cond_rows", [2 * KB, P])
    cond = k.put("cond", [P, KB, 32])
    sel = k.put("sel", [P, 2])
    w = [k.put(f"ada_w{s}", [P, KB, WB * P]) for s in range(RING)]
    sums = [k.put(f"ada_s{s}", [P, WB * P]) for s in range(RING)]
    k.at = k.rest
    rows_in, w_in = k.sem("rows_in"), [k.sem(f"ada_in{s}") for s in range(RING)]
    w_used = [k.sem(f"ada_used{s}") for s in range(RING)]
    turned, cond_ready, cond_zero, vec_ready, coef = [k.sem(n) for n in (
        "rows_turned", "cond_ready", "cond_zero", "vec_ready", "mod_coef")]
    copied, added, evac = [[k.sem(f"ada_{n}{s}") for s in range(RING)] for n in ("copied", "added", "evac")]
    d = k.d
    with (
        nc.psum_tensor("ps_rows", [P, 512], F32) as ps_rows,
        nc.psum_tensor("ps_m", [P, RING, 512], F32) as ps_m,
        nc.psum_tensor("ps_q", [P, RING, 512], F32) as ps_q,
        nc.Block() as block,
    ):
        @block.sync
        def _(sp):
            for dst, src in ((k.ident[:], d["const_ident"]), (k.mean[:], d["const_mean"]), (sel[:], d["const_sel"]),
                             (rows[0:MODB, :], d["b_ada"].rearrange("a (b p) -> (a b) p", p=P)),
                             (rows[MODB:MODB + 24, :], d["norm_pre"].rearrange("a i (b p) -> (a i b) p", p=P)),
                             (rows[MODB + 24:MODB + 48, :], d["norm_post"].rearrange("a i (b p) -> (a i b) p", p=P)),
                             (cond_rows[0:KB, :], d["c_ctx"].rearrange("(b p) -> b p", p=P)),
                             (cond_rows[KB:2 * KB, :], d["c"].rearrange("a (b p) -> (a b) p", p=P))):
                sp.dma_start(dst, src).then_inc(rows_in, 16)
            w_ada = d["w_ada"].rearrange("a (k p) n -> (a p) k n", p=P)
            with sp.Fori(0, ROUNDS) as i:
                for s in range(RING):
                    sp.wait_ge(w_used[s], i + 1)
                    sp.dma_start(w[s][:], w_ada[:, :, ds(i * (RING * WB * P) + s * WB * P, WB * P)]).then_inc(w_in[s], 16)

        @block.gpsimd
        def _(pool):
            pool.memset(cond[:], 0.0).then_inc(cond_zero, 1)

        @block.tensor
        def _(pe):
            for s in range(RING):
                pe.sem_inc(w_used[s], 1)
            pe.wait_ge(rows_in, 16 * 8)
            pe.transpose(ps_rows[:, 0:MODB + 48], rows[:], k.ident[0:MODB + 48, 0:MODB + 48])
            pe.transpose(ps_rows[:, 256:256 + 2 * KB], cond_rows[:], k.ident[0:2 * KB, 0:2 * KB]).then_inc(turned, 1)
            pe.wait_ge(cond_ready, 1)
            with pe.Fori(0, ROUNDS) as i:
                for s in range(RING):
                    pe.wait_ge(w_in[s], i * 16 + 16)
                    pe.wait_ge(copied[s], i + 1)
                    for kk in range(KB):
                        c = kk % COLT
                        mm = pe.matmul(ps_m[32 * c:32 * c + 32, s], cond[:, kk], w[s][:, kk], start=kk < COLT,
                                       stop=kk >= KB - COLT, skip_group_check=True)
                    mm.then_inc(w_used[s], 1)
                    pe.wait_ge(copied[s], i + 2)
                    pe.wait_ge(evac[s], i + 1)
                    for b in range(WB):
                        mm = pe.matmul(ps_q[:, s, 2 * b:2 * b + 2], sums[s][:, b * P:(b + 1) * P], sel[:], start=True, stop=True)
                    mm.then_inc(added[s], 1)

        @block.scalar
        def _(act):
            for s in range(RING):
                act.sem_inc(copied[s], 1)
            act.wait_ge(turned, 1)
            act.wait_ge(cond_zero, 1)
            act.activation(cond[:, :, 0:2], ps_rows[:, 256:256 + 2 * KB].rearrange("p (c k) -> p k c", c=2),
                           ACT.Silu).then_inc(cond_ready, 1)
            with act.Fori(0, ROUNDS) as i:
                for s in range(RING):
                    act.wait_ge(w_used[s], i + 2)
                    act.activation(sums[s][:], ps_m[:, s], ACT.Copy).then_inc(copied[s], 1)

        @block.vector
        def _(dve):
            for s in range(RING):
                dve.sem_inc(evac[s], 1)
            dve.memset(k.eps[:], EPS)
            dve.wait_ge(cond_ready, 1)
            dve.tensor_copy(k.vec[:], ps_rows[:, 0:MODB + 48]).then_inc(vec_ready, 1)
            dve.wait_ge(vec_ready, 1)
            with dve.Fori(0, ROUNDS) as i:
                for s in range(RING):
                    dve.wait_ge(added[s], i + 1)
                    at = i * (RING * WB) + s * WB
                    dve.tensor_tensor(k.mod[:, ds(at, WB), :], ps_q[:, s, 0:2 * WB].rearrange("p (b c) -> p b c", c=2),
                                      k.vec[:, ds(at, WB)].unsqueeze(2).broadcast_to([P, WB, 2]),
                                      ALU.add).then_inc(evac[s], 1)
            for s in range(RING):
                dve.wait_ge(evac[s], ROUNDS + 1)
            for i in range(3):
                shift = MODB + KB * i
                dve.scalar_tensor_tensor(
                    out=k.pre[:, i], in0=k.mod[:, (3 * i + 1) * KB:(3 * i + 2) * KB, :], scalar=1.0,
                    in1=k.vec[:, shift:shift + KB].unsqueeze(2).broadcast_to([P, KB, 2]),
                    op0=ALU.add, op1=ALU.mult).then_inc(coef, 1)
                dve.scalar_tensor_tensor(
                    out=k.gate[:, i], in0=k.mod[:, (3 * i + 2) * KB:(3 * i + 3) * KB, :], scalar=1.0 if i == 1 else 0.5,
                    in1=k.vec[:, shift + 24:shift + 24 + KB].unsqueeze(2).broadcast_to([P, KB, 2]),
                    op0=ALU.mult, op1=ALU.mult).then_inc(coef, 1)
            dve.wait_ge(coef, 6)


def norm_stage(nc, k, i_post, i_pre, acc):
    n_ = f"n{0 if i_post is None else i_post + 1}_"
    first, final = i_post is None, i_pre is None
    put = lambda name, shape, dt=F32: k.put(n_ + name, shape, dt)
    sem = lambda name: k.sem(n_ + name)
    XR = 3
    x = [put(f"x{s}", [P, KB, CH]) for s in range(XR)]
    if first or final:
        nat = [put(f"nat{s}", [P, 2, D]) for s in range(2)]
    if not first:
        tmp_o, sq_o = put("tmp_o", [P, KB, CH]), put("sq_o", [P, KB, CH])
    if not final:
        tmp_p = [put(f"tmp_p{s}", [P, KB, CH]) for s in range(2)]
        v = [put(f"v{s}", [P, KB, CH]) for s in range(2)]
        sq_p = put("sq_p", [P, KB, CH])
    std = put("std", [P, 2, CH])
    rstd = put("rstd", [P, 2, CH])
    x_in = [sem(f"x_in{s}") for s in range(XR)]
    x_out = [sem(f"x_out{s}") for s in range(XR)]
    x_ready = sem("x_ready")
    if not first:
        o_sq, o_mean, o_std, o_rstd, o_scaled = [sem(s) for s in ("o_sq", "o_mean", "o_std", "o_rstd", "o_scaled")]
    if not final:
        p_sq, p_mean, p_std, p_rstd, p_scaled, p_v, p_hi, p_lo = [sem(s) for s in (
            "p_sq", "p_mean", "p_std", "p_rstd", "p_scaled", "p_v", "p_hi", "p_lo")]
    if first or final:
        turned, evac = sem("turned"), sem("evac")
    d, o = k.d, k.o
    x_rows = [d["x_prompt"][0].rearrange("(a p) f -> p a f", p=P)] + [
        d["x_sample"][0, CH * n:CH * (n + 1)].rearrange("(a p) f -> p a f", p=P) for n in range(NCH - 1)]
    y_rows = [o[0][0].rearrange("(a p) f -> p a f", p=P)] + [
        o[1][0, CH * n:CH * (n + 1)].rearrange("(a p) f -> p a f", p=P) for n in range(NCH - 1)]
    chunk = lambda n: slice(n * CH, (n + 1) * CH)
    cond = lambda n: 0 if n == 0 else 1
    uses = lambda s, ring: len(range(s, NCH, ring))
    with (
        nc.psum_tensor(n_ + "ps_o", [P, 512], F32) as ps_o,
        nc.psum_tensor(n_ + "ps_p", [P, 512], F32) as ps_p,
        nc.psum_tensor(n_ + "ps_x", [P, KB, CH], F32) as ps_x,
        nc.Block() as block,
    ):
        def store(sp, n):
            if final:
                sp.wait_ge(evac, n + 1)
                sp.dma_start(y_rows[n], nat[n % 2][:]).then_inc(x_out[n % 2], 16)
            else:
                sp.wait_ge(x_ready, n + 1)
                sp.dma_start(k.x_t[:, :, chunk(n)], x[n % XR][:]).then_inc(x_out[n % XR], 16)

        @block.sync
        def _(sp):
            for n in range(NCH):
                if first:
                    if n >= 2:
                        sp.wait_ge(turned, n - 1)
                    sp.dma_start(nat[n % 2][:], x_rows[n]).then_inc(x_in[n % 2], 16)
                else:
                    if n >= XR:
                        if final:
                            sp.wait_ge(turned, n - XR + 1)
                        else:
                            sp.wait_ge(x_out[n % XR], 16 * (n // XR))
                            sp.wait_ge(p_scaled, n - XR + 1)
                    sp.dma_start(x[n % XR][:], k.x_t[:, :, chunk(n)]).then_inc(x_in[n % XR], 16)
                if n >= 2:
                    store(sp, n - 2)
            store(sp, NCH - 2)
            store(sp, NCH - 1)
            ring = 2 if final else XR
            for s in range(ring):
                sp.wait_ge(x_out[s], 16 * uses(s, ring))

        @block.tensor
        def _(pe):
            def turn_in(n):
                pe.wait_ge(x_in[n % 2], 16 * (n // 2 + 1))
                if n >= 1:
                    pe.wait_ge(x_ready, n)
                for a in range(2):
                    for b in range(KB):
                        mm = pe.transpose(ps_x[:, b, a * P:(a + 1) * P], nat[n % 2][:, a, b * P:(b + 1) * P], k.ident[:])
                mm.then_inc(turned, 1)

            def turn_out(n):
                pe.wait_ge(x_ready, n + 1)
                if n >= 1:
                    pe.wait_ge(evac, n)
                for a in range(2):
                    for b in range(KB):
                        mm = pe.transpose(ps_x[:].rearrange("p b t -> p (b t)")[:, a * D + b * P:a * D + (b + 1) * P],
                                          x[n % XR][:, b, a * P:(a + 1) * P], k.ident[:])
                mm.then_inc(turned, 1)

            def mean(n, squares, sq, bank, std_ready, out_sem):
                pe.wait_ge(squares, n + 1)
                if n >= 1:
                    pe.wait_ge(std_ready, n)
                for b in range(KB):
                    mm = pe.matmul(bank[:, 0:CH], k.mean[:], sq[:, b], start=b == 0, stop=b == KB - 1)
                mm.then_inc(out_sem, 1)

            for i in range(-1, NCH):
                if i + 1 < NCH:
                    if first:
                        turn_in(i + 1)
                    else:
                        mean(i + 1, o_sq, sq_o, ps_o, o_std, o_mean)
                if i >= 0:
                    if final:
                        turn_out(i)
                    else:
                        mean(i, p_sq, sq_p, ps_p, p_std, p_mean)

        @block.scalar
        def _(act):
            def square_o(n):
                if first:
                    act.wait_ge(turned, n + 1)
                    if n >= XR:
                        act.wait_ge(x_out[n % XR], 16 * (n // XR))
                        act.wait_ge(p_scaled, n - XR + 1)
                    act.activation(x[n % XR][:], ps_x[:], ACT.Copy).then_inc(x_ready, 1)
                else:
                    if n >= 1:
                        act.wait_ge(o_mean, n)
                    act.activation(sq_o[:], acc[:, :, chunk(n)], ACT.Square).then_inc(o_sq, 1)

            def root(n, mean_ready, rstd_ready, bank, row, out_sem):
                act.wait_ge(mean_ready, n + 1)
                if n >= 1:
                    act.wait_ge(rstd_ready, n)
                act.activation(std[:, row, :], bank[:, 0:CH], ACT.Sqrt, bias=k.eps[:]).then_inc(out_sem, 1)

            def square_p(n):
                act.wait_ge(x_ready, n + 1)
                if n >= 1:
                    act.wait_ge(p_mean, n)
                act.activation(sq_p[:], x[n % XR][:], ACT.Square).then_inc(p_sq, 1)

            def modulate(n):
                s, c = n % 2, cond(n)
                act.wait_ge(p_scaled, n + 1)
                if n >= 2:
                    act.wait_ge(p_lo, n - 1)
                for b in range(KB):
                    act.activation(v[s][:, b], tmp_p[s][:, b], ACT.Identity, bias=k.mod[:, 3 * i_pre * KB + b, c:c + 1],
                                   scale=k.pre[:, i_pre, b, c:c + 1]).then_inc(p_v, 1)
                act.wait_ge(p_v, KB * (n + 1))
                act.activation(k.h_hi[:, :, chunk(n)], v[s][:], ACT.Copy).then_inc(p_hi, 1)

            def rows_out(n):
                act.wait_ge(turned, n + 1)
                if n >= 2:
                    act.wait_ge(x_out[n % 2], 16 * (n // 2))
                act.activation(nat[n % 2][:].rearrange("p a f -> p (a f)"), ps_x[:].rearrange("p b t -> p (b t)"),
                               ACT.Copy).then_inc(evac, 1)

            for i in range(-1, NCH + (0 if final else 2)):
                if i + 1 < NCH:
                    square_o(i + 1)
                if not final and 0 <= i - 1 < NCH:
                    root(i - 1, p_mean, p_rstd, ps_p, 1, p_std)
                if not final and i - 2 >= 0:
                    modulate(i - 2)
                if not first and i + 1 < NCH:
                    root(i + 1, o_mean, o_rstd, ps_o, 0, o_std)
                if 0 <= i < NCH:
                    rows_out(i) if final else square_p(i)

        @block.gpsimd
        def _(pool):
            if not final:
                for n in range(NCH):
                    pool.wait_ge(p_hi, n + 1)
                    pool.tensor_tensor(k.h_lo[:, :, chunk(n)], v[n % 2][:], f32(k.h_hi[:, :, chunk(n)]),
                                       ALU.subtract).then_inc(p_lo, 1)
                pool.wait_ge(p_lo, NCH)

        @block.vector
        def _(dve):
            def scale(n, std_ready, row, rstd_ready, src, dst, out_sem):
                dve.wait_ge(std_ready, n + 1)
                if n >= 1:
                    dve.wait_ge(out_sem, n)
                dve.reciprocal(rstd[:, row, :], std[:, row, :]).then_inc(rstd_ready, 1)
                dve.wait_ge(rstd_ready, n + 1)
                dve.tensor_tensor(dst, src, rstd[:, row:row + 1, :].broadcast_to([P, KB, CH]), ALU.mult).then_inc(out_sem, 1)

            def residual(n):
                c, xs = cond(n), x[n % XR]
                if n >= 1:
                    dve.wait_ge(x_ready, n)
                scale(n, o_std, 0, o_rstd, acc[:, :, chunk(n)], tmp_o[:], o_scaled)
                dve.wait_ge(x_in[n % XR], 16 * (n // XR + 1))
                dve.wait_ge(o_scaled, n + 1)
                for b in range(KB):
                    ins = dve.scalar_tensor_tensor(out=xs[:, b], in0=tmp_o[:, b], scalar=k.gate[:, i_post, b, c:c + 1],
                                                   in1=xs[:, b], op0=ALU.mult, op1=ALU.add)
                ins.then_inc(x_ready, 1)

            def norm(n):
                if n >= 2:
                    dve.wait_ge(p_v, KB * (n - 1))
                dve.wait_ge(x_ready, n + 1)
                scale(n, p_std, 1, p_rstd, x[n % XR][:], tmp_p[n % 2][:], p_scaled)

            for i in range(NCH + 1):
                if not first and i < NCH:
                    residual(i)
                if not final and i >= 1:
                    norm(i - 1)


def gemm_stage(nc, k, name, w_halves, tail_cols, blocks, out_buf, parts=2):
    put = lambda n, shape, dt=F32: k.put(f"{name}_{n}", shape, dt)
    sem = lambda n: k.sem(f"{name}_{n}")
    raw = [put(f"raw{b}", [P, KB, P]) for b in range(2)]
    hi = [put(f"hi{b}", [P, KB, P], F32R) for b in range(2)]
    lo = [put(f"lo{b}", [P, KB, P], F32R) for b in range(2)]
    landed = [sem(f"landed{b}") for b in range(2)]
    rounded = [sem(f"rounded{b}") for b in range(2)]
    split = [sem(f"split{b}") for b in range(2)]
    ready = sem("ready")
    evac = [sem(f"evac{t}") for t in range(2 * NSP)]
    rounds = blocks // 2
    tail = tail_cols is not None
    with (
        nc.psum_tensor(name + "_ps", [P, 2 * NSP, 512], F32) as ps,
        nc.Block() as block,
    ):
        @block.sync
        def _(sp):
            for rng, halves in w_halves:
                def load(i, first):
                    for b in range(2):
                        if not first:
                            sp.wait_ge(split[b], i)
                        for part, src in halves(i, b):
                            sp.dma_start(part(raw[b]), src).then_inc(landed[b], 16)
                lo_, hi_ = rng
                if lo_ == 0:
                    load(0, True)
                    lo_ = 1
                if hi_ - lo_ == 1:
                    load(lo_, False)
                elif hi_ > lo_:
                    with sp.Fori(lo_, hi_) as i:
                        load(i, False)
            if tail:
                sp.wait_ge(split[0], rounds)
                for part, src in tail_cols:
                    sp.dma_start(part(raw[0]), src).then_inc(landed[0], 16)

        @block.tensor
        def _(pe):
            def one(i, b):
                pe.wait_ge(split[b], i + 1)
                for t, (at, n) in enumerate(SPANS):
                    pe.wait_ge(evac[NSP * b + t], i + 1)
                    for kk in range(KB):
                        mm = product3(pe, ps[:, NSP * b + t, 0:n], hi[b][:, kk], lo[b][:, kk],
                                      k.h_hi[:, kk, at:at + n], k.h_lo[:, kk, at:at + n], kk == 0, kk == KB - 1)
                    mm.then_inc(ready, 1)
            with pe.Fori(0, rounds) as i:
                for b in range(2):
                    one(i, b)
            if tail:
                one(rounds, 0)

        def split_hi(act, i, b):
            act.wait_ge(landed[b], i * (16 * parts) + 16 * parts)
            act.activation(hi[b][:], raw[b][:], ACT.Copy).then_inc(rounded[b], 1)

        def split_lo(dve, i, b):
            dve.wait_ge(rounded[b], i + 1)
            dve.tensor_tensor(lo[b][:], raw[b][:], f32(hi[b][:]), ALU.subtract).then_inc(split[b], 1)

        def free_banks(eng, spans):
            for b in range(2):
                for t in spans:
                    eng.sem_inc(evac[NSP * b + t], 1)

        def out_of(eng, i, b, spans, op, with_next):
            for t in spans:
                at, n = SPANS[t]
                eng.wait_ge(ready, i * (2 * NSP) + NSP * b + t + 1)
                dst = out_buf[:, ds(2 * i + b, 1), at:at + n]
                op(dst, ps[:, NSP * b + t:NSP * b + t + 1, 0:n]).then_inc(evac[NSP * b + t], 1)
            if with_next:
                eng.wait_ge(ready, i * (2 * NSP) + NSP * (b + 1))

        @block.scalar
        def _(act):
            copy = lambda dst, src: act.activation(dst, src, ACT.Copy)
            free_banks(act, (0, 1))
            for b in range(2):
                split_hi(act, 0, b)
            if rounds > 1:
                with act.Fori(0, rounds - 1) as i:
                    for b in range(2):
                        out_of(act, i, b, (0, 1), copy, True)
                        split_hi(act, i + 1, b)
            out_of(act, rounds - 1, 0, (0, 1), copy, tail)
            if tail:
                split_hi(act, rounds, 0)
            out_of(act, rounds - 1, 1, (0, 1), copy, False)
            if tail:
                out_of(act, rounds, 0, (0, 1), copy, False)

        @block.vector
        def _(dve):
            free_banks(dve, (2,))
            for b in range(2):
                split_lo(dve, 0, b)
            if rounds > 1:
                with dve.Fori(0, rounds - 1) as i:
                    for b in range(2):
                        out_of(dve, i, b, (2,), dve.tensor_copy, True)
                        split_lo(dve, i + 1, b)
            out_of(dve, rounds - 1, 0, (2,), dve.tensor_copy, tail)
            if tail:
                split_lo(dve, rounds, 0)
            out_of(dve, rounds - 1, 1, (2,), dve.tensor_copy, False)
            if tail:
                out_of(dve, rounds, 0, (2,), dve.tensor_copy, False)


def ffn_stage(nc, k, which, acc):
    f = f"f{which}_"
    put = lambda n, shape, dt=F32: k.put(f + n, shape, dt)
    sem = lambda n: k.sem(f + n)
    raw = [put(f"raw{s}", [P, KB, P]) for s in range(2)]
    hi = [put(f"w_hi{j}", [P, KB, P], F32R) for j in range(6)]
    lo = [put(f"w_lo{j}", [P, KB, P], F32R) for j in range(6)]
    hid_hi = put("hid_hi", [P, GROUP, TOK], F32R)
    hid_lo = put("hid_lo", [P, GROUP, TOK], F32R)
    act_t = [put(f"act{s}", [P, 512]) for s in range(2)]
    landed = [sem(f"landed{s}") for s in range(2)]
    rounded, split = [sem(f"rounded{s}") for s in range(2)], [sem(f"split{s}") for s in range(2)]
    up_ready = [sem(f"up_ready{b}") for b in range(GROUP)]
    silu_done, prod_done = [sem(f"silu{s}") for s in range(2)], [sem(f"prod{s}") for s in range(2)]
    hid_r, hid_ready = [sem(f"hid_r{s}") for s in range(2)], [sem(f"hid_ready{t}") for t in range(NSP)]
    down_ready, down_evac = sem("down_ready"), [sem(f"down_evac{s}") for s in range(4)]
    zeroed = sem("zeroed")
    w1 = k.d["ffn_w1"][0, which].rearrange("(k p) n -> p k n", p=P)
    w3 = k.d["ffn_w3"][0, which].rearrange("(k p) n -> p k n", p=P)
    w2 = k.d["ffn_w2"][0, which]
    LAST = FF_GROUPS - 1
    with (
        nc.psum_tensor(f + "ps_g", [P, 2, 512], F32) as ps_g,
        nc.psum_tensor(f + "ps_u", [P, 2, 512], F32) as ps_u,
        nc.psum_tensor(f + "ps_d", [P, 4, 512], F32) as ps_d,
        nc.Block() as block,
    ):
        @block.sync
        def _(sp):
            def load(i, first):
                for j in range(6):
                    s, n = j % 2, j // 2
                    if not (first and n == 0):
                        sp.wait_ge(split[s], i * 3 + n)
                    if j < 4:
                        src = (w1, w3)[j % 2][:, :, ds(i * (GROUP * P) + (j // 2) * P, P)]
                        sp.dma_start(raw[s][:], src).then_inc(landed[s], 16)
                    else:
                        src = w2[ds(i * (GROUP * P) + (j - 4) * P, P), :]
                        sp.dma_start(raw[s][:].rearrange("p k n -> p (k n)"), src).then_inc(landed[s], 16)
            load(0, True)
            with sp.Fori(1, FF_GROUPS) as i:
                load(i, False)

        @block.tensor
        def _(pe):
            with pe.Fori(0, FF_GROUPS) as i:
                for b in range(GROUP):
                    for t, (at, n) in enumerate(SPANS):
                        s = (NSP * b + t) % 2
                        pe.wait_ge(prod_done[s], i * 3 + (NSP * b + t) // 2 + 1)
                        for ps, j in ((ps_g, 2 * b), (ps_u, 2 * b + 1)):
                            pe.wait_ge(split[j % 2], i * 3 + j // 2 + 1)
                            for kk in range(KB):
                                mm = product3(pe, ps[:, s, 0:n], hi[j][:, kk], lo[j][:, kk],
                                              k.h_hi[:, kk, at:at + n], k.h_lo[:, kk, at:at + n], kk == 0, kk == KB - 1)
                        mm.then_inc(up_ready[b], 1)
                for j in (4, 5):
                    pe.wait_ge(split[j % 2], i * 3 + 3)
                for t, (at, n) in enumerate(SPANS):
                    pe.wait_ge(hid_ready[t], i * GROUP + GROUP + 1)
                    for m in range(KB):
                        s = m % 4
                        pe.wait_ge(down_evac[s], i * (2 * NSP) + 2 * t + m // 4 + 1)
                        for b in range(GROUP):
                            mm = product3(pe, ps_d[:, s, 0:n], hi[4 + b][:, m], lo[4 + b][:, m],
                                          hid_hi[:, b, at:at + n], hid_lo[:, b, at:at + n], b == 0, b == GROUP - 1)
                        mm.then_inc(down_ready, 1)

        def free_of(eng, i, j):
            if j < 4:
                eng.wait_ge(up_ready[j // 2], i * NSP + NSP)
            else:
                eng.wait_ge(down_ready, i * (NSP * KB) + NSP * KB)

        def split_hi(act, i, j):
            act.wait_ge(landed[j % 2], i * 48 + 16 * (j // 2) + 16)
            act.activation(hi[j][:], raw[j % 2][:], ACT.Copy).then_inc(rounded[j % 2], 1)

        def split_lo(dve, i, j):
            dve.wait_ge(rounded[j % 2], i * 3 + j // 2 + 1)
            dve.tensor_tensor(lo[j][:], raw[j % 2][:], f32(hi[j][:]), ALU.subtract).then_inc(split[j % 2], 1)

        @block.scalar
        def _(act):
            for j in range(6):
                split_hi(act, 0, j)

            def group(i, more):
                for b in range(GROUP):
                    for t, (at, n) in enumerate(SPANS):
                        q = NSP * b + t
                        s = q % 2
                        act.wait_ge(up_ready[b], i * NSP + t + 1)
                        pb, pt = divmod((q - 2) % 6, NSP)
                        act.wait_ge(hid_ready[pt], i * GROUP + (pb + 2 if q >= 2 else 1))
                        act.activation(act_t[s][:, 0:n], ps_g[:, s, 0:n], ACT.Silu).then_inc(silu_done[s], 1)
                        act.wait_ge(prod_done[s], i * 3 + q // 2 + 2)
                        act.activation(hid_hi[:, b, at:at + n], act_t[s][:, 0:n], ACT.Copy).then_inc(hid_r[s], 1)
                    if more:
                        for j in (2 * b, 2 * b + 1):
                            free_of(act, i, j)
                            split_hi(act, i + 1, j)
                if more:
                    for j in (4, 5):
                        free_of(act, i, j)
                        split_hi(act, i + 1, j)
            with act.Fori(0, LAST) as i:
                group(i, True)
            group(LAST, False)

        @block.gpsimd
        def _(pool):
            pool.memset(acc[:], 0.0).then_inc(zeroed, 1)

        @block.vector
        def _(dve):
            for free in prod_done + hid_ready + down_evac:
                dve.sem_inc(free, 1)
            for j in range(6):
                split_lo(dve, 0, j)

            def group(i, more):
                for b in range(GROUP):
                    for t, (at, n) in enumerate(SPANS):
                        q = NSP * b + t
                        s = q % 2
                        dve.wait_ge(silu_done[s], i * 3 + q // 2 + 1)
                        dve.tensor_tensor(act_t[s][:, 0:n], ps_u[:, s, 0:n], act_t[s][:, 0:n],
                                          ALU.mult).then_inc(prod_done[s], 1)
                        dve.wait_ge(hid_r[s], i * 3 + q // 2 + 1)
                        dve.wait_ge(prod_done[s], i * 3 + q // 2 + 2)
                        dve.tensor_tensor(hid_lo[:, b, at:at + n], act_t[s][:, 0:n], f32(hid_hi[:, b, at:at + n]),
                                          ALU.subtract).then_inc(hid_ready[t], 1)
                    if more and b == 0:
                        for j in (0, 1):
                            split_lo(dve, i + 1, j)
                for t, (at, n) in enumerate(SPANS):
                    if more and t == 2:
                        for j in (2, 3):
                            split_lo(dve, i + 1, j)
                    for m in range(KB):
                        dve.wait_ge(down_ready, i * (NSP * KB) + KB * t + m + 1)
                        dve.tensor_tensor(acc[:, m, at:at + n], ps_d[:, m % 4, 0:n], acc[:, m, at:at + n],
                                          ALU.add).then_inc(down_evac[m % 4], 1)
                if more:
                    for j in (4, 5):
                        split_lo(dve, i + 1, j)
            dve.wait_ge(zeroed, 1)
            with dve.Fori(0, LAST) as i:
                group(i, True)
            group(LAST, False)
            for s in range(4):
                dve.wait_ge(down_evac[s], FF_GROUPS * 2 * NSP + 1)


def turn_stage(nc, k, proj, b):
    sem = lambda n: k.sem("t_" + n)
    tabs_in, turned, evac = sem("tabs_in"), sem("turned"), [sem(f"evac{s}") for s in range(4)]
    shuffled, rotated, stored, pads = sem("shuffled"), sem("rotated"), sem("stored"), sem("pads")
    tile = lambda t: slice(t * P, (t + 1) * P)
    groups = [([b.kc_rows[:, a, :] for a in range(2)], b.kc_t[:].rearrange("p (a t) -> p a t", a=2)),
              ([proj[:, B_K, tile(t)] for t in range(2)], b.k_new[:])]
    for t in range(TILES):
        groups.append(([proj[:, B_V, tile(t)]], proj[:, B_V:B_V + 1, tile(t)]))
        groups.append(([proj[:, B_GK + p, tile(t)] for p in range(2)],
                       b.gk_rows[:, t, :].rearrange("p (a f) -> p a f", a=2)))
        groups.append(([proj[:, B_GV + h, tile(t)] for h in range(GH)], proj[:, B_GV:B_GV + GH, tile(t)]))
    n_on = [sum(1 for g in range(len(groups)) if g % 4 == s) for s in range(4)]
    LOADS = 9
    with nc.psum_tensor("t_ps", [P, 4, 512], F32) as ps, nc.Block() as block:
        @block.sync
        def _(sp):
            d = k.d
            for dst, src in ((b.rope[:], d["const_rope"]), (b.mask[:], d["const_mask"]), (b.gla_c[:], d["const_gla"]),
                             (b.kc_rows[:], d["cache_k"][0, 0].rearrange("(a p) g e -> p a (g e)", p=P)),
                             (b.vc[:], d["cache_v"][0, 0].rearrange("(a p) g e -> p a (g e)", p=P)),
                             (b.sink[:], d["attn_sink"][0].partition_broadcast(P)),
                             (b.b_up[:], d["gla_b_up"][0].rearrange("a n -> (a n)").partition_broadcast(P))):
                sp.dma_start(dst, src).then_inc(tabs_in, 16)
            sp.wait_ge(pads, 1)
            for a in range(2):
                sp.dma_start(b.w_up[96 + 16 * a:112 + 16 * a, 256 * a:256 * a + 256], d["gla_w_up"][0, a]).then_inc(tabs_in, 16)
            for g in (1, 2, 5):
                sp.wait_ge(evac[g % 4], g // 4 + 1)
            sp.dma_start(k.o[2][0, 0].rearrange("(a p) g e -> p a (g e)", p=P), b.k_new[:]).then_inc(stored, 16)
            sp.dma_start(k.o[3][0, 0].rearrange("(a p) g e -> p a (g e)", p=P),
                         proj[:, B_V, 0:CTX].rearrange("p (a f) -> p a f", a=2)).then_inc(stored, 16)
            sp.wait_ge(stored, 32)
            sp.wait_ge(tabs_in, 16 * LOADS)

        @block.gpsimd
        def _(pool):
            pool.memset(b.w_up[96:P, :], 0.0).then_inc(pads, 1)
            for n, buf in enumerate(b.kin + b.qp + b.qin):
                pool.wait_ge(pads, n + 1)
                pool.memset(buf[:], 0.0).then_inc(pads, 1)
            pool.wait_ge(pads, 7)

        @block.tensor
        def _(pe):
            pe.wait_ge(tabs_in, 16 * LOADS)
            for g, (srcs, _) in enumerate(groups):
                if g >= 4:
                    pe.wait_ge(evac[g % 4], g // 4)
                for a, src in enumerate(srcs):
                    mm = pe.transpose(ps[:, g % 4, a * P:(a + 1) * P], src, k.ident[:])
                mm.then_inc(turned, 1)

        def read_out(eng, g, op):
            srcs, dst = groups[g]
            eng.wait_ge(turned, g + 1)
            op(dst, ps[:, g % 4, 0:len(srcs) * P].rearrange("p (a f) -> p a f", f=P)).then_inc(evac[g % 4], 1)

        @block.scalar
        def _(act):
            for g in range(len(groups)):
                if g % 4 != 3:
                    read_out(act, g, lambda dst, src: act.activation(dst, src, ACT.Copy))

        @block.vector
        def _(dve):
            dve.wait_ge(tabs_in, 16 * LOADS)
            swap = [(i + 16) % 32 for i in range(32)]
            for q in range(5):
                x = proj[:, q, CTX:TOK]
                dve.stream_shuffle(b.rot[:], x, swap).then_inc(shuffled, 1)
                dve.wait_ge(shuffled, q + 1)
                dve.tensor_tensor(b.rot[:], b.rot[:], b.rope[:, LAT:2 * LAT], ALU.mult).then_inc(rotated, 1)
                dve.tensor_tensor(x, x, b.rope[:, 0:LAT], ALU.mult).then_inc(rotated, 1)
                dve.wait_ge(rotated, 3 * q + 2)
                dve.tensor_tensor(x, x, b.rot[:], ALU.add).then_inc(rotated, 1)
                dve.wait_ge(rotated, 3 * q + 3)
                for g in range(3 + 8 * q, min(3 + 8 * q + 8, len(groups)), 4):
                    read_out(dve, g, dve.tensor_copy)


def attention_stage(nc, k, proj, b):
    sem = lambda n: k.sem("a_" + n)
    (k_hi_done, k_lo_done, q_hi_done, q_lo_done, zeroed, scored, masked, neg_max, exped, sink_exped, den_done, inv_done,
     normed, turned, pt_done, weighted, out_done) = [sem(n) for n in (
         "k_hi", "k_lo", "q_hi", "q_lo", "zeroed", "scored", "masked", "neg_max", "exped", "sink_exped", "den", "inv",
         "normed", "turned", "pt", "weighted", "out")]
    flat = proj[:].rearrange("p b t -> p (b t)")
    units = [(t, q, g) for t in range(TILES) for q in range(4) for g in range(NKV)]
    U, PER = len(units), NQ
    keys = lambda t: CTX if t < CTX_TILES else 3 * P + CTX
    tile = lambda t: slice(t * P, (t + 1) * P)
    half = lambda g: slice(HD * g, HD * (g + 1))
    with (
        nc.psum_tensor("a_s0", [P, 1024], F32) as s0, nc.psum_tensor("a_s1", [P, 1024], F32) as s1,
        nc.psum_tensor("a_t", [P, 1024], F32) as ps_t, nc.psum_tensor("a_v", [P, 2, 512], F32) as ps_v,
        nc.Block() as block,
    ):
        ps_s = [s0, s1]

        @block.gpsimd
        def _(pool):
            n = 0
            for buf in [b.k_hi[:, TOK:TOK + P], b.k_lo[:, TOK:TOK + P]] + [
                    q[:] for part in (b.q_hi, b.q_lo) for ring in part for q in ring]:
                pool.memset(f32(buf), 0.0).then_inc(zeroed, 1)
                n += 1
                pool.wait_ge(zeroed, n)

        @block.tensor
        def _(pe):
            def scores(u):
                t, q, g = units[u]
                if u == 0:
                    pe.wait_ge(k_lo_done, 2)
                if u % PER == 0:
                    pe.wait_ge(q_lo_done, NKV * (t + 1))
                if u >= 2:
                    pe.wait_ge(masked, u - 1)
                spans = [(512, 768, b.k_hi[:, 0:CTX], b.k_lo[:, 0:CTX])] if t < CTX_TILES else [
                    (P, 512, b.k_hi[:, (t - 1) * P:(t + 2) * P], b.k_lo[:, (t - 1) * P:(t + 2) * P]),
                    (512, 768, b.kc_hi[:], b.kc_lo[:])]
                for lo, hi, kh, kl in spans:
                    mm = product3(pe, ps_s[u % 2][:, lo:hi], b.q_hi[t % 2][g][:, q], b.q_lo[t % 2][g][:, q], kh, kl, True, True)
                mm.then_inc(scored, 1)

            def turn(u):
                pe.wait_ge(normed, u + 1)
                if u >= 1:
                    pe.wait_ge(pt_done, u)
                for a in range(keys(units[u][0]) // P):
                    mm = pe.transpose(ps_t[:, tile(a)], b.prob[u % 2][:, tile(a)], k.ident[:])
                mm.then_inc(turned, 1)

            def weigh(u):
                t, q, g = units[u]
                pe.wait_ge(pt_done, u + 1)
                if u % PER == 0 and t >= 2:
                    pe.wait_ge(out_done, t - 1)
                n = keys(t) // P
                for a in range(n):
                    if t < CTX_TILES:
                        v = proj[:, B_V, a * P + g * HD:a * P + (g + 1) * HD]
                    elif a < 3:
                        at = B_V * TOK + (t - 1 + a) * P + g * HD
                        v = flat[:, at:at + HD]
                    else:
                        v = b.vc[:, a - 3, half(g)]
                    mm = pe.matmul(ps_v[half(g), t % 2, tile(q)], v, b.prob_t[u % 2][:, tile(a)], start=a == 0, stop=a == n - 1)
                mm.then_inc(weighted, 1)

            for u in range(U + 3):
                if u < U:
                    scores(u)
                if 2 <= u <= U + 1:
                    turn(u - 2)
                if u >= 3:
                    weigh(u - 3)

        @block.scalar
        def _(act):
            def query_hi(t):
                if t >= 2:
                    act.wait_ge(scored, PER * (t - 1))
                for g in range(NKV):
                    act.activation(b.q_hi[t % 2][g][half(g)], proj[half(g), 0:4, tile(t)], ACT.Copy).then_inc(q_hi_done, 1)

            def exps(u):
                t, q, g = units[u]
                act.wait_ge(neg_max, u + 1)
                if u >= 2:
                    act.wait_ge(turned, u - 1)
                act.activation(b.prob[u % 2][:, 0:keys(t)], b.score[u % 2][:, 0:keys(t)], ACT.Exp, bias=b.negm[:, u:u + 1],
                               accum_out=b.rsum[:, u:u + 1]).then_inc(exped, 1)
                act.activation(b.esink[:, u:u + 1], b.sink[:, q + 4 * g:q + 4 * g + 1], ACT.Exp,
                               bias=b.negm[:, u:u + 1]).then_inc(sink_exped, 1)

            def copy_t(u):
                act.wait_ge(turned, u + 1)
                if u >= 2:
                    act.wait_ge(weighted, u - 1)
                n = keys(units[u][0])
                act.activation(b.prob_t[u % 2][:, 0:n], ps_t[:, 0:n], ACT.Copy).then_inc(pt_done, 1)

            act.activation(b.k_hi[:, 0:TOK], proj[:, B_K], ACT.Copy).then_inc(k_hi_done, 1)
            act.activation(b.kc_hi[:], b.kc_t[:], ACT.Copy).then_inc(k_hi_done, 1)
            act.wait_ge(zeroed, 10)
            query_hi(0)
            for u in range(U + 5):
                if u < U:
                    exps(u)
                if 2 <= u <= U + 1:
                    copy_t(u - 2)
                if u % PER == 3 and u < U and u // PER + 1 < TILES:
                    query_hi(u // PER + 1)
                if u >= 5 and (u - 5) % PER == PER - 1:
                    t = (u - 5) // PER
                    act.wait_ge(weighted, PER * (t + 1))
                    act.activation(proj[:, 0:4, tile(t)], ps_v[:, t % 2].rearrange("p (a f) -> p a f", a=4),
                                   ACT.Copy).then_inc(out_done, 1)

        @block.vector
        def _(dve):
            def query_lo(t):
                for g in range(NKV):
                    dve.wait_ge(q_hi_done, NKV * t + g + 1)
                    dve.tensor_tensor(b.q_lo[t % 2][g][half(g)], proj[half(g), 0:4, tile(t)], f32(b.q_hi[t % 2][g][half(g)]),
                                      ALU.subtract).then_inc(q_lo_done, 1)

            def mask(u):
                t, q, g = units[u]
                lo = 512 if t < CTX_TILES else P
                kind = 0 if t == CTX_TILES else 2 if t == TILES - 1 else 1
                at = kind * (3 * P + CTX) + (3 * P if t < CTX_TILES else 0)
                dve.wait_ge(scored, u + 1)
                if u >= 2:
                    dve.wait_ge(exped, u - 1)
                dve.tensor_tensor_reduce(b.score[u % 2][:, 0:keys(t)], ps_s[u % 2][:, lo:768], b.mask[:, at:at + keys(t)],
                                         HD ** -0.5, -3.0e38, ALU.add, ALU.max, b.rmax[:, u:u + 1]).then_inc(masked, 1)
                dve.wait_ge(masked, u + 1)
                dve.tensor_scalar(b.negm[:, u:u + 1], b.rmax[:, u:u + 1], b.sink[:, q + 4 * g:q + 4 * g + 1], -1.0,
                                  ALU.max, ALU.mult).then_inc(neg_max, 1)

            def norm(u):
                n = keys(units[u][0])
                dve.wait_ge(sink_exped, u + 1)
                dve.tensor_tensor(b.den[:, u:u + 1], b.rsum[:, u:u + 1], b.esink[:, u:u + 1], ALU.add).then_inc(den_done, 1)
                dve.wait_ge(den_done, u + 1)
                dve.reciprocal(b.inv[:, u:u + 1], b.den[:, u:u + 1]).then_inc(inv_done, 1)
                dve.wait_ge(inv_done, u + 1)
                dve.tensor_scalar(b.prob[u % 2][:, 0:n], b.prob[u % 2][:, 0:n], b.inv[:, u:u + 1], None,
                                  ALU.mult).then_inc(normed, 1)

            dve.wait_ge(k_hi_done, 2)
            dve.tensor_tensor(b.k_lo[:, 0:TOK], proj[:, B_K], f32(b.k_hi[:, 0:TOK]), ALU.subtract).then_inc(k_lo_done, 1)
            dve.tensor_tensor(b.kc_lo[:], b.kc_t[:], f32(b.kc_hi[:]), ALU.subtract).then_inc(k_lo_done, 1)
            query_lo(0)
            for u in range(U + 1):
                if u < U:
                    mask(u)
                if u >= 1:
                    norm(u - 1)
                if u % PER == 4 and u // PER + 1 < TILES and u < U:
                    query_lo(u // PER + 1)


def gla_stage(nc, k, proj, b):
    sem = lambda n: k.sem("g_" + n)
    (z_ready, z_sum, z_neg, z_exp, ln_ready, la_ready, b_ready, half_done, rel_done, ex_ready, qk_done, kin_done,
     qin_done, s_ready, kv_ready, at_ready, st_ready, o_ready, st_in) = [sem(n) for n in (
         "z_ready", "z_sum", "z_neg", "z_exp", "ln_ready", "la_ready", "b_ready", "half", "rel", "ex_ready", "qk",
         "kin", "qin", "s_ready", "kv_ready", "at_ready", "st_ready", "o_ready", "st_in")]
    o_used = [sem("o_used0"), sem("o_used1")]
    zeroed, st_out = sem("zeroed"), sem("st_out")
    order = [(0, t) for t in range(TILES)] + [(1, t) for t in (1, 0)] + [(1, t) for t in range(TILES - 1, CTX_TILES - 1, -1)]
    U = len(order)
    starts = {0: b.zero, CTX_TILES: b.s_in[0], TILES: b.zero, TILES + CTX_TILES: b.s_in[1]}
    ends = {CTX_TILES - 1: b.s_end[0], TILES + CTX_TILES - 1: b.s_end[1], TILES - 1: b.s_junk, U - 1: b.s_junk}
    tile = lambda t: slice(t * P, (t + 1) * P)
    steps = 2 * CPT
    last_col = lambda dr: GLA_C - 1 if dr == 0 else 0
    chunks = lambda dr: range(CPT) if dr == 0 else range(CPT - 1, -1, -1)

    def state(n, i):
        if i == CPT:
            return ends[n] if n in ends else b.state[(n + 1) % 2][:, 0]
        return starts[n] if i == 0 and n in starts else b.state[n % 2][:, i]

    with (
        nc.psum_tensor("g_z", [P, 512], F32) as ps_z, nc.psum_tensor("g_b", [P, 512], F32) as ps_b,
        nc.psum_tensor("g_s", [P, 512], F32) as ps_s, nc.psum_tensor("g_o", [P, 2, 512], F32) as ps_o,
        nc.psum_tensor("g_kv", [P, CPT, 2, P], F32) as ps_kv, nc.Block() as block,
    ):
        decay = ps_b[:, 0:2 * P].rearrange("p (a t) -> p a t", a=2)
        rest = ps_b[:, 2 * P:4 * P]

        @block.sync
        def _(sp):
            for dr, name in ((0, "state_gla_fwd"), (1, "state_gla_bwd")):
                for a in range(2):
                    sp.dma_start(b.s_in[dr][a * DK:(a + 1) * DK], k.d[name][0, 0, a::2].rearrange("q e v -> e q v")).then_inc(st_in, 16)
            for dr, n in ((0, CTX_TILES - 1), (1, TILES + CTX_TILES - 1)):
                sp.wait_ge(st_ready, steps * (n + 1))
                for a in range(2):
                    sp.dma_start(k.o[4 + dr][0, 0, a::2].rearrange("q e v -> e q v"),
                                 b.s_end[dr][a * DK:(a + 1) * DK]).then_inc(st_out, 16)
            sp.wait_ge(st_out, 64)

        @block.gpsimd
        def _(pool):
            pool.memset(b.zero[:], 0.0).then_inc(zeroed, 1)

        @block.tensor
        def _(pe):
            def gates(n):
                dr, t = order[n]
                if n >= 1:
                    pe.wait_ge(z_sum, n)
                pe.matmul(ps_z[:, 0:256], proj[96:P, B_LR, tile(t)], b.w_up[96:P, dr * 256:dr * 256 + 256],
                          start=True, stop=True).then_inc(z_ready, 1)

            def sums(n):
                dr, t = order[n]
                pe.wait_ge(la_ready, n + 1)
                if n >= 1:
                    pe.wait_ge(ex_ready, 4 * n)
                for a in range(2):
                    pe.matmul(decay[:, a], b.la[n % 2][:, tile(a)], b.gla_c[:, tile(3 * dr)], start=True, stop=True)
                pe.matmul(rest, b.gla_c[:, tile(3 * dr + 1)], b.la[n % 2][:], start=True, stop=True).then_inc(b_ready, 1)

            def scores(n):
                pe.wait_ge(qk_done, 3 * n + 3)
                if n >= 1:
                    pe.wait_ge(at_ready, n)
                for a in range(2):
                    mm = pe.matmul(ps_s[:, 256 * a:256 * a + 256], b.kp[n % 2][:, a], b.qp[n % 2][:, a], start=True, stop=True)
                mm.then_inc(s_ready, 1)

            def outer(n):
                dr, t = order[n]
                pe.wait_ge(kin_done, CPT * (n + 1))
                if n >= 1:
                    pe.wait_ge(st_ready, steps * n)
                for c in chunks(dr):
                    for h in range(GH):
                        mm = pe.matmul(ps_kv[DK * (h % 2):DK * (h % 2) + DK, c, h // 2, :], b.kin[n % 2][:, c, h * DK:(h + 1) * DK],
                                       proj[:, B_GV + h, tile(t)], start=True, stop=True)
                mm.then_inc(kv_ready, 1)

            def outputs(n):
                dr, t = order[n]
                pe.wait_ge(at_ready, n + 1)
                if n >= 2:
                    m = n - 2
                    pe.wait_ge(o_used[m // TILES], m % TILES + 1)
                for h in range(GH):
                    pe.matmul(ps_o[:, n % 2, tile(h)], b.at[:, h], proj[:, B_GV + h, tile(t)], start=h == 0, stop=False,
                              skip_group_check=True)
                pe.wait_ge(qin_done, 2 * (n + 1))
                if n == 0:
                    pe.wait_ge(zeroed, 1)
                    pe.wait_ge(st_in, 64)
                for i, c in enumerate(chunks(dr)):
                    cc = slice(c * GLA_C, (c + 1) * GLA_C)
                    if steps * n + 2 * i:
                        pe.wait_ge(st_ready, steps * n + 2 * i)
                    for h in range(GH):
                        mm = pe.matmul(ps_o[cc, n % 2, tile(h)], b.qin[n % 2][:, h // 2, h % 2, cc], state(n, i)[:, h // 2],
                                       start=False, stop=i == CPT - 1, skip_group_check=True)
                mm.then_inc(o_ready, 1)

            for n in range(-2, U):
                if n >= 0:
                    scores(n)
                if 0 <= n + 1 < U:
                    sums(n + 1)
                if n + 2 < U:
                    gates(n + 2)
                if n >= 0:
                    outer(n)
                    outputs(n)

        @block.scalar
        def _(act):
            def factors(n):
                act.wait_ge(rel_done, n + 1)
                if n >= 2:
                    act.wait_ge(st_ready, steps * (n - 1))
                if n >= 1:
                    act.wait_ge(kin_done, CPT * n)
                    act.wait_ge(qin_done, 2 * n)
                act.activation(b.ep[:], b.rel[:], ACT.Exp).then_inc(ex_ready, 1)
                act.activation(b.en[:], b.rel[:], ACT.Exp, scale=-1.0).then_inc(ex_ready, 1)
                act.activation(b.er[:], rest, ACT.Exp).then_inc(ex_ready, 1)
                act.activation(b.eb[n % 2][:], decay, ACT.Exp).then_inc(ex_ready, 1)

            def log_sum(n):
                act.wait_ge(z_neg, n + 1)
                act.activation(b.ze[:], b.zn[:], ACT.Exp).then_inc(z_exp, 1)
                act.wait_ge(z_exp, n + 1)
                if n >= 1:
                    act.wait_ge(la_ready, n)
                act.activation(b.zl[:], b.ze[:], ACT.Ln, bias=1.0).then_inc(ln_ready, 1)

            def collect(n):
                act.wait_ge(o_ready, n + 1)
                act.activation(b.o_rows[:, order[n][1]], ps_o[:, n % 2], ACT.Copy).then_inc(o_used[0], 1)

            for n in range(-2, U):
                if 0 <= n + 1 < U:
                    factors(n + 1)
                if n + 2 < U:
                    log_sum(n + 2)
                if n >= 1 and order[n - 1][0] == 0:
                    collect(n - 1)

        @block.vector
        def _(dve):
            def gate_in(n):
                dr, t = order[n]
                dve.wait_ge(z_ready, n + 1)
                if n >= 1:
                    dve.wait_ge(la_ready, n)
                dve.tensor_tensor(b.z[:], ps_z[:, 0:256], b.b_up[:, dr * 256:dr * 256 + 256], ALU.add).then_inc(z_sum, 1)
                dve.wait_ge(z_sum, n + 1)
                if n >= 1:
                    dve.wait_ge(z_exp, n)
                dve.scalar_tensor_tensor(out=b.zn[:], in0=b.z[:], scalar=-1.0, in1=b.z[:], op0=ALU.mult, op1=ALU.min).then_inc(z_neg, 1)

            def log_gate(n):
                dve.wait_ge(ln_ready, n + 1)
                dve.scalar_tensor_tensor(out=b.la[n % 2][:], in0=b.z[:], scalar=0.0, in1=b.zl[:], op0=ALU.min,
                                         op1=ALU.subtract).then_inc(la_ready, 1)

            def relative(n):
                dr, t = order[n]
                dve.wait_ge(b_ready, n + 1)
                chunked = decay.rearrange("p a (c t) -> p a c t", t=GLA_C)
                if n >= 1:
                    dve.wait_ge(rel_done, n)
                dve.tensor_scalar(b.half[:], chunked[:, :, :, last_col(dr)], 0.5, None, ALU.mult).then_inc(half_done, 1)
                dve.wait_ge(half_done, n + 1)
                if n >= 1:
                    dve.wait_ge(ex_ready, 4 * n)
                dve.tensor_tensor(b.rel[:].rearrange("p a (c t) -> p a c t", t=GLA_C), chunked,
                                  b.half[:].unsqueeze(3).broadcast_to([P, 2, CPT, GLA_C]), ALU.subtract).then_inc(rel_done, 1)

            def scaled(n, src, factor, dst, done):
                for g in range(2):
                    rows = slice(DK * g, DK * (g + 1))
                    dve.scalar_tensor_tensor(out=dst[rows, :, g], in0=src[rows], scalar=DK ** -0.5, in1=factor[rows],
                                             op0=ALU.mult, op1=ALU.mult).then_inc(done, 1)

            def score_factors(n):
                t = order[n][1]
                dve.wait_ge(ex_ready, 4 * n + 2)
                scaled(n, proj[:, B_GQ:B_GQ + 2, tile(t)], b.ep, b.qp[n % 2], qk_done)
                dve.tensor_tensor(b.kp[n % 2][:], proj[:, B_GK:B_GK + 2, tile(t)], b.en[:], ALU.mult).then_inc(qk_done, 1)

            def state_factors(n):
                t = order[n][1]
                dve.wait_ge(ex_ready, 4 * n + 4)
                for c in range(CPT):
                    rows = slice(c * GLA_C, (c + 1) * GLA_C)
                    dve.tensor_tensor(b.kin[n % 2][rows, c], b.gk_rows[rows, t], b.er[rows], ALU.mult).then_inc(kin_done, 1)
                scaled(n, proj[:, B_GQ:B_GQ + 2, tile(t)], b.eb[n % 2], b.qin[n % 2], qin_done)

            def mask(n):
                dr, t = order[n]
                dve.wait_ge(s_ready, n + 1)
                m = b.gla_c[:, tile(3 * dr + 2)]
                dve.tensor_tensor(b.at[:], ps_s[:].rearrange("p (a t) -> p a t", a=GH), m.unsqueeze(1).broadcast_to([P, GH, P]),
                                  ALU.mult).then_inc(at_ready, 1)

            def chain(n):
                dr, t = order[n]
                if n == 0:
                    dve.wait_ge(zeroed, 1)
                dve.wait_ge(kv_ready, n + 1)
                for i, c in enumerate(chunks(dr)):
                    if i or n:
                        dve.wait_ge(st_ready, steps * n + 2 * i)
                    last = c * GLA_C + last_col(dr)
                    for a in range(2):
                        dve.scalar_tensor_tensor(out=state(n, i + 1)[:, a], in0=state(n, i)[:, a],
                                                 scalar=b.eb[n % 2][:, a, last:last + 1], in1=ps_kv[:, c, a],
                                                 op0=ALU.mult, op1=ALU.add).then_inc(st_ready, 1)

            def collect(n):
                dve.wait_ge(o_ready, n + 1)
                dst = b.o_rows[:, order[n][1]]
                dve.tensor_tensor(dst, ps_o[:, n % 2], dst, ALU.add).then_inc(o_used[1], 1)

            dve.wait_ge(st_in, 64)
            for n in range(-2, U):
                if n >= 0:
                    mask(n)
                if 0 <= n + 1 < U:
                    relative(n + 1)
                if n + 2 < U:
                    gate_in(n + 2)
                if 0 <= n + 1 < U:
                    score_factors(n + 1)
                if n + 2 < U:
                    log_gate(n + 2)
                if n >= 0:
                    chain(n)
                if 0 <= n + 1 < U:
                    state_factors(n + 1)
                if n >= 1 and order[n - 1][0] == 1:
                    dve.wait_ge(o_used[0], TILES)
                    collect(n - 1)
            collect(U - 1)


def gla_out_stage(nc, k, proj, b):
    sem = lambda n: k.sem("e_" + n)
    sq_done, var_done, std_done, inv_done, normed, turned, evac, silu_done, w_in = [sem(n) for n in (
        "sq_done", "var_done", "std_done", "inv_done", "normed", "turned", "evac", "silu_done", "w_in")]
    tile = lambda t: slice(t * P, (t + 1) * P)
    with nc.psum_tensor("e_ps", [P, 2, 512], F32) as ps, nc.Block() as block:
        @block.sync
        def _(sp):
            with nc.allow_non_contiguous_dma(reason="one column of 128 values"):
                sp.dma_start(b.nw[:], k.d["gla_norm"].rearrange("a v -> v a")).then_inc(w_in, 16)

        @block.scalar
        def _(act):
            for t in range(TILES):
                for h in range(GH):
                    n = t * GH + h
                    if n >= 4:
                        act.wait_ge(sq_done, n - 3)
                    act.activation(b.junk[:, n % 4], b.o_rows[:, t, h * DV:(h + 1) * DV], ACT.Square,
                                   accum_out=b.var[:, t * GH + h:t * GH + h + 1]).then_inc(sq_done, 1)
            act.wait_ge(sq_done, TILES * GH)
            act.activation(b.std[:], b.var[:], ACT.Sqrt, bias=k.eps[:], scale=1.0 / DV).then_inc(std_done, 1)
            for h in range(GH):
                act.activation(proj[:, B_GG + h], proj[:, B_GG + h], ACT.Silu).then_inc(silu_done, 1)

        @block.vector
        def _(dve):
            dve.wait_ge(std_done, 1)
            dve.reciprocal(b.istd[:], b.std[:]).then_inc(inv_done, 1)
            dve.wait_ge(inv_done, 1)
            for t in range(TILES):
                o = b.o_rows[:, t].rearrange("p (h v) -> p h v", h=GH)
                dve.tensor_tensor(o, o, b.istd[:, t * GH:(t + 1) * GH].unsqueeze(2).broadcast_to([P, GH, DV]),
                                  ALU.mult).then_inc(normed, 1)
            dve.wait_ge(silu_done, GH)
            dve.wait_ge(w_in, 16)
            for t in range(TILES):
                dve.wait_ge(turned, t + 1)
                g = proj[:, B_GG:B_GG + GH, tile(t)]
                dve.scalar_tensor_tensor(out=g, in0=ps[:, t % 2].rearrange("p (h t) -> p h t", h=GH), scalar=b.nw[:, 0:1],
                                         in1=g, op0=ALU.mult, op1=ALU.mult).then_inc(evac, 1)

        @block.tensor
        def _(pe):
            for t in range(TILES):
                pe.wait_ge(normed, t + 1)
                if t >= 2:
                    pe.wait_ge(evac, t - 1)
                for h in range(GH):
                    mm = pe.transpose(ps[:, t % 2, h * P:(h + 1) * P], b.o_rows[:, t, h * DV:(h + 1) * DV], k.ident[:])
                mm.then_inc(turned, 1)


def mix_split_stage(nc, k, proj):
    rounded, split = k.sem("m_rounded"), k.sem("m_split")
    src = [0, 1, 2, 3] + [B_GG + h for h in range(GH)]
    with nc.Block() as block:
        @block.scalar
        def _(act):
            for j, q in enumerate(src):
                act.activation(k.h_hi[:, j], proj[:, q], ACT.Copy).then_inc(rounded, 1)

        @block.vector
        def _(dve):
            for j, q in enumerate(src):
                dve.wait_ge(rounded, j + 1)
                dve.tensor_tensor(k.h_lo[:, j], proj[:, q], f32(k.h_hi[:, j]), ALU.subtract).then_inc(split, 1)
            dve.wait_ge(split, len(src))


class MixerBuffers:

    def __init__(self, k):
        k.at = k.hi_at
        put = lambda name, shape, dt=F32: k.put("x_" + name, shape, dt)
        self.kc_rows, self.vc, self.k_new = put("kc_rows", [P, 2, P]), put("vc", [P, 2, P]), put("k_new", [P, 2, P])
        self.kc_t = put("kc_t", [P, CTX])
        self.sink, self.b_up, self.w_up = put("sink", [P, NQ]), put("b_up", [P, 512]), put("w_up", [P, 512])
        self.gk_rows = put("gk_rows", [P, TILES, 2 * P])
        self.gla_c = put("gla_c", [P, 6 * P])
        shared = k.at
        self.mask = put("mask", [P, 3 * (3 * P + CTX)])
        tables = k.at
        self.rope, self.rot = put("rope", [P, 2 * LAT]), put("rot", [P, LAT])
        k.at = tables
        self.score = [put(f"score{s}", [P, 3 * P + CTX]) for s in range(2)]
        self.prob = [put(f"prob{s}", [P, 3 * P + CTX]) for s in range(2)]
        self.prob_t = [put(f"prob_t{s}", [P, 3 * P + CTX]) for s in range(2)]
        self.k_hi, self.k_lo = [put(n, [P, TOK + P], F32R) for n in ("k_hi", "k_lo")]
        self.kc_hi, self.kc_lo = [put(n, [P, CTX], F32R) for n in ("kc_hi", "kc_lo")]
        self.q_hi, self.q_lo = [[[put(f"{n}{s}{g}", [P, 4, P], F32R) for g in range(NKV)] for s in range(2)]
                                for n in ("q_hi", "q_lo")]
        self.rmax, self.negm, self.rsum, self.esink, self.den, self.inv = [
            put(n, [P, TILES * NQ]) for n in ("rmax", "negm", "rsum", "esink", "den", "inv")]
        assert k.at <= k.rest
        k.at = shared
        self.o_rows = put("o_rows", [P, TILES, GH * DV])
        self.z, self.zn, self.ze, self.zl, self.er = [put(n, [P, 256]) for n in ("z", "zn", "ze", "zl", "er")]
        self.la = [put(f"la{s}", [P, 256]) for s in range(2)]
        self.ep, self.en, self.rel = [put(n, [P, 2, P]) for n in ("ep", "en", "rel")]
        self.eb, self.kp = [[put(f"{n}{s}", [P, 2, P]) for s in range(2)] for n in ("eb", "kp")]
        self.half = put("half", [P, 2, CPT])
        self.at = put("at", [P, GH, P])
        self.state = [put(f"state{s}", [P, CPT, 2, DV]) for s in range(2)]
        self.s_in, self.s_end = [[put(f"{n}{s}", [P, 2, DV]) for s in range(2)] for n in ("s_in", "s_end")]
        self.zero, self.s_junk = put("zero", [P, 2, DV]), put("s_junk", [P, 2, DV])
        self.junk, self.nw = put("junk", [P, 4, DV]), put("nw", [P, 1])
        self.var, self.std, self.istd = [put(n, [P, TILES * GH]) for n in ("var", "std", "istd")]
        assert k.at <= k.rest
        k.at = k.rest + 4 * PROJB * TOK
        self.kin = [put(f"kin{s}", [P, CPT, GH * DK]) for s in range(2)]
        self.qp, self.qin = [[put(f"{n}{s}", [P, 2, 2, P]) for s in range(2)] for n in ("qp", "qin")]


def mixer(nc, k):
    k.at = k.rest
    proj = k.put("proj", [P, PROJB, TOK])
    w_in = k.d["w_in"][0].rearrange("(k p) n -> p k n", p=P)

    def heads(i, b):
        return [(lambda r, q=q: r[:, :, q * HD:(q + 1) * HD], w_in[:, :, 64 * (2 * i + b) + 256 * q:64 * (2 * i + b) + 256 * q + 64])
                for q in range(2)]

    def plain(i, b):
        return k_halves(w_in, i * (2 * P) + b * P)

    gemm_stage(nc, k, "wi", [((0, 2), heads), ((2, 9), plain)], k_halves(w_in, IN_W - P), 18, proj)
    b = MixerBuffers(k)
    turn_stage(nc, k, proj, b)
    attention_stage(nc, k, proj, b)
    gla_stage(nc, k, proj, b)
    gla_out_stage(nc, k, proj, b)
    mix_split_stage(nc, k, proj)


def k_halves(w, col):
    h = KB // 2
    return [(lambda r, q=q: r[:, q * h:(q + 1) * h, :], w[:, q * h:(q + 1) * h, ds(col, P)]) for q in range(2)]


def layer(nc, d, o):
    k = Core(nc, d, o)
    ACC = 4 * KB * TOK

    def accumulator(n):
        k.at = k.rest
        return k.put(f"acc{n}", [P, KB, TOK])

    modulation_stage(nc, k)
    k.at = k.rest
    norm_stage(nc, k, None, 0, None)
    acc = accumulator(0)
    ffn_stage(nc, k, 0, acc)
    k.at = k.rest + ACC
    norm_stage(nc, k, 0, 1, acc)
    mixer(nc, k)
    k.recycle()
    acc = accumulator(1)
    w_out = d["w_out"][0]

    def mixed(i, b):
        col = ds(i * (2 * P) + b * P, P)
        heads = [(lambda r, g=g: r[HD * g:HD * (g + 1), 0:4, :],
                  w_out[256 * g:256 * (g + 1), col].rearrange("(k p) n -> p k n", p=HD)) for g in range(NKV)]
        return heads + [(lambda r: r[:, 4:8, :], w_out[512:1024, col].rearrange("(k p) n -> p k n", p=P))]

    gemm_stage(nc, k, "wo", [((0, KB // 2), mixed)], None, KB, acc, parts=3)
    k.at = k.rest + ACC
    norm_stage(nc, k, 1, 2, acc)
    acc = accumulator(2)
    ffn_stage(nc, k, 1, acc)
    k.at = k.rest + ACC
    norm_stage(nc, k, 2, None, acc)


_INS = ["x_prompt", "x_sample", "cache_k", "cache_v", "state_gla_fwd", "state_gla_bwd", "c", "c_ctx", "w_ada", "b_ada",
        "norm_pre", "norm_post", "ffn_w1", "ffn_w3", "ffn_w2", "w_in", "gla_w_up", "gla_b_up", "gla_norm", "attn_sink",
        "w_out"]
_OUTS = [(1, CTX, D), (1, LAT, D), (1, 1, CTX, NKV, HD), (1, 1, CTX, NKV, HD), (1, 1, GH, DK, DV), (1, 1, GH, DK, DV)]


def kernel(**inputs):
    import concourse.bacc as bacc
    from concourse.bass_utils import run_bass_kernel_spmd

    nc = bacc.Bacc("TRN2", target_bir_lowering=False, num_devices=1)
    arrays = {name: np.ascontiguousarray(inputs[name]) for name in _INS}
    arrays.update(shape_constants())
    d = {name: nc.dram_tensor(f"in_{name}", a.shape, mybir.dt.from_np(a.dtype), kind="ExternalInput").ap()
         for name, a in arrays.items()}
    o = [nc.dram_tensor(f"out_{i}", shape, F32, kind="ExternalOutput").ap() for i, shape in enumerate(_OUTS)]
    layer(nc, d, o)
    r = run_bass_kernel_spmd(nc, [{f"in_{name}": a for name, a in arrays.items()}], core_ids=[0])
    return tuple(r.results[0][f"out_{i}"] for i in range(len(_OUTS)))
```

```python
import numpy as np
import concourse.bass as bass
from concourse import mybir

F32 = mybir.dt.float32
F32R = mybir.dt.float32r
ALU = mybir.AluOpType
ACT = mybir.ActivationFunctionType
AX_X = mybir.AxisListType.X
ds = bass.ds

P = 128
D = 1024
KB = D // P
CTX, LAT = 256, 1024
TOK = CTX + LAT
TILES = TOK // P
CTX_TILES = CTX // P
FF = 2816
FFB = FF // P
GROUP = 2
FF_GROUPS = FFB // GROUP
N_MOD = 9
MODB = N_MOD * KB
SPANS = [(0, 512), (512, 512), (1024, 256)]
NSP = len(SPANS)
CH = 256
NCH = TOK // CH
EPS = 1e-6
NEG = -1e30
GRID_W = 64
HD = 64
NQ, NKV = 8, 2
GLA_C = 32
CPT = P // GLA_C
GH, DK, DV = 4, 64, 128
IN_W = 2336
B_Q, B_K, B_V, B_GQ, B_GK, B_GV, B_GG, B_LR = 0, 4, 5, 6, 8, 10, 14, 18
PROJB = 19


def shape_constants():
    ident = np.eye(P, dtype=np.float32)
    ones = np.full((P, P), 1.0 / D, np.float32)
    t = np.arange(LAT)
    half = HD // 2
    inv = (10000.0 ** (-np.arange(0, half, 2, dtype=np.float32) / np.float32(half))).astype(np.float32)
    p = np.arange(P)
    in_col = (p % HD) >= half
    freq = inv[p % (half // 2)]
    pos = np.where(in_col[:, None], (t % GRID_W)[None], (t // GRID_W)[None]).astype(np.float32)
    ang = (pos * freq[:, None]).astype(np.float32)
    cos = np.cos(ang).astype(np.float32)
    sin = np.sin(ang).astype(np.float32) * np.where((p % half) < half // 2, -1, 1)[:, None]
    r = np.arange(P)[:, None]
    j = np.arange(3 * P)[None]
    win = np.where(np.abs(j - P - r) <= P, 0.0, NEG).astype(np.float32)
    masks = []
    for first, last in ((True, False), (False, False), (False, True)):
        m = np.zeros((P, 3 * P + CTX), np.float32)
        m[:, :3 * P] = win
        if first:
            m[:, :P] = NEG
        if last:
            m[:, 2 * P:3 * P] = NEG
        masks.append(m)
    s, q = np.arange(P)[:, None], np.arange(P)[None]
    same = (s // GLA_C) == (q // GLA_C)
    tau = 1.0 / 16.0
    gla = []
    for incl, rest in ((s <= q, s > q), (s >= q, s < q)):
        gla += [np.where(same & incl, tau, 0.0), np.where(same & rest, tau, 0.0), np.where(same & incl, 1.0, 0.0)]
    return {
        "const_ident": ident, "const_sel": (np.arange(P)[:, None] % 32 == np.arange(2)[None]).astype(np.float32), "const_mean": ones,
        "const_rope": np.concatenate([cos, sin], 1).astype(np.float32),
        "const_mask": np.concatenate(masks, 1).astype(np.float32),
        "const_gla": np.concatenate(gla, 1).astype(np.float32),
    }


class Core:

    def __init__(self, nc, d, o):
        self.nc, self.d, self.o = nc, d, o
        self.live = []
        self.base = -(-nc.sbuf_base // 64) * 64
        self.end = nc.sbuf_usable_end
        self.at = self.base
        put = self.put
        self.ident = put("ident", [P, P])
        self.mean = put("mean", [P, P])
        self.mod = put("mod", [P, MODB, 2])
        self.vec = put("vec", [P, MODB + 48])
        self.pre = put("pre", [P, 3, KB, 2])
        self.gate = put("gate", [P, 3, KB, 2])
        self.eps = put("eps", [P, 1])
        self.cond = put("cond", [P, KB, 32])
        self.sel = put("sel", [P, 2])
        top = self.at
        self.at = self.top = (self.end - (2 + 4) * 4 * KB * P) // 64 * 64
        self.raw = [put(f"raw{s}", [P, KB, P]) for s in range(2)]
        self.w_hi, self.w_lo = [[put(f"{n}{s}", [P, KB, P], F32R) for s in range(2)] for n in ("w_hi", "w_lo")]
        self.at = self.hi_at = top
        self.h_hi = put("h_hi", [P, KB, TOK], F32R)
        self.h_lo = put("h_lo", [P, KB, TOK], F32R)
        self.rest = self.at
        self.x_t = nc.dram_tensor("x_t", [P, KB, TOK], F32, kind="Internal").ap()

    def put(self, name, shape, dt=F32):
        n = -(-int(np.prod(shape[1:])) * 4 // 32) * 32
        assert self.at + n <= self.end, (name, self.at + n - self.end)
        t = self.nc.alloc_sbuf_tensor_at(name, shape, dt, offset=self.at)
        self.at += n
        return t

    def below_weights(self):
        assert self.at <= self.top, self.at - self.top

    def sem(self, name):
        s = self.nc.alloc_semaphore(name)
        self.live.append(s)
        return s

    def recycle(self):
        self.nc.clear_and_free_semaphores(self.live)
        self.nc.all_engine_barrier()
        self.live = []


def f32(ap):
    return ap.bitcast(F32)


def product3(pe, out, w_hi, w_lo, x_hi, x_lo, first, last):
    pe.matmul(out, w_hi, x_hi, start=first, stop=False)
    pe.matmul(out, w_hi, x_lo, start=False, stop=False)
    return pe.matmul(out, w_lo, x_hi, start=False, stop=last)


class FirstWeights:

    def __init__(self, k, name, loads):
        self.k, self.loads = k, loads
        self.landed, self.rounded, self.split = [[k.sem(f"{name}_{n}{s}") for s in range(2)]
                                                 for n in ("landed", "rounded", "split")]

    def load(self, sp, blocks):
        for n in blocks:
            if n >= 2:
                sp.wait_ge(self.split[n % 2], 1)
            for part, src in self.loads[n]:
                sp.dma_start(part(self.k.raw[n % 2]), src).then_inc(self.landed[n % 2], 16)

    def hi(self, act):
        for s in range(2):
            act.wait_ge(self.landed[s], 16 * len(self.loads[s]))
            act.activation(self.k.w_hi[s][:], self.k.raw[s][:], ACT.Copy).then_inc(self.rounded[s], 1)

    def lo(self, eng):
        for s in range(2):
            eng.wait_ge(self.rounded[s], 1)
            eng.tensor_tensor(self.k.w_lo[s][:], self.k.raw[s][:], f32(self.k.w_hi[s][:]), ALU.subtract).then_inc(self.split[s], 1)


class ModUnits:
    WB = 2
    COLT = 4
    SUMS = WB * P

    def __init__(self, k, name, base, count, ring, banks):
        self.k, self.base, self.count, self.ring, self.banks = k, base, count, ring, banks
        self.w = [k.put(f"{name}_w{s}", [P, KB, self.WB * P]) for s in range(ring)]
        self.sums = [k.put(f"{name}_sums{s}", [P, self.WB * P]) for s in range(ring)]
        self.w_in, self.w_used, self.copied, self.added, self.evac = [[k.sem(f"{name}_{n}{s}") for s in range(ring)] for n in (
            "w_in", "w_used", "copied", "added", "evac")]
        self.coef = k.sem(f"{name}_coef")
        self.src = k.d["w_ada"].rearrange("a (k p) n -> (a p) k n", p=P)

    def load(self, sp, u):
        s, n = u % self.ring, u // self.ring
        if n >= 1:
            sp.wait_ge(self.w_used[s], n)
        at = (self.base + u) * self.WB * P
        sp.dma_start(self.w[s][:], self.src[:, :, at:at + self.WB * P]).then_inc(self.w_in[s], 16)

    def products(self, pe, u):
        s, n = u % self.ring, u // self.ring
        pe.wait_ge(self.w_in[s], 16 * (n + 1))
        if n >= 1:
            pe.wait_ge(self.evac[s], n)
        for kk in range(KB):
            c = kk % self.COLT
            mm = pe.matmul(self.banks[s][32 * c:32 * c + 32, 0:self.SUMS], self.k.cond[:, kk], self.w[s][:, kk],
                           start=kk < self.COLT, stop=kk >= KB - self.COLT, skip_group_check=True)
        mm.then_inc(self.w_used[s], 1)

    def copy(self, act, u):
        s, n = u % self.ring, u // self.ring
        act.wait_ge(self.w_used[s], n + 1)
        act.activation(self.sums[s][:], self.banks[s][:, 0:self.SUMS], ACT.Copy).then_inc(self.copied[s], 1)

    def turn(self, pe, u):
        s, n = u % self.ring, u // self.ring
        pe.wait_ge(self.copied[s], n + 1)
        for b in range(self.WB):
            at = self.SUMS + 2 * b
            mm = pe.matmul(self.banks[s][:, at:at + 2], self.sums[s][:, b * P:(b + 1) * P], self.k.sel[:], start=True, stop=True)
        mm.then_inc(self.added[s], 1)

    def add(self, dve, u):
        s, n = u % self.ring, u // self.ring
        dve.wait_ge(self.added[s], n + 1)
        k, at = self.k, (self.base + u) * self.WB
        dve.tensor_tensor(k.mod[:, at:at + self.WB, :],
                          self.banks[s][:, self.SUMS:self.SUMS + 2 * self.WB].rearrange("p (b c) -> p b c", c=2),
                          k.vec[:, at:at + self.WB].unsqueeze(2).broadcast_to([P, self.WB, 2]),
                          ALU.add).then_inc(self.evac[s], 1)

    def all_added(self, dve, units):
        for s in range(self.ring):
            dve.wait_ge(self.evac[s], len(range(s, units, self.ring)))

    def pre(self, dve, i):
        k, shift = self.k, MODB + KB * i
        dve.scalar_tensor_tensor(
            out=k.pre[:, i], in0=k.mod[:, (3 * i + 1) * KB:(3 * i + 2) * KB, :], scalar=1.0,
            in1=k.vec[:, shift:shift + KB].unsqueeze(2).broadcast_to([P, KB, 2]),
            op0=ALU.add, op1=ALU.mult).then_inc(self.coef, 1)

    def gate(self, dve, i):
        k, shift = self.k, MODB + KB * i + 24
        dve.scalar_tensor_tensor(
            out=k.gate[:, i], in0=k.mod[:, (3 * i + 2) * KB:(3 * i + 3) * KB, :], scalar=1.0 if i == 1 else 0.5,
            in1=k.vec[:, shift:shift + KB].unsqueeze(2).broadcast_to([P, KB, 2]),
            op0=ALU.mult, op1=ALU.mult).then_inc(self.coef, 1)


MODS_FIRST = 2 * KB // ModUnits.WB
MODS_NORM0 = 5 * KB // ModUnits.WB


def conditions_stage(nc, k, block, ps_rows):
    k.at = k.hi_at
    rows = k.put("mod_rows", [MODB + 48, P])
    cond_rows = k.put("cond_rows", [2 * KB, P])
    k.at = k.rest
    rows_in, turned, cond_ready, cond_zero, vec_ready = [k.sem(n) for n in (
        "rows_in", "rows_turned", "cond_ready", "cond_zero", "vec_ready")]
    d = k.d

    @block.sync
    def _(sp):
        for dst, src in ((k.ident[:], d["const_ident"]),
                         (rows[0:MODB, :], d["b_ada"].rearrange("a (b p) -> (a b) p", p=P)),
                         (rows[MODB:MODB + 24, :], d["norm_pre"].rearrange("a i (b p) -> (a i b) p", p=P)),
                         (rows[MODB + 24:MODB + 48, :], d["norm_post"].rearrange("a i (b p) -> (a i b) p", p=P)),
                         (cond_rows[0:KB, :], d["c_ctx"].rearrange("(b p) -> b p", p=P)),
                         (cond_rows[KB:2 * KB, :], d["c"].rearrange("a (b p) -> (a b) p", p=P)),
                         (k.sel[:], d["const_sel"]), (k.mean[:], d["const_mean"])):
            sp.dma_start(dst, src).then_inc(rows_in, 16)

    @block.gpsimd
    def _(pool):
        pool.memset(k.cond[:], 0.0).then_inc(cond_zero, 1)

    @block.tensor
    def _(pe):
        pe.wait_ge(rows_in, 16 * 8)
        pe.transpose(ps_rows[:, 0:MODB + 48], rows[:], k.ident[0:MODB + 48, 0:MODB + 48])
        pe.transpose(ps_rows[:, 256:256 + 2 * KB], cond_rows[:], k.ident[0:2 * KB, 0:2 * KB]).then_inc(turned, 1)
        pe.wait_ge(cond_ready, 1)
        pe.wait_ge(vec_ready, 1)

    @block.scalar
    def _(act):
        act.wait_ge(turned, 1)
        act.wait_ge(cond_zero, 1)
        act.activation(k.cond[:, :, 0:2], ps_rows[:, 256:256 + 2 * KB].rearrange("p (c k) -> p k c", c=2),
                       ACT.Silu).then_inc(cond_ready, 1)

    @block.vector
    def _(dve):
        dve.memset(k.eps[:], EPS)
        dve.wait_ge(cond_ready, 1)
        dve.tensor_copy(k.vec[:], ps_rows[:, 0:MODB + 48]).then_inc(vec_ready, 1)
        dve.wait_ge(vec_ready, 1)


class NormDone:

    def __init__(self, h_done, stored, last_mean):
        self.h_done, self.stored, self.last_mean = h_done, stored, last_mean

    def tokens(self, eng, end):
        self.h_done(eng, end // CH)

    def buffers_free(self, eng):
        self.h_done(eng, NCH)
        for s, n in self.stored:
            eng.wait_ge(s, n)


def norm_stage(nc, k, block, i_post, i_pre, acc, ahead=None):
    HALVES = [slice(0, KB // 2), slice(KB // 2, KB)]
    on_vector = lambda n: n >= NCH - 2
    n_ = f"n{0 if i_post is None else i_post + 1}_"
    first, final = i_post is None, i_pre is None
    put = lambda name, shape, dt=F32: k.put(n_ + name, shape, dt)
    sem = lambda name: k.sem(n_ + name)
    XR = 3
    x = [put(f"x{s}", [P, KB, CH]) for s in range(XR)]
    if first or final:
        nat = [put(f"nat{s}", [P, 2, D]) for s in range(2)]
    if not first:
        sq_o = put("sq_o", [P, KB, CH])
    if not final:
        tmp_p = [put(f"tmp_p{s}", [P, KB, CH]) for s in range(2)]
        sq_p = put("sq_p", [P, KB, CH])
    std = put("std", [P, 2, CH])
    rstd = put("rstd", [P, 2, CH])
    x_in = [sem(f"x_in{s}") for s in range(XR)]
    x_out = [sem(f"x_out{s}") for s in range(XR)]
    x_ready = sem("x_ready")
    if not first:
        o_sq, o_mean, o_std, o_rstd, o_scaled = [sem(s) for s in ("o_sq", "o_mean", "o_std", "o_rstd", "o_scaled")]
    if not final:
        p_sq, p_mean, p_std, p_rstd, p_scaled, p_v, p_hi, p_lo, p_lo_v = [sem(s) for s in (
            "p_sq", "p_mean", "p_std", "p_rstd", "p_scaled", "p_v", "p_hi", "p_lo", "p_lo_v")]
    if first or final:
        turned, evac = sem("turned"), sem("evac")
    d, o = k.d, k.o
    x_rows = [d["x_prompt"][0].rearrange("(a p) f -> p a f", p=P)] + [
        d["x_sample"][0, CH * n:CH * (n + 1)].rearrange("(a p) f -> p a f", p=P) for n in range(NCH - 1)]
    y_rows = [o[0][0].rearrange("(a p) f -> p a f", p=P)] + [
        o[1][0, CH * n:CH * (n + 1)].rearrange("(a p) f -> p a f", p=P) for n in range(NCH - 1)]
    chunk = lambda n: slice(n * CH, (n + 1) * CH)
    cond = lambda n: 0 if n == 0 else 1
    uses = lambda s, ring: len(range(s, NCH, ring))
    with (
        nc.psum_tensor(n_ + "ps_x", [P, KB, CH], F32) as ps_x,
        nc.psum_tensor(n_ + "ps_m", [P, 2, 512], F32) as ps_m,
        nc.psum_tensor(n_ + "ps_o", [P, 512], F32) as ps_o,
        nc.psum_tensor(n_ + "ps_p", [P, 512], F32) as ps_p,
    ):
        if first:
            mods = ModUnits(k, "m0", 0, MODS_NORM0, 3, [ps_m[:, 0], ps_m[:, 1], ps_o[:]])
            conditions_stage(nc, k, block, ps_p)
        k.below_weights()

        def mean(pe, n, squares, sq, bank, std_ready, out_sem):
            pe.wait_ge(squares, n + 1)
            if n >= 1:
                pe.wait_ge(std_ready, n)
            for b in range(KB):
                mm = pe.matmul(bank[:, 0:CH], k.mean[:], sq[:, b], start=b == 0, stop=b == KB - 1)
            mm.then_inc(out_sem, 1)

        first_on_vector = min(n for n in range(NCH) if on_vector(n))
        pool_halves = lambda chunks: 2 * min(chunks, first_on_vector) + max(0, chunks - first_on_vector)

        def low(eng, n, h, done):
            eng.wait_ge(p_hi, 2 * n + h + 1)
            eng.tensor_tensor(k.h_lo[:, HALVES[h], chunk(n)], tmp_p[n % 2][:, HALVES[h]], f32(k.h_hi[:, HALVES[h], chunk(n)]),
                              ALU.subtract).then_inc(done, 1)

        def h_done(eng, chunks):
            eng.wait_ge(p_lo, pool_halves(chunks))
            if chunks > first_on_vector:
                eng.wait_ge(p_lo_v, chunks - first_on_vector)

        def p_mean_of(pe, n):
            mean(pe, n, p_sq, sq_p, ps_p, p_std, p_mean)

        def units(i):
            if not first or i >= NCH - 1:
                return range(0)
            h, rest = MODS_FIRST // 2, (MODS_NORM0 - MODS_FIRST) // (NCH - 1)
            return range(h * (i + 2), h * (i + 3)) if i < 0 else range(MODS_FIRST + rest * i, MODS_FIRST + rest * (i + 1))

        def store(sp, n):
            if final:
                sp.wait_ge(evac, n + 1)
                sp.dma_start(y_rows[n], nat[n % 2][:]).then_inc(x_out[n % 2], 16)
            else:
                sp.wait_ge(x_ready, n + 1)
                sp.dma_start(k.x_t[:, :, chunk(n)], x[n % XR][:]).then_inc(x_out[n % XR], 16)

        @block.sync
        def _(sp):
            for n in range(NCH):
                if first:
                    if n == 0:
                        for u in range(MODS_FIRST):
                            mods.load(sp, u)
                            if u == 1:
                                sp.dma_start(nat[0][:], x_rows[0]).then_inc(x_in[0], 16)
                        continue
                    if n >= 2:
                        sp.wait_ge(turned, n - 1)
                    sp.dma_start(nat[n % 2][:], x_rows[n]).then_inc(x_in[n % 2], 16)
                    for u in units(n - 1):
                        mods.load(sp, u)
                else:
                    if n >= XR:
                        if final:
                            sp.wait_ge(turned, n - XR + 1)
                        else:
                            sp.wait_ge(x_out[n % XR], 16 * (n // XR))
                            sp.wait_ge(p_scaled, n - XR + 1)
                    sp.dma_start(x[n % XR][:], k.x_t[:, :, chunk(n)]).then_inc(x_in[n % XR], 16)
                if n >= 2:
                    store(sp, n - 2)
                if ahead and n == 1:
                    ahead.load(sp, (0, 1))
            store(sp, NCH - 2)
            store(sp, NCH - 1)
            if ahead:
                ahead.load(sp, (2, 3))
            ring = 2 if final else XR
            for s in range(ring):
                sp.wait_ge(x_out[s], 16 * uses(s, ring))

        @block.tensor
        def _(pe):
            def turn_in(n):
                pe.wait_ge(x_in[n % 2], 16 * (n // 2 + 1))
                if n >= 1:
                    pe.wait_ge(x_ready, n)
                for a in range(2):
                    for b in range(KB):
                        mm = pe.transpose(ps_x[:, b, a * P:(a + 1) * P], nat[n % 2][:, a, b * P:(b + 1) * P], k.ident[:])
                mm.then_inc(turned, 1)

            def turn_out(n):
                pe.wait_ge(x_ready, n + 1)
                if n >= 1:
                    pe.wait_ge(evac, n)
                for a in range(2):
                    for b in range(KB):
                        mm = pe.transpose(ps_x[:].rearrange("p b t -> p (b t)")[:, a * D + b * P:a * D + (b + 1) * P],
                                          x[n % XR][:, b, a * P:(a + 1) * P], k.ident[:])
                mm.then_inc(turned, 1)

            for i in range(-2 if first else -1, NCH):
                if first:
                    if 0 <= i + 1 < NCH:
                        turn_in(i + 1)
                    for u in units(i):
                        mods.products(pe, u)
                        if u > units(i)[0]:
                            mods.turn(pe, u - 1)
                    for u in units(i)[-1:]:
                        mods.turn(pe, u)
                elif i + 1 < NCH:
                    mean(pe, i + 1, o_sq, sq_o, ps_o, o_std, o_mean)
                if i >= 0 and final:
                    turn_out(i)
                elif 0 <= i < NCH - 1:
                    p_mean_of(pe, i)
            if first:
                pe.wait_ge(x_ready, NCH)

        @block.scalar
        def _(act):
            def square_o(n):
                if first:
                    act.wait_ge(turned, n + 1)
                    if n >= XR:
                        act.wait_ge(x_out[n % XR], 16 * (n // XR))
                        act.wait_ge(p_scaled, n - XR + 1)
                    act.activation(x[n % XR][:], ps_x[:], ACT.Copy).then_inc(x_ready, 1)
                else:
                    if n >= 1:
                        act.wait_ge(o_mean, n)
                    act.activation(sq_o[:], acc[:, :, chunk(n)], ACT.Square).then_inc(o_sq, 1)

            def root(n, mean_ready, rstd_ready, bank, row, out_sem):
                act.wait_ge(mean_ready, n + 1)
                if n >= 1:
                    act.wait_ge(rstd_ready, n)
                act.activation(std[:, row, :], bank[:, 0:CH], ACT.Sqrt, bias=k.eps[:]).then_inc(out_sem, 1)

            def square_p(n):
                act.wait_ge(x_ready, n + 1)
                if n >= 1:
                    act.wait_ge(p_mean, n)
                act.activation(sq_p[:], x[n % XR][:], ACT.Square).then_inc(p_sq, 1)

            def modulate(n, h):
                s, c = n % 2, cond(n)
                if h == 0:
                    act.wait_ge(p_scaled, n + 1)
                if first and (n, h) == (0, 0):
                    act.wait_ge(mods.coef, 1)
                blocks = HALVES[h]
                for b in range(blocks.start, blocks.stop):
                    act.activation(tmp_p[s][:, b], tmp_p[s][:, b], ACT.Identity, bias=k.mod[:, 3 * i_pre * KB + b, c:c + 1],
                                   scale=k.pre[:, i_pre, b, c:c + 1]).then_inc(p_v, 1)
                act.wait_ge(p_v, KB * n + blocks.stop)
                act.activation(k.h_hi[:, blocks, chunk(n)], tmp_p[s][:, blocks], ACT.Copy).then_inc(p_hi, 1)

            def rows_out(n):
                act.wait_ge(turned, n + 1)
                if n >= 2:
                    act.wait_ge(x_out[n % 2], 16 * (n // 2))
                act.activation(nat[n % 2][:].rearrange("p a f -> p (a f)"), ps_x[:].rearrange("p b t -> p (b t)"),
                               ACT.Copy).then_inc(evac, 1)

            if final:
                square_o(0)
                for i in range(-1, NCH):
                    if i + 1 < NCH:
                        root(i + 1, o_mean, o_rstd, ps_o, 0, o_std)
                    if i + 2 < NCH:
                        square_o(i + 2)
                    if i >= 0:
                        rows_out(i)
                return

            for i in range(-2 if first else -1, NCH + 2):
                if 0 <= i + 1 < NCH:
                    square_o(i + 1)
                for u in units(i):
                    mods.copy(act, u)
                late = i == NCH
                mod = i >= 2
                if late:
                    modulate(i - 2, 0)
                if 0 <= i - 1 < NCH:
                    root(i - 1, p_mean, p_rstd, ps_p, 1, p_std)
                if mod and not late:
                    modulate(i - 2, 0)
                if not first and i + 1 < NCH:
                    root(i + 1, o_mean, o_rstd, ps_o, 0, o_std)
                if 0 <= i < NCH:
                    square_p(i)
                if mod:
                    modulate(i - 2, 1)
                if ahead and i == 2:
                    ahead.hi(act)

        @block.gpsimd
        def _(pool):
            if not final:
                for n in range(NCH):
                    for h in range(1 if on_vector(n) else 2):
                        low(pool, n, h, p_lo)
                    if ahead and n == 1:
                        ahead.lo(pool)
                pool.wait_ge(p_lo, NCH)

        @block.vector
        def _(dve):
            def scale(n, std_ready, row, rstd_ready, src, dst, out_sem):
                dve.wait_ge(std_ready, n + 1)
                if n >= 1:
                    dve.wait_ge(out_sem, n)
                dve.reciprocal(rstd[:, row, :], std[:, row, :]).then_inc(rstd_ready, 1)
                dve.wait_ge(rstd_ready, n + 1)
                dve.tensor_tensor(dst, src, rstd[:, row:row + 1, :].broadcast_to([P, KB, CH]), ALU.mult).then_inc(out_sem, 1)

            def residual(n):
                c, xs = cond(n), x[n % XR]
                out = acc[:, :, chunk(n)]
                scale(n, o_std, 0, o_rstd, out, out, o_scaled)
                dve.wait_ge(x_in[n % XR], 16 * (n // XR + 1))
                dve.wait_ge(o_scaled, n + 1)
                for b in range(KB):
                    ins = dve.scalar_tensor_tensor(out=xs[:, b], in0=out[:, b], scalar=k.gate[:, i_post, b, c:c + 1],
                                                   in1=xs[:, b], op0=ALU.mult, op1=ALU.add)
                ins.then_inc(x_ready, 1)

            def norm(n):
                if n >= 2:
                    h_done(dve, n - 1)
                dve.wait_ge(x_ready, n + 1)
                scale(n, p_std, 1, p_rstd, x[n % XR][:], tmp_p[n % 2][:], p_scaled)

            for i in range(-2 if first else 0, NCH + 1):
                for u in units(i):
                    mods.add(dve, u)
                if first and i == -1:
                    mods.all_added(dve, MODS_FIRST)
                    mods.pre(dve, 0)
                if first and i == NCH - 2:
                    mods.all_added(dve, MODS_NORM0)
                    mods.gate(dve, 0)
                    mods.pre(dve, 1)
                if not first and i < NCH:
                    residual(i)
                if not final and 1 <= i < NCH:
                    norm(i - 1)
                if not final and i == NCH:
                    norm(i - 1)
                    low(dve, NCH - 2, 1, p_lo_v)
                    low(dve, NCH - 1, 1, p_lo_v)
                    dve.wait_ge(p_lo_v, NCH - first_on_vector)

    if not final:
        return NormDone(h_done, [(x_out[s], 16 * uses(s, XR)) for s in range(XR)], lambda pe: p_mean_of(pe, NCH - 1))


def gemm_stage(nc, k, block, name, norm, first, w_halves, tail_cols, blocks, out_buf, parts=2):
    sem = lambda n: k.sem(f"{name}_{n}")
    raw, hi, lo, landed, rounded, split = k.raw, k.w_hi, k.w_lo, first.landed, first.rounded, first.split
    k.below_weights()
    ready = sem("ready")
    evac = [sem(f"evac{t}") for t in range(2 * NSP)]
    rounds = blocks // 2
    tail = tail_cols is not None
    with (
        nc.psum_tensor(name + "_ps", [P, 2 * NSP, 512], F32) as ps,
    ):
        @block.sync
        def _(sp):
            for rng, halves in w_halves:
                def load(i):
                    for b in range(2):
                        sp.wait_ge(split[b], i)
                        for part, src in halves(i, b):
                            sp.dma_start(part(raw[b]), src).then_inc(landed[b], 16)
                lo_, hi_ = max(rng[0], 2), rng[1]
                if hi_ > lo_:
                    with sp.Fori(lo_, hi_) as i:
                        load(i)
            if tail:
                sp.wait_ge(split[0], rounds)
                for part, src in tail_cols:
                    sp.dma_start(part(raw[0]), src).then_inc(landed[0], 16)

        @block.tensor
        def _(pe):
            def one(i, b, first_round=False, behind_first=None):
                pe.wait_ge(split[b], i + 1)
                for t, (at, n) in enumerate(SPANS):
                    norm.tokens(pe, at + n)
                    if not first_round:
                        pe.wait_ge(evac[NSP * b + t], i + 1)
                    for kk in range(KB):
                        mm = product3(pe, ps[:, NSP * b + t, 0:n], hi[b][:, kk], lo[b][:, kk],
                                      k.h_hi[:, kk, at:at + n], k.h_lo[:, kk, at:at + n], kk == 0, kk == KB - 1)
                    mm.then_inc(ready, 1)
                    if behind_first and t == 0:
                        behind_first(pe)
            one(0, 0, True, norm.last_mean)
            one(0, 1, True)
            with pe.Fori(1, rounds) as i:
                for b in range(2):
                    one(i, b)
            if tail:
                one(rounds, 0)

        def split_hi(act, i, b):
            act.wait_ge(landed[b], i * (16 * parts) + 16 * parts)
            act.activation(hi[b][:], raw[b][:], ACT.Copy).then_inc(rounded[b], 1)

        def split_lo(dve, i, b):
            dve.wait_ge(rounded[b], i + 1)
            dve.tensor_tensor(lo[b][:], raw[b][:], f32(hi[b][:]), ALU.subtract).then_inc(split[b], 1)

        def free_banks(eng, spans):
            for b in range(2):
                for t in spans:
                    eng.sem_inc(evac[NSP * b + t], 1)

        def out_of(eng, i, b, spans, op, with_next):
            for t in spans:
                at, n = SPANS[t]
                eng.wait_ge(ready, i * (2 * NSP) + NSP * b + t + 1)
                dst = out_buf[:, ds(2 * i + b, 1), at:at + n]
                op(dst, ps[:, NSP * b + t:NSP * b + t + 1, 0:n]).then_inc(evac[NSP * b + t], 1)
            if with_next:
                eng.wait_ge(ready, i * (2 * NSP) + NSP * (b + 1))

        @block.scalar
        def _(act):
            copy = lambda dst, src: act.activation(dst, src, ACT.Copy)
            free_banks(act, (0, 1))
            norm.buffers_free(act)
            if rounds > 1:
                with act.Fori(0, rounds - 1) as i:
                    for b in range(2):
                        out_of(act, i, b, (0, 1), copy, True)
                        split_hi(act, i + 1, b)
            out_of(act, rounds - 1, 0, (0, 1), copy, tail)
            if tail:
                split_hi(act, rounds, 0)
            out_of(act, rounds - 1, 1, (0, 1), copy, False)
            if tail:
                out_of(act, rounds, 0, (0, 1), copy, False)

        @block.vector
        def _(dve):
            free_banks(dve, (2,))
            norm.buffers_free(dve)
            if rounds > 1:
                with dve.Fori(0, rounds - 1) as i:
                    for b in range(2):
                        out_of(dve, i, b, (2,), dve.tensor_copy, True)
                        split_lo(dve, i + 1, b)
            out_of(dve, rounds - 1, 0, (2,), dve.tensor_copy, tail)
            if tail:
                split_lo(dve, rounds, 0)
            out_of(dve, rounds - 1, 1, (2,), dve.tensor_copy, False)
            if tail:
                out_of(dve, rounds, 0, (2,), dve.tensor_copy, False)


def first_ffn_weights(k, which):
    w1, w3 = [k.d[n][0, which].rearrange("(k p) n -> p k n", p=P) for n in ("ffn_w1", "ffn_w3")]
    return FirstWeights(k, f"f{which}", [[(lambda r: r[:], w[:, :, b * P:(b + 1) * P])] for b in range(2) for w in (w1, w3)])


def ffn_stage(nc, k, block, which, acc, norm, first):
    f = f"f{which}_"
    put = lambda n, shape, dt=F32: k.put(f + n, shape, dt)
    sem = lambda n: k.sem(f + n)
    raw, landed, rounded, split = k.raw, first.landed, first.rounded, first.split
    hi = k.w_hi + [put(f"w_hi{j}", [P, KB, P], F32R) for j in range(2, 6)]
    lo = k.w_lo + [put(f"w_lo{j}", [P, KB, P], F32R) for j in range(2, 6)]
    hid_hi = put("hid_hi", [P, GROUP, TOK], F32R)
    hid_lo = put("hid_lo", [P, GROUP, TOK], F32R)
    act_t = [put(f"act{s}", [P, 512]) for s in range(2)]
    k.below_weights()
    up_ready = [sem(f"up_ready{b}") for b in range(GROUP)]
    silu_done, prod_done = [sem(f"silu{s}") for s in range(2)], [sem(f"prod{s}") for s in range(2)]
    hid_r, hid_ready = [sem(f"hid_r{s}") for s in range(2)], [sem(f"hid_ready{t}") for t in range(NSP)]
    down_ready, down_evac = sem("down_ready"), [sem(f"down_evac{s}") for s in range(4)]
    zeroed = sem("zeroed")
    w1 = k.d["ffn_w1"][0, which].rearrange("(k p) n -> p k n", p=P)
    w3 = k.d["ffn_w3"][0, which].rearrange("(k p) n -> p k n", p=P)
    w2 = k.d["ffn_w2"][0, which]
    LAST = FF_GROUPS - 1
    with (
        nc.psum_tensor(f + "ps_g", [P, 2, 512], F32) as ps_g,
        nc.psum_tensor(f + "ps_u", [P, 2, 512], F32) as ps_u,
        nc.psum_tensor(f + "ps_d", [P, 4, 512], F32) as ps_d,
    ):
        @block.sync
        def _(sp):
            def load(i, js):
                for j in js:
                    s, n = j % 2, j // 2
                    sp.wait_ge(split[s], i * 3 + n)
                    if j < 4:
                        src = (w1, w3)[j % 2][:, :, ds(i * (GROUP * P) + (j // 2) * P, P)]
                        sp.dma_start(raw[s][:], src).then_inc(landed[s], 16)
                    else:
                        src = w2[ds(i * (GROUP * P) + (j - 4) * P, P), :]
                        sp.dma_start(raw[s][:].rearrange("p k n -> p (k n)"), src).then_inc(landed[s], 16)
            load(0, (4, 5))
            with sp.Fori(1, FF_GROUPS) as i:
                load(i, range(6))

        @block.tensor
        def _(pe):
            def group(i, behind_first=None):
                for b in range(GROUP):
                    for t, (at, n) in enumerate(SPANS):
                        s = (NSP * b + t) % 2
                        if b == 0:
                            norm.tokens(pe, at + n)
                        if not (behind_first and NSP * b + t < 2):
                            pe.wait_ge(prod_done[s], i * 3 + (NSP * b + t) // 2 + 1)
                        for ps, j in ((ps_g, 2 * b), (ps_u, 2 * b + 1)):
                            pe.wait_ge(split[j % 2], i * 3 + j // 2 + 1)
                            for kk in range(KB):
                                mm = product3(pe, ps[:, s, 0:n], hi[j][:, kk], lo[j][:, kk],
                                              k.h_hi[:, kk, at:at + n], k.h_lo[:, kk, at:at + n], kk == 0, kk == KB - 1)
                            if behind_first and (b, t, j) == (0, 0, 0):
                                behind_first(pe)
                        mm.then_inc(up_ready[b], 1)
                for j in (4, 5):
                    pe.wait_ge(split[j % 2], i * 3 + 3)
                for t, (at, n) in enumerate(SPANS):
                    pe.wait_ge(hid_ready[t], i * GROUP + GROUP + 1)
                    for m in range(KB):
                        s = m % 4
                        pe.wait_ge(down_evac[s], i * (2 * NSP) + 2 * t + m // 4 + 1)
                        for b in range(GROUP):
                            mm = product3(pe, ps_d[:, s, 0:n], hi[4 + b][:, m], lo[4 + b][:, m],
                                          hid_hi[:, b, at:at + n], hid_lo[:, b, at:at + n], b == 0, b == GROUP - 1)
                        mm.then_inc(down_ready, 1)

            group(0, norm.last_mean)
            with pe.Fori(1, FF_GROUPS) as i:
                group(i)

        def free_of(eng, i, j):
            if j < 4:
                eng.wait_ge(up_ready[j // 2], i * NSP + NSP)
            else:
                eng.wait_ge(down_ready, i * (NSP * KB) + NSP * KB)

        def split_hi(act, i, j):
            act.wait_ge(landed[j % 2], i * 48 + 16 * (j // 2) + 16)
            act.activation(hi[j][:], raw[j % 2][:], ACT.Copy).then_inc(rounded[j % 2], 1)

        def split_lo(dve, i, j):
            dve.wait_ge(rounded[j % 2], i * 3 + j // 2 + 1)
            dve.tensor_tensor(lo[j][:], raw[j % 2][:], f32(hi[j][:]), ALU.subtract).then_inc(split[j % 2], 1)

        @block.scalar
        def _(act):
            norm.buffers_free(act)
            for j in range(2, 6):
                split_hi(act, 0, j)

            def group(i, more):
                for b in range(GROUP):
                    for t, (at, n) in enumerate(SPANS):
                        q = NSP * b + t
                        s = q % 2
                        act.wait_ge(up_ready[b], i * NSP + t + 1)
                        pb, pt = divmod((q - 2) % 6, NSP)
                        act.wait_ge(hid_ready[pt], i * GROUP + (pb + 2 if q >= 2 else 1))
                        act.activation(act_t[s][:, 0:n], ps_g[:, s, 0:n], ACT.Silu).then_inc(silu_done[s], 1)
                        act.wait_ge(prod_done[s], i * 3 + q // 2 + 2)
                        act.activation(hid_hi[:, b, at:at + n], act_t[s][:, 0:n], ACT.Copy).then_inc(hid_r[s], 1)
                    if more:
                        for j in (2 * b, 2 * b + 1):
                            free_of(act, i, j)
                            split_hi(act, i + 1, j)
                if more:
                    for j in (4, 5):
                        free_of(act, i, j)
                        split_hi(act, i + 1, j)
            with act.Fori(0, LAST) as i:
                group(i, True)
            group(LAST, False)

        @block.gpsimd
        def _(pool):
            norm.buffers_free(pool)
            pool.memset(acc[:], 0.0).then_inc(zeroed, 1)

        @block.vector
        def _(dve):
            for free in prod_done + hid_ready + down_evac:
                dve.sem_inc(free, 1)
            for j in range(2, 6):
                split_lo(dve, 0, j)

            def group(i, more):
                for b in range(GROUP):
                    for t, (at, n) in enumerate(SPANS):
                        q = NSP * b + t
                        s = q % 2
                        dve.wait_ge(silu_done[s], i * 3 + q // 2 + 1)
                        dve.tensor_tensor(act_t[s][:, 0:n], ps_u[:, s, 0:n], act_t[s][:, 0:n],
                                          ALU.mult).then_inc(prod_done[s], 1)
                        dve.wait_ge(hid_r[s], i * 3 + q // 2 + 1)
                        dve.wait_ge(prod_done[s], i * 3 + q // 2 + 2)
                        dve.tensor_tensor(hid_lo[:, b, at:at + n], act_t[s][:, 0:n], f32(hid_hi[:, b, at:at + n]),
                                          ALU.subtract).then_inc(hid_ready[t], 1)
                    if more and b == 0:
                        for j in (0, 1):
                            split_lo(dve, i + 1, j)
                for t, (at, n) in enumerate(SPANS):
                    for m in range(KB):
                        if more and t == 1 and m % 4 == 0:
                            split_lo(dve, i + 1, 2 + m // 4)
                        dve.wait_ge(down_ready, i * (NSP * KB) + KB * t + m + 1)
                        dve.tensor_tensor(acc[:, m, at:at + n], ps_d[:, m % 4, 0:n], acc[:, m, at:at + n],
                                          ALU.add).then_inc(down_evac[m % 4], 1)
                if more:
                    for j in (4, 5):
                        split_lo(dve, i + 1, j)
            dve.wait_ge(zeroed, 1)
            with dve.Fori(0, LAST) as i:
                group(i, True)
            group(LAST, False)
            for s in range(4):
                dve.wait_ge(down_evac[s], FF_GROUPS * 2 * NSP + 1)


def turn_stage(nc, k, proj, b):
    sem = lambda n: k.sem("t_" + n)
    tabs_in, kc_in, turned, evac = sem("tabs_in"), sem("kc_in"), sem("turned"), [sem(f"evac{s}") for s in range(4)]
    shuffled, rotated, stored, pads = sem("shuffled"), sem("rotated"), sem("stored"), sem("pads")
    tile = lambda t: slice(t * P, (t + 1) * P)
    groups = [([proj[:, B_K, tile(t)] for t in range(2)], b.k_new[:])]
    for t in range(TILES):
        groups.append(([proj[:, B_V, tile(t)]], proj[:, B_V:B_V + 1, tile(t)]))
        if t == 1:
            groups.append(([b.kc_rows[:, a, :] for a in range(2)], b.kc_t[:].rearrange("p (a t) -> p a t", a=2)))
            KC = len(groups) - 1
        groups.append(([proj[:, B_GK + p, tile(t)] for p in range(2)],
                       b.gk_rows[:, t, :].rearrange("p (a f) -> p a f", a=2)))
        groups.append(([proj[:, B_GV + h, tile(t)] for h in range(GH)], proj[:, B_GV:B_GV + GH, tile(t)]))
    V_GROUPS = [g for g, (srcs, _) in enumerate(groups) if len(srcs) == 1]
    LOADS = 7
    Q_ORDER = (4, 0, 1, 2, 3)
    rope_in, cosined, k_hi_done, k_lo_done = sem("rope_in"), sem("cosined"), sem("k_hi"), sem("k_lo")
    with nc.psum_tensor("t_ps", [P, 4, 512], F32) as ps, nc.Block() as block:
        @block.sync
        def _(sp):
            d = k.d
            sp.dma_start(b.rope[:], d["const_rope"]).then_inc(rope_in, 16)
            sp.dma_start(b.kc_rows[:], d["cache_k"][0, 0].rearrange("(a p) g e -> p a (g e)", p=P)).then_inc(kc_in, 16)
            for dst, src in ((b.mask[:], d["const_mask"]), (b.gla_c[:], d["const_gla"]),
                             (b.vc[:], d["cache_v"][0, 0].rearrange("(a p) g e -> p a (g e)", p=P)),
                             (b.sink[:], d["attn_sink"][0].partition_broadcast(P)),
                             (b.b_up[:], d["gla_b_up"][0].rearrange("a n -> (a n)").partition_broadcast(P))):
                sp.dma_start(dst, src).then_inc(tabs_in, 16)
            sp.wait_ge(pads, 1)
            for a in range(2):
                sp.dma_start(b.w_up[96 + 16 * a:112 + 16 * a, 256 * a:256 * a + 256], d["gla_w_up"][0, a]).then_inc(tabs_in, 16)
            for g in (0, V_GROUPS[0], V_GROUPS[1]):
                sp.wait_ge(evac[g % 4], g // 4 + 1)
            sp.dma_start(k.o[2][0, 0].rearrange("(a p) g e -> p a (g e)", p=P), b.k_new[:]).then_inc(stored, 16)
            sp.dma_start(k.o[3][0, 0].rearrange("(a p) g e -> p a (g e)", p=P),
                         proj[:, B_V, 0:CTX].rearrange("p (a f) -> p a f", a=2)).then_inc(stored, 16)
            sp.wait_ge(stored, 32)
            sp.wait_ge(tabs_in, 16 * LOADS)

        @block.gpsimd
        def _(pool):
            padded = [f32(buf) for buf in [b.k_hi[:, TOK:TOK + P], b.k_lo[:, TOK:TOK + P]] + [
                q[:] for part in (b.q_hi, b.q_lo) for ring in part for q in ring]]
            early = [b.w_up[96:P, :]] + [x[:] for x in b.kin + b.qp + b.qin]
            for at, buf in enumerate(early + padded):
                if at:
                    pool.wait_ge(pads, at)
                if at >= len(early) and (at - len(early)) % 2 == 0:
                    n = (at - len(early)) // 2
                    if n == 0:
                        pool.wait_ge(rope_in, 16)
                    pool.wait_ge(shuffled, n + 1)
                    x = proj[:, Q_ORDER[n], CTX:TOK]
                    pool.tensor_tensor(x, x, b.rope[:, 0:LAT], ALU.mult).then_inc(cosined, 1)
                    pool.wait_ge(cosined, n + 1)
                pool.memset(buf, 0.0).then_inc(pads, 1)
            pool.wait_ge(pads, 17)

        @block.tensor
        def _(pe):
            for g, (srcs, _) in enumerate(groups):
                if g == KC:
                    pe.wait_ge(kc_in, 16)
                if g >= 4:
                    pe.wait_ge(evac[g % 4], g // 4)
                for a, src in enumerate(srcs):
                    mm = pe.transpose(ps[:, g % 4, a * P:(a + 1) * P], src, k.ident[:])
                mm.then_inc(turned, 1)

        def read_out(eng, g, op):
            srcs, dst = groups[g]
            eng.wait_ge(turned, g + 1)
            op(dst, ps[:, g % 4, 0:len(srcs) * P].rearrange("p (a f) -> p a f", f=P)).then_inc(evac[g % 4], 1)

        @block.scalar
        def _(act):
            for g in range(len(groups)):
                read_out(act, g, lambda dst, src: act.activation(dst, src, ACT.Copy))
            act.wait_ge(rotated, 2)
            act.activation(b.k_hi[:, 0:TOK], proj[:, B_K], ACT.Copy).then_inc(k_hi_done, 1)
            act.wait_ge(evac[KC % 4], KC // 4 + 1)
            act.activation(b.kc_hi[:], b.kc_t[:], ACT.Copy).then_inc(k_hi_done, 1)

        @block.vector
        def _(dve):
            swap = [(i + 16) % 32 for i in range(32)]

            def shuffle(n):
                if n >= 2:
                    dve.wait_ge(rotated, 2 * n - 2)
                dve.stream_shuffle(b.rot[n % 2][:], proj[:, Q_ORDER[n], CTX:TOK], swap).then_inc(shuffled, 1)

            shuffle(0)
            for n, q in enumerate(Q_ORDER):
                if n + 1 < len(Q_ORDER):
                    shuffle(n + 1)
                x, rot = proj[:, q, CTX:TOK], b.rot[n % 2][:]
                dve.wait_ge(shuffled, n + 1)
                if n == 0:
                    dve.wait_ge(rope_in, 16)
                dve.tensor_tensor(rot, rot, b.rope[:, LAT:2 * LAT], ALU.mult).then_inc(rotated, 1)
                dve.wait_ge(rotated, 2 * n + 1)
                dve.wait_ge(cosined, n + 1)
                dve.tensor_tensor(x, x, rot, ALU.add).then_inc(rotated, 1)
                if n == 3:
                    dve.wait_ge(k_hi_done, 2)
                    dve.tensor_tensor(b.k_lo[:, 0:TOK], proj[:, B_K], f32(b.k_hi[:, 0:TOK]), ALU.subtract).then_inc(k_lo_done, 1)
                    dve.tensor_tensor(b.kc_lo[:], b.kc_t[:], f32(b.kc_hi[:]), ALU.subtract).then_inc(k_lo_done, 1)
            dve.wait_ge(rotated, 2 * len(Q_ORDER))


def attention_stage(nc, k, proj, b):
    sem = lambda n: k.sem("a_" + n)
    (q_hi_done, q_lo_done, scored, masked, neg_max, exped, sink_exped, den_done, inv_done,
     normed, turned, pt_done, weighted, out_done) = [sem(n) for n in (
         "q_hi", "q_lo", "scored", "masked", "neg_max", "exped", "sink_exped", "den", "inv",
         "normed", "turned", "pt", "weighted", "out")]
    flat = proj[:].rearrange("p b t -> p (b t)")
    units = [(t, q, g) for t in range(TILES) for q in range(4) for g in range(NKV)]
    U, PER = len(units), NQ
    keys = lambda t: CTX if t < CTX_TILES else 3 * P + CTX
    tile = lambda t: slice(t * P, (t + 1) * P)
    half = lambda g: slice(HD * g, HD * (g + 1))
    with (
        nc.psum_tensor("a_s0", [P, 1024], F32) as s0, nc.psum_tensor("a_s1", [P, 1024], F32) as s1,
        nc.psum_tensor("a_t", [P, 1024], F32) as ps_t, nc.psum_tensor("a_v", [P, 2, 512], F32) as ps_v,
        nc.Block() as block,
    ):
        ps_s = [s0, s1]

        @block.tensor
        def _(pe):
            def scores(u):
                t, q, g = units[u]
                if u % PER == 0:
                    pe.wait_ge(q_lo_done, NKV * (t + 1))
                if u >= 2:
                    pe.wait_ge(masked, u - 1)
                spans = [(512, 768, b.k_hi[:, 0:CTX], b.k_lo[:, 0:CTX])] if t < CTX_TILES else [
                    (P, 512, b.k_hi[:, (t - 1) * P:(t + 2) * P], b.k_lo[:, (t - 1) * P:(t + 2) * P]),
                    (512, 768, b.kc_hi[:], b.kc_lo[:])]
                for lo, hi, kh, kl in spans:
                    mm = product3(pe, ps_s[u % 2][:, lo:hi], b.q_hi[t % 2][g][:, q], b.q_lo[t % 2][g][:, q], kh, kl, True, True)
                mm.then_inc(scored, 1)

            def turn(u):
                pe.wait_ge(normed, u + 1)
                if u >= 1:
                    pe.wait_ge(pt_done, u)
                for a in range(keys(units[u][0]) // P):
                    mm = pe.transpose(ps_t[:, tile(a)], b.prob[u % 3][:, tile(a)], k.ident[:])
                mm.then_inc(turned, 1)

            def weigh(u):
                t, q, g = units[u]
                pe.wait_ge(pt_done, u + 1)
                if u % PER == 0 and t >= 2:
                    pe.wait_ge(out_done, t - 1)
                n = keys(t) // P
                for a in range(n):
                    if t < CTX_TILES:
                        v = proj[:, B_V, a * P + g * HD:a * P + (g + 1) * HD]
                    elif a < 3:
                        at = B_V * TOK + (t - 1 + a) * P + g * HD
                        v = flat[:, at:at + HD]
                    else:
                        v = b.vc[:, a - 3, half(g)]
                    mm = pe.matmul(ps_v[half(g), t % 2, tile(q)], v, b.prob_t[u % 2][:, tile(a)], start=a == 0, stop=a == n - 1)
                mm.then_inc(weighted, 1)

            for u in range(U + 4):
                if u < U:
                    scores(u)
                if u >= 4:
                    weigh(u - 4)
                if 3 <= u <= U + 2:
                    turn(u - 3)

        @block.scalar
        def _(act):
            def query_hi(t):
                if t >= 2:
                    act.wait_ge(scored, PER * (t - 1))
                for g in range(NKV):
                    act.activation(b.q_hi[t % 2][g][half(g)], proj[half(g), 0:4, tile(t)], ACT.Copy).then_inc(q_hi_done, 1)

            def exps(u):
                t, q, g = units[u]
                act.wait_ge(neg_max, u + 1)
                if u >= 3:
                    act.wait_ge(turned, u - 2)
                act.activation(b.prob[u % 3][:, 0:keys(t)], b.score[u % 2][:, 0:keys(t)], ACT.Exp, bias=b.negm[:, u:u + 1],
                               accum_out=b.rsum[:, u:u + 1]).then_inc(exped, 1)
                act.activation(b.esink[:, u:u + 1], b.sink[:, q + 4 * g:q + 4 * g + 1], ACT.Exp,
                               bias=b.negm[:, u:u + 1]).then_inc(sink_exped, 1)

            def copy_t(u):
                act.wait_ge(turned, u + 1)
                if u >= 2:
                    act.wait_ge(weighted, u - 1)
                n = keys(units[u][0])
                act.activation(b.prob_t[u % 2][:, 0:n], ps_t[:, 0:n], ACT.Copy).then_inc(pt_done, 1)

            query_hi(0)
            for u in range(U + 5):
                if 3 <= u <= U + 2:
                    copy_t(u - 3)
                if u < U:
                    exps(u)
                if u % PER == 3 and u < U and u // PER + 1 < TILES:
                    query_hi(u // PER + 1)
                if u >= 5 and (u - 5) % PER == PER - 1:
                    t = (u - 5) // PER
                    act.wait_ge(weighted, PER * (t + 1))
                    act.activation(proj[:, 0:4, tile(t)], ps_v[:, t % 2].rearrange("p (a f) -> p a f", a=4),
                                   ACT.Copy).then_inc(out_done, 1)

        @block.vector
        def _(dve):
            def query_lo(t):
                for g in range(NKV):
                    dve.wait_ge(q_hi_done, NKV * t + g + 1)
                    dve.tensor_tensor(b.q_lo[t % 2][g][half(g)], proj[half(g), 0:4, tile(t)], f32(b.q_hi[t % 2][g][half(g)]),
                                      ALU.subtract).then_inc(q_lo_done, 1)

            def mask(u):
                t, q, g = units[u]
                lo = 512 if t < CTX_TILES else P
                kind = 0 if t == CTX_TILES else 2 if t == TILES - 1 else 1
                at = kind * (3 * P + CTX) + (3 * P if t < CTX_TILES else 0)
                dve.wait_ge(scored, u + 1)
                if u >= 2:
                    dve.wait_ge(exped, u - 1)
                dve.tensor_tensor_reduce(b.score[u % 2][:, 0:keys(t)], ps_s[u % 2][:, lo:768], b.mask[:, at:at + keys(t)],
                                         HD ** -0.5, -3.0e38, ALU.add, ALU.max, b.rmax[:, u:u + 1]).then_inc(masked, 1)
                dve.wait_ge(masked, u + 1)
                dve.tensor_scalar(b.negm[:, u:u + 1], b.rmax[:, u:u + 1], b.sink[:, q + 4 * g:q + 4 * g + 1], -1.0,
                                  ALU.max, ALU.mult).then_inc(neg_max, 1)

            def norm(u):
                n = keys(units[u][0])
                dve.wait_ge(sink_exped, u + 1)
                dve.tensor_tensor(b.den[:, u:u + 1], b.rsum[:, u:u + 1], b.esink[:, u:u + 1], ALU.add).then_inc(den_done, 1)
                dve.wait_ge(den_done, u + 1)
                dve.reciprocal(b.inv[:, u:u + 1], b.den[:, u:u + 1]).then_inc(inv_done, 1)
                dve.wait_ge(inv_done, u + 1)
                dve.tensor_scalar(b.prob[u % 3][:, 0:n], b.prob[u % 3][:, 0:n], b.inv[:, u:u + 1], None,
                                  ALU.mult).then_inc(normed, 1)

            query_lo(0)
            for u in range(U + 1):
                if u < U:
                    mask(u)
                if u >= 1:
                    norm(u - 1)
                if u % PER == 4 and u // PER + 1 < TILES and u < U:
                    query_lo(u // PER + 1)


def gla_stage(nc, k, proj, b):
    sem = lambda n: k.sem("g_" + n)
    (z_ready, z_sum, z_neg, z_exp, ln_ready, la_ready, b_ready, half_done, rel_done, ex_ready, qk_done, kin_done,
     qin_done, s_ready, kv_ready, at_ready, st_ready, o_ready, st_in) = [sem(n) for n in (
         "z_ready", "z_sum", "z_neg", "z_exp", "ln_ready", "la_ready", "b_ready", "half", "rel", "ex_ready", "qk",
         "kin", "qin", "s_ready", "kv_ready", "at_ready", "st_ready", "o_ready", "st_in")]
    o_used = [sem("o_used0"), sem("o_used1")]
    zeroed, st_out, sq_done = sem("zeroed"), sem("st_out"), sem("sq_done")
    order = [(0, t) for t in range(TILES)] + [(1, t) for t in (1, 0)] + [(1, t) for t in range(TILES - 1, CTX_TILES - 1, -1)]
    U = len(order)
    starts = {0: b.zero, CTX_TILES: b.s_in[0], TILES: b.zero, TILES + CTX_TILES: b.s_in[1]}
    ends = {CTX_TILES - 1: b.s_end[0], TILES + CTX_TILES - 1: b.s_end[1], TILES - 1: b.s_junk, U - 1: b.s_junk}
    tile = lambda t: slice(t * P, (t + 1) * P)
    steps = 2 * CPT
    last_col = lambda dr: GLA_C - 1 if dr == 0 else 0
    chunks = lambda dr: range(CPT) if dr == 0 else range(CPT - 1, -1, -1)

    def state(n, i):
        if i == CPT:
            return ends[n] if n in ends else b.state[(n + 1) % 2][:, 0]
        return starts[n] if i == 0 and n in starts else b.state[n % 2][:, i]

    with (
        nc.psum_tensor("g_z", [P, 512], F32) as ps_z, nc.psum_tensor("g_b", [P, 512], F32) as ps_b,
        nc.psum_tensor("g_s", [P, 512], F32) as ps_s, nc.psum_tensor("g_o", [P, 2, 512], F32) as ps_o,
        nc.psum_tensor("g_kv", [P, CPT, 2, P], F32) as ps_kv, nc.psum_tensor("g_m", [P, 512], F32) as ps_m,
        nc.Block() as block,
    ):
        k.at = b.behind
        mods = ModUnits(k, "m1", MODS_NORM0, MODB // ModUnits.WB - MODS_NORM0, 1, [ps_m[:]])
        decay = ps_b[:, 0:2 * P].rearrange("p (a t) -> p a t", a=2)
        rest = ps_b[:, 2 * P:4 * P]

        @block.sync
        def _(sp):
            for dr, name in ((0, "state_gla_fwd"), (1, "state_gla_bwd")):
                for a in range(2):
                    sp.dma_start(b.s_in[dr][a * DK:(a + 1) * DK], k.d[name][0, 0, a::2].rearrange("q e v -> e q v")).then_inc(st_in, 16)
            store_at = {CTX_TILES + 1: (0, CTX_TILES - 1), TILES + CTX_TILES + 1: (1, TILES + CTX_TILES - 1)}
            for u in range(mods.count):
                mods.load(sp, u)
                if u not in store_at:
                    continue
                dr, n = store_at[u]
                sp.wait_ge(st_ready, steps * (n + 1))
                for a in range(2):
                    sp.dma_start(k.o[4 + dr][0, 0, a::2].rearrange("q e v -> e q v"),
                                 b.s_end[dr][a * DK:(a + 1) * DK]).then_inc(st_out, 16)
            sp.wait_ge(st_out, 64)

        @block.gpsimd
        def _(pool):
            pool.memset(b.zero[:], 0.0).then_inc(zeroed, 1)

        @block.tensor
        def _(pe):
            def gates(n):
                dr, t = order[n]
                if n >= 1:
                    pe.wait_ge(z_sum, n)
                pe.matmul(ps_z[:, 0:256], proj[96:P, B_LR, tile(t)], b.w_up[96:P, dr * 256:dr * 256 + 256],
                          start=True, stop=True).then_inc(z_ready, 1)

            def sums(n):
                dr, t = order[n]
                pe.wait_ge(la_ready, n + 1)
                if n >= 1:
                    pe.wait_ge(ex_ready, 4 * n)
                for a in range(2):
                    pe.matmul(decay[:, a], b.la[n % 2][:, tile(a)], b.gla_c[:, tile(3 * dr)], start=True, stop=True)
                pe.matmul(rest, b.gla_c[:, tile(3 * dr + 1)], b.la[n % 2][:], start=True, stop=True).then_inc(b_ready, 1)

            def scores(n):
                pe.wait_ge(qk_done, 3 * n + 3)
                if n >= 1:
                    pe.wait_ge(at_ready, n)
                for a in range(2):
                    mm = pe.matmul(ps_s[:, 256 * a:256 * a + 256], b.kp[n % 2][:, a], b.qp[n % 2][:, a], start=True, stop=True)
                mm.then_inc(s_ready, 1)

            def outer(n):
                dr, t = order[n]
                pe.wait_ge(kin_done, CPT * (n + 1))
                if n >= 1:
                    pe.wait_ge(st_ready, steps * n)
                for c in chunks(dr):
                    for h in range(GH):
                        mm = pe.matmul(ps_kv[DK * (h % 2):DK * (h % 2) + DK, c, h // 2, :], b.kin[n % 2][:, c, h * DK:(h + 1) * DK],
                                       proj[:, B_GV + h, tile(t)], start=True, stop=True)
                mm.then_inc(kv_ready, 1)

            def outputs(n):
                dr, t = order[n]
                pe.wait_ge(at_ready, n + 1)
                if n >= 2:
                    m = n - 2
                    pe.wait_ge(o_used[m // TILES], m % TILES + 1)
                for h in range(GH):
                    pe.matmul(ps_o[:, n % 2, tile(h)], b.at[:, h], proj[:, B_GV + h, tile(t)], start=h == 0, stop=False,
                              skip_group_check=True)
                pe.wait_ge(qin_done, 2 * (n + 1))
                if n == 0:
                    pe.wait_ge(zeroed, 1)
                    pe.wait_ge(st_in, 64)
                for i, c in enumerate(chunks(dr)):
                    cc = slice(c * GLA_C, (c + 1) * GLA_C)
                    if steps * n + 2 * i:
                        pe.wait_ge(st_ready, steps * n + 2 * i)
                    for h in range(GH):
                        mm = pe.matmul(ps_o[cc, n % 2, tile(h)], b.qin[n % 2][:, h // 2, h % 2, cc], state(n, i)[:, h // 2],
                                       start=False, stop=i == CPT - 1, skip_group_check=True)
                mm.then_inc(o_ready, 1)

            for n in range(-2, U):
                if n >= 0:
                    scores(n)
                if 0 <= n + 1 < U:
                    sums(n + 1)
                if n + 2 < U:
                    gates(n + 2)
                if 0 <= n < mods.count:
                    mods.products(pe, n)
                if n >= 0:
                    outer(n)
                    outputs(n)
                if 0 <= n < mods.count:
                    mods.turn(pe, n)

        @block.scalar
        def _(act):
            def factors(n):
                act.wait_ge(rel_done, n + 1)
                if n >= 2:
                    act.wait_ge(st_ready, steps * (n - 1))
                if n >= 1:
                    act.wait_ge(kin_done, CPT * n)
                    act.wait_ge(qin_done, 2 * n)
                act.activation(b.ep[:], b.rel[:], ACT.Exp).then_inc(ex_ready, 1)
                act.activation(b.en[:], b.rel[:], ACT.Exp, scale=-1.0).then_inc(ex_ready, 1)
                act.activation(b.er[:], rest, ACT.Exp).then_inc(ex_ready, 1)
                act.activation(b.eb[n % 2][:], decay, ACT.Exp).then_inc(ex_ready, 1)

            def log_sum(n):
                act.wait_ge(z_neg, n + 1)
                act.activation(b.ze[:], b.zn[:], ACT.Exp).then_inc(z_exp, 1)
                act.wait_ge(z_exp, n + 1)
                if n >= 1:
                    act.wait_ge(la_ready, n)
                act.activation(b.zl[:], b.ze[:], ACT.Ln, bias=1.0).then_inc(ln_ready, 1)

            def collect(n):
                act.wait_ge(o_ready, n + 1)
                act.activation(b.o_rows[:, order[n][1]], ps_o[:, n % 2], ACT.Copy).then_inc(o_used[0], 1)

            def squares(n):
                m, t = n - TILES, order[n][1]
                act.wait_ge(o_used[1], m + 1)
                for h in range(GH):
                    if m or h:
                        act.wait_ge(sq_done, m * GH + h)
                    act.activation(b.junk[:, 0], b.o_rows[:, t, h * DV:(h + 1) * DV], ACT.Square,
                                   accum_out=b.var[:, t * GH + h:t * GH + h + 1]).then_inc(sq_done, 1)

            for n in range(-2, U):
                if 0 <= n + 1 < U:
                    factors(n + 1)
                if n + 2 < U:
                    log_sum(n + 2)
                if 0 <= n < mods.count:
                    mods.copy(act, n)
                if n >= 1 and order[n - 1][0] == 0:
                    collect(n - 1)
                if n >= TILES + 2:
                    squares(n - 2)
            squares(U - 2)
            squares(U - 1)

        @block.vector
        def _(dve):
            def gate_in(n):
                dr, t = order[n]
                dve.wait_ge(z_ready, n + 1)
                if n >= 1:
                    dve.wait_ge(la_ready, n)
                dve.tensor_tensor(b.z[:], ps_z[:, 0:256], b.b_up[:, dr * 256:dr * 256 + 256], ALU.add).then_inc(z_sum, 1)
                dve.wait_ge(z_sum, n + 1)
                if n >= 1:
                    dve.wait_ge(z_exp, n)
                dve.scalar_tensor_tensor(out=b.zn[:], in0=b.z[:], scalar=-1.0, in1=b.z[:], op0=ALU.mult, op1=ALU.min).then_inc(z_neg, 1)

            def log_gate(n):
                dve.wait_ge(ln_ready, n + 1)
                dve.scalar_tensor_tensor(out=b.la[n % 2][:], in0=b.z[:], scalar=0.0, in1=b.zl[:], op0=ALU.min,
                                         op1=ALU.subtract).then_inc(la_ready, 1)

            def relative(n):
                dr, t = order[n]
                dve.wait_ge(b_ready, n + 1)
                chunked = decay.rearrange("p a (c t) -> p a c t", t=GLA_C)
                if n >= 1:
                    dve.wait_ge(rel_done, n)
                dve.tensor_scalar(b.half[:], chunked[:, :, :, last_col(dr)], 0.5, None, ALU.mult).then_inc(half_done, 1)
                dve.wait_ge(half_done, n + 1)
                if n >= 1:
                    dve.wait_ge(ex_ready, 4 * n)
                dve.tensor_tensor(b.rel[:].rearrange("p a (c t) -> p a c t", t=GLA_C), chunked,
                                  b.half[:].unsqueeze(3).broadcast_to([P, 2, CPT, GLA_C]), ALU.subtract).then_inc(rel_done, 1)

            def scaled(n, src, factor, dst, done):
                for g in range(2):
                    rows = slice(DK * g, DK * (g + 1))
                    dve.scalar_tensor_tensor(out=dst[rows, :, g], in0=src[rows], scalar=DK ** -0.5, in1=factor[rows],
                                             op0=ALU.mult, op1=ALU.mult).then_inc(done, 1)

            def score_factors(n):
                t = order[n][1]
                dve.wait_ge(ex_ready, 4 * n + 2)
                scaled(n, proj[:, B_GQ:B_GQ + 2, tile(t)], b.ep, b.qp[n % 2], qk_done)
                dve.tensor_tensor(b.kp[n % 2][:], proj[:, B_GK:B_GK + 2, tile(t)], b.en[:], ALU.mult).then_inc(qk_done, 1)

            def state_factors(n):
                t = order[n][1]
                dve.wait_ge(ex_ready, 4 * n + 4)
                for c in range(CPT):
                    rows = slice(c * GLA_C, (c + 1) * GLA_C)
                    dve.tensor_tensor(b.kin[n % 2][rows, c], b.gk_rows[rows, t], b.er[rows], ALU.mult).then_inc(kin_done, 1)
                scaled(n, proj[:, B_GQ:B_GQ + 2, tile(t)], b.eb[n % 2], b.qin[n % 2], qin_done)

            def mask(n):
                dr, t = order[n]
                dve.wait_ge(s_ready, n + 1)
                m = b.gla_c[:, tile(3 * dr + 2)]
                dve.tensor_tensor(b.at[:], ps_s[:].rearrange("p (a t) -> p a t", a=GH), m.unsqueeze(1).broadcast_to([P, GH, P]),
                                  ALU.mult).then_inc(at_ready, 1)

            def chain(n):
                dr, t = order[n]
                if n == 0:
                    dve.wait_ge(zeroed, 1)
                dve.wait_ge(kv_ready, n + 1)
                for i, c in enumerate(chunks(dr)):
                    if i or n:
                        dve.wait_ge(st_ready, steps * n + 2 * i)
                    last = c * GLA_C + last_col(dr)
                    for a in range(2):
                        dve.scalar_tensor_tensor(out=state(n, i + 1)[:, a], in0=state(n, i)[:, a],
                                                 scalar=b.eb[n % 2][:, a, last:last + 1], in1=ps_kv[:, c, a],
                                                 op0=ALU.mult, op1=ALU.add).then_inc(st_ready, 1)

            def collect(n):
                dve.wait_ge(o_ready, n + 1)
                dst = b.o_rows[:, order[n][1]]
                dve.tensor_tensor(dst, ps_o[:, n % 2], dst, ALU.add).then_inc(o_used[1], 1)

            dve.wait_ge(st_in, 64)
            for n in range(-2, U):
                if n >= 0:
                    mask(n)
                if 0 <= n - 1 < mods.count:
                    mods.add(dve, n - 1)
                if 0 <= n + 1 < U:
                    relative(n + 1)
                if n + 2 < U:
                    gate_in(n + 2)
                if 0 <= n + 1 < U:
                    score_factors(n + 1)
                if n + 2 < U:
                    log_gate(n + 2)
                if n >= 0:
                    chain(n)
                if 0 <= n + 1 < U:
                    state_factors(n + 1)
                if n >= 1 and order[n - 1][0] == 1:
                    dve.wait_ge(o_used[0], TILES)
                    collect(n - 1)
            collect(U - 1)
            mods.all_added(dve, mods.count)
            mods.gate(dve, 1)
            mods.pre(dve, 2)
            mods.gate(dve, 2)


class MixDone:

    def __init__(self, split_heads, split_gla):
        self.sems = [(split_heads, KB // 2), (split_gla, KB // 2)]
        self.last_mean = None

    def tokens(self, eng, end):
        for s, n in self.sems:
            eng.wait_ge(s, n)

    def buffers_free(self, eng):
        self.tokens(eng, TOK)


def gla_out_stage(nc, k, block, proj, b, ahead):
    sem = lambda n: k.sem("e_" + n)
    std_done, inv_done, normed, turned, evac, silu_done, w_in = [sem(n) for n in (
        "std_done", "inv_done", "normed", "turned", "evac", "silu_done", "w_in")]
    heads_hi, heads_lo, gla_hi, gla_lo = [sem(n) for n in ("heads_hi", "heads_lo", "gla_hi", "gla_lo")]
    tile = lambda t: slice(t * P, (t + 1) * P)
    H = KB // 2
    with nc.psum_tensor("e_pad", [P, 6, 512], F32), nc.psum_tensor("e_ps", [P, 2, 512], F32) as ps:
        @block.sync
        def _(sp):
            with nc.allow_non_contiguous_dma(reason="one column of 128 values"):
                sp.dma_start(b.nw[:], k.d["gla_norm"].rearrange("a v -> v a")).then_inc(w_in, 16)
            ahead.load(sp, (0, 1, 2, 3))

        @block.scalar
        def _(act):
            act.activation(b.std[:], b.var[:], ACT.Sqrt, bias=k.eps[:], scale=1.0 / DV).then_inc(std_done, 1)
            for h in range(GH):
                act.activation(proj[:, B_GG + h], proj[:, B_GG + h], ACT.Silu).then_inc(silu_done, 1)
            for h in range(H):
                act.activation(k.h_hi[:, h], proj[:, h], ACT.Copy).then_inc(heads_hi, 1)
            ahead.hi(act)
            act.wait_ge(evac, TILES)
            for h in range(H):
                act.activation(k.h_hi[:, H + h], proj[:, B_GG + h], ACT.Copy).then_inc(gla_hi, 1)

        @block.gpsimd
        def _(pool):
            for h in range(H):
                pool.wait_ge(heads_hi, h + 1)
                pool.tensor_tensor(k.h_lo[:, h], proj[:, h], f32(k.h_hi[:, h]), ALU.subtract).then_inc(heads_lo, 1)
            ahead.lo(pool)

        @block.vector
        def _(dve):
            dve.wait_ge(std_done, 1)
            dve.reciprocal(b.istd[:], b.std[:]).then_inc(inv_done, 1)
            dve.wait_ge(inv_done, 1)
            dve.wait_ge(w_in, 16)

            def norm(t):
                o = b.o_rows[:, t].rearrange("p (h v) -> p h v", h=GH)
                dve.tensor_tensor(o, o, b.istd[:, t * GH:(t + 1) * GH].unsqueeze(2).broadcast_to([P, GH, DV]),
                                  ALU.mult).then_inc(normed, 1)

            def gate(t):
                dve.wait_ge(turned, t + 1)
                g = proj[:, B_GG:B_GG + GH, tile(t)]
                dve.scalar_tensor_tensor(out=g, in0=ps[:, t % 2].rearrange("p (h t) -> p h t", h=GH), scalar=b.nw[:, 0:1],
                                         in1=g, op0=ALU.mult, op1=ALU.mult).then_inc(evac, 1)

            for t in range(TILES):
                norm(t)
                if t == 5:
                    dve.wait_ge(silu_done, GH)
                if t >= 5:
                    gate(t - 5)
            for t in range(TILES - 5, TILES):
                gate(t)
            for h in range(H):
                dve.wait_ge(gla_hi, h + 1)
                dve.tensor_tensor(k.h_lo[:, H + h], proj[:, B_GG + h], f32(k.h_hi[:, H + h]), ALU.subtract).then_inc(gla_lo, 1)

        @block.tensor
        def _(pe):
            for t in range(TILES):
                pe.wait_ge(normed, t + 1)
                if t >= 2:
                    pe.wait_ge(evac, t - 1)
                for h in range(GH):
                    mm = pe.transpose(ps[:, t % 2, h * P:(h + 1) * P], b.o_rows[:, t, h * DV:(h + 1) * DV], k.ident[:])
                mm.then_inc(turned, 1)
    return MixDone(heads_lo, gla_lo)


class MixerBuffers:

    def __init__(self, k):
        k.at = k.hi_at
        put = lambda name, shape, dt=F32: k.put("x_" + name, shape, dt)
        self.kc_rows, self.vc, self.k_new = put("kc_rows", [P, 2, P]), put("vc", [P, 2, P]), put("k_new", [P, 2, P])
        self.kc_t = put("kc_t", [P, CTX])
        self.sink, self.b_up, self.w_up = put("sink", [P, NQ]), put("b_up", [P, 512]), put("w_up", [P, 512])
        self.gk_rows = put("gk_rows", [P, TILES, 2 * P])
        shared = k.hi_at + 4 * 4 * TOK
        assert k.at <= shared
        tail = k.rest - 4 * 6 * P
        k.at = tail
        self.gla_c = put("gla_c", [P, 6 * P])
        k.at = shared
        self.mask = put("mask", [P, 3 * (3 * P + CTX)])
        tables = k.at
        self.rope, self.rot = put("rope", [P, 2 * LAT]), [put(f"rot{s}", [P, LAT]) for s in range(2)]
        k.at = tables
        self.score = [put(f"score{s}", [P, 3 * P + CTX]) for s in range(2)]
        self.prob = [put(f"prob{s}", [P, 3 * P + CTX]) for s in range(3)]
        self.prob_t = [put(f"prob_t{s}", [P, 3 * P + CTX]) for s in range(2)]
        assert k.at >= tables + 4 * 4 * LAT
        self.k_hi, self.k_lo = [put(n, [P, TOK + P], F32R) for n in ("k_hi", "k_lo")]
        self.kc_hi, self.kc_lo = [put(n, [P, CTX], F32R) for n in ("kc_hi", "kc_lo")]
        self.q_hi, self.q_lo = [[[put(f"{n}{s}{g}", [P, 4, P], F32R) for g in range(NKV)] for s in range(2)]
                                for n in ("q_hi", "q_lo")]
        self.rmax, self.negm, self.rsum, self.esink, self.den, self.inv = [
            put(n, [P, TILES * NQ]) for n in ("rmax", "negm", "rsum", "esink", "den", "inv")]
        assert k.at <= tail
        k.at = shared
        self.o_rows = put("o_rows", [P, TILES, GH * DV])
        self.z, self.zn, self.ze, self.zl, self.er = [put(n, [P, 256]) for n in ("z", "zn", "ze", "zl", "er")]
        self.la = [put(f"la{s}", [P, 256]) for s in range(2)]
        self.ep, self.en, self.rel = [put(n, [P, 2, P]) for n in ("ep", "en", "rel")]
        self.eb, self.kp = [[put(f"{n}{s}", [P, 2, P]) for s in range(2)] for n in ("eb", "kp")]
        self.half = put("half", [P, 2, CPT])
        self.at = put("at", [P, GH, P])
        self.state = [put(f"state{s}", [P, CPT, 2, DV]) for s in range(2)]
        self.s_in, self.s_end = [[put(f"{n}{s}", [P, 2, DV]) for s in range(2)] for n in ("s_in", "s_end")]
        self.zero, self.s_junk = put("zero", [P, 2, DV]), put("s_junk", [P, 2, DV])
        k.at = max(k.at, k.hi_at + 12 * 4 * TOK)
        self.junk, self.nw = put("junk", [P, 4, DV]), put("nw", [P, 1])
        self.var, self.std, self.istd = [put(n, [P, TILES * GH]) for n in ("var", "std", "istd")]
        assert k.at <= tail
        k.at = k.rest + 4 * PROJB * TOK
        self.kin = [put(f"kin{s}", [P, CPT, GH * DK]) for s in range(2)]
        self.qp, self.qin = [[put(f"{n}{s}", [P, 2, 2, P]) for s in range(2)] for n in ("qp", "qin")]
        self.behind = k.at


def in_halves(k):
    w_in = k.d["w_in"][0].rearrange("(k p) n -> p k n", p=P)

    def heads(i, b):
        return [(lambda r, q=q: r[:, :, q * HD:(q + 1) * HD], w_in[:, :, 64 * (2 * i + b) + 256 * q:64 * (2 * i + b) + 256 * q + 64])
                for q in range(2)]

    def plain(i, b):
        return k_halves(w_in, i * (2 * P) + b * P)

    return w_in, heads, plain


def mixer(nc, k, proj):
    b = MixerBuffers(k)
    turn_stage(nc, k, proj, b)
    attention_stage(nc, k, proj, b)
    gla_stage(nc, k, proj, b)
    k.recycle()
    return b


def out_parts(k):
    w_out = k.d["w_out"][0]

    def mixed(i, b):
        col = ds(i * (2 * P) + b * P, P)
        heads = [(lambda r, g=g: r[HD * g:HD * (g + 1), 0:4, :],
                  w_out[256 * g:256 * (g + 1), col].rearrange("(k p) n -> p k n", p=HD)) for g in range(NKV)]
        return heads + [(lambda r: r[:, 4:8, :], w_out[512:1024, col].rearrange("(k p) n -> p k n", p=P))]

    return mixed


def k_halves(w, col):
    h = KB // 2
    return [(lambda r, q=q: r[:, q * h:(q + 1) * h, :], w[:, q * h:(q + 1) * h, ds(col, P)]) for q in range(2)]


def layer(nc, d, o):
    k = Core(nc, d, o)
    ACC = 4 * KB * TOK

    def accumulator(n):
        k.at = k.rest
        return k.put(f"acc{n}", [P, KB, TOK])

    k.at = k.rest
    first = first_ffn_weights(k, 0)
    with nc.Block() as block:
        norm = norm_stage(nc, k, block, None, 0, None, first)
        acc = accumulator(0)
        ffn_stage(nc, k, block, 0, acc, norm, first)
    k.at = k.rest + ACC
    _, heads, plain = in_halves(k)
    first = FirstWeights(k, "wi", [heads(i, b) for i in range(2) for b in range(2)])
    with nc.Block() as block:
        norm = norm_stage(nc, k, block, 0, 1, acc, first)
        k.at = k.rest
        proj = k.put("proj", [P, PROJB, TOK])
        gemm_stage(nc, k, block, "wi", norm, first, [((2, 9), plain)], k_halves(in_halves(k)[0], IN_W - P), 18, proj)
    b = mixer(nc, k, proj)
    first = FirstWeights(k, "wo", [out_parts(k)(i, b) for i in range(2) for b in range(2)])
    with nc.Block() as block:
        mixed = gla_out_stage(nc, k, block, proj, b, first)
        acc = accumulator(1)
        gemm_stage(nc, k, block, "wo", mixed, first, [((0, KB // 2), out_parts(k))], None, KB, acc, parts=3)
    k.at = k.rest + ACC
    first = first_ffn_weights(k, 1)
    with nc.Block() as block:
        norm = norm_stage(nc, k, block, 1, 2, acc, first)
        acc = accumulator(2)
        ffn_stage(nc, k, block, 1, acc, norm, first)
    k.at = k.rest + ACC
    with nc.Block() as block:
        norm_stage(nc, k, block, 2, None, acc)


_INS = ["x_prompt", "x_sample", "cache_k", "cache_v", "state_gla_fwd", "state_gla_bwd", "c", "c_ctx", "w_ada", "b_ada",
        "norm_pre", "norm_post", "ffn_w1", "ffn_w3", "ffn_w2", "w_in", "gla_w_up", "gla_b_up", "gla_norm", "attn_sink",
        "w_out"]
_OUTS = [(1, CTX, D), (1, LAT, D), (1, 1, CTX, NKV, HD), (1, 1, CTX, NKV, HD), (1, 1, GH, DK, DV), (1, 1, GH, DK, DV)]


def kernel(**inputs):
    import concourse.bacc as bacc
    from concourse.bass_utils import run_bass_kernel_spmd

    nc = bacc.Bacc("TRN2", target_bir_lowering=False, num_devices=1)
    arrays = {name: np.ascontiguousarray(inputs[name]) for name in _INS}
    arrays.update(shape_constants())
    d = {name: nc.dram_tensor(f"in_{name}", a.shape, mybir.dt.from_np(a.dtype), kind="ExternalInput").ap()
         for name, a in arrays.items()}
    o = [nc.dram_tensor(f"out_{i}", shape, F32, kind="ExternalOutput").ap() for i, shape in enumerate(_OUTS)]
    layer(nc, d, o)
    r = run_bass_kernel_spmd(nc, [{f"in_{name}": a for name, a in arrays.items()}], core_ids=[0])
    return tuple(r.results[0][f"out_{i}"] for i in range(len(_OUTS)))
```
